# Optimizing a Trainium2 kernel written in Bass

```python
import math
import jax, jax.numpy as jnp
from jax import lax
import numpy as np

D_MODEL = 1024
BATCH = 1
SEQ = 512
DEPTH = 1

HEAD_DIM = 64
N_HEADS_MOBA = 8
N_HEADS_DSA = 8
ROT_DIM = HEAD_DIM // 4
ROPE_THETA = 500000.0
MOBA_BLOCK = 256
MOBA_TOPK = 3
MOBA_Q_CHUNK = 16
IDX_HEADS = 8
IDX_DIM = 64
DSA_TOPK_MAX = 256
DSA_Q_CHUNK = 64
N_GROUPS = 4
EXPERTS_PER_GROUP = 8
N_EXPERTS = N_GROUPS * EXPERTS_PER_GROUP
EXPERT_TOPK = 2
D_EXPERT = 512
MOE_ROWS = 256
PLE_DIM = 256
RMS_EPS = 1e-6

A_W = N_HEADS_MOBA * HEAD_DIM
B_W = N_HEADS_DSA * HEAD_DIM
IQ_W = IDX_HEADS * IDX_DIM
IN_SPLITS = (A_W, A_W, A_W, B_W, B_W, B_W, IQ_W, IDX_DIM, IDX_HEADS, D_MODEL, D_MODEL)
IN_COLS = sum(IN_SPLITS)

kernel_name = "hybrid_moba_dsa_hiermoe_ple"

def rms_norm(x, g):
    xf = x.astype(jnp.float32)
    y = xf * lax.rsqrt(jnp.mean(xf * xf, axis=-1, keepdims=True) + RMS_EPS)
    return (y * g.astype(jnp.float32)).astype(x.dtype)

def rope_tables(seq):
    inv = 1.0 / (ROPE_THETA ** (jnp.arange(0, ROT_DIM, 2, dtype=jnp.float32) / ROT_DIM))
    ang = jnp.arange(seq, dtype=jnp.float32)[:, None] * inv[None, :]
    return jnp.cos(ang), jnp.sin(ang)

def apply_rope(x, cos, sin):
    half = ROT_DIM // 2
    xf = x.astype(jnp.float32)
    x1 = xf[..., :half]
    x2 = xf[..., half:ROT_DIM]
    c = cos[None, :, None, :]
    s = sin[None, :, None, :]
    out = jnp.concatenate([x1 * c - x2 * s, x2 * c + x1 * s, xf[..., ROT_DIM:]], axis=-1)
    return out.astype(x.dtype)

def moba_attention(q, k, v):
    b, s, h, dh = q.shape
    n_blk = -(-s // MOBA_BLOCK)
    pad = n_blk * MOBA_BLOCK - s
    kp = jnp.pad(k, ((0, 0), (0, pad), (0, 0), (0, 0)))
    vp = jnp.pad(v, ((0, 0), (0, pad), (0, 0), (0, 0)))
    k_bh = kp.reshape(b, n_blk, MOBA_BLOCK, h, dh).transpose(0, 3, 1, 2, 4)
    v_bh = vp.reshape(b, n_blk, MOBA_BLOCK, h, dh).transpose(0, 3, 1, 2, 4)
    k_mean = jnp.mean(k_bh.astype(jnp.float32), axis=3)
    n_sel = min(MOBA_TOPK, n_blk - 1)
    scale = HEAD_DIM ** -0.5
    n_chunks = s // MOBA_Q_CHUNK
    qc = q.reshape(b, n_chunks, MOBA_Q_CHUNK, h, dh).transpose(1, 0, 2, 3, 4)
    bi = jnp.arange(b)[:, None, None, None]
    hi = jnp.arange(h)[None, None, :, None]
    kpos_in_blk = jnp.arange(MOBA_BLOCK)

    def chunk_fn(args):
        q_c, c = args
        t0 = c * MOBA_Q_CHUNK
        pos = t0 + jnp.arange(MOBA_Q_CHUNK)
        cur = t0 // MOBA_BLOCK
        k_own = lax.dynamic_index_in_dim(k_bh, cur, axis=2, keepdims=False)
        v_own = lax.dynamic_index_in_dim(v_bh, cur, axis=2, keepdims=False)
        s_own = jnp.einsum('bqhd,bhkd->bqhk', q_c, k_own,
                           preferred_element_type=jnp.float32) * scale
        causal = (cur * MOBA_BLOCK + kpos_in_blk)[None, :] <= pos[:, None]
        s_own = jnp.where(causal[None, :, None, :], s_own, -jnp.inf)
        if n_sel > 0:
            gate = jnp.einsum('bqhd,bhnd->bqhn', q_c.astype(jnp.float32), k_mean)
            past = jnp.arange(n_blk) < cur
            gate = jnp.where(past[None, None, None, :], gate, -jnp.inf)
            _, sel = lax.top_k(gate, n_sel)
            sel_ok = sel < cur
            k_sel = k_bh[bi, hi, sel]
            v_sel = v_bh[bi, hi, sel]
            s_past = jnp.einsum('bqhd,bqhnkd->bqhnk', q_c, k_sel,
                                preferred_element_type=jnp.float32) * scale
            s_past = jnp.where(sel_ok[..., None], s_past, -jnp.inf)
            s_past = s_past.reshape(b, MOBA_Q_CHUNK, h, n_sel * MOBA_BLOCK)
            probs = jax.nn.softmax(jnp.concatenate([s_past, s_own], axis=-1), axis=-1)
            p_past = probs[..., :n_sel * MOBA_BLOCK].reshape(b, MOBA_Q_CHUNK, h, n_sel, MOBA_BLOCK)
            p_own = probs[..., n_sel * MOBA_BLOCK:]
            o = (jnp.einsum('bqhnk,bqhnkd->bqhd', p_past, v_sel.astype(jnp.float32))
                 + jnp.einsum('bqhk,bhkd->bqhd', p_own, v_own.astype(jnp.float32)))
        else:
            p_own = jax.nn.softmax(s_own, axis=-1)
            o = jnp.einsum('bqhk,bhkd->bqhd', p_own, v_own.astype(jnp.float32))
        return o.astype(q.dtype)

    out = lax.map(chunk_fn, (qc, jnp.arange(n_chunks)))
    return out.transpose(1, 0, 2, 3, 4).reshape(b, s, h, dh)

def dsa_attention(q, k, v, iq, ik, iw):
    b, s, h, dh = q.shape
    topk = min(DSA_TOPK_MAX, s // 4)
    scale = HEAD_DIM ** -0.5
    idx_scale = IDX_DIM ** -0.5
    w_scale = IDX_HEADS ** -0.5
    n_chunks = s // DSA_Q_CHUNK

    def to_chunks(a):
        return a.reshape((b, n_chunks, DSA_Q_CHUNK) + a.shape[2:]).swapaxes(0, 1)

    key_pos = jnp.arange(s)
    bi = jnp.arange(b)[:, None, None]

    def chunk_fn(args):
        q_c, iq_c, iw_c, c = args
        pos = c * DSA_Q_CHUNK + jnp.arange(DSA_Q_CHUNK)
        rel = jnp.einsum('bqhd,bsd->bhqs', iq_c, ik,
                         preferred_element_type=jnp.float32) * idx_scale
        score = jnp.einsum('bhqs,bqh->bqs', jax.nn.relu(rel),
                           iw_c.astype(jnp.float32) * w_scale)
        admissible = key_pos[None, :] <= pos[:, None]
        score = jnp.where(admissible[None], score, -jnp.inf)
        _, idx = lax.top_k(score, topk)
        ok = idx <= pos[None, :, None]
        k_sel = k[bi, idx]
        v_sel = v[bi, idx]
        logits = jnp.einsum('bqhd,bqkhd->bqhk', q_c, k_sel,
                            preferred_element_type=jnp.float32) * scale
        logits = jnp.where(ok[:, :, None, :], logits, -jnp.inf)
        probs = jax.nn.softmax(logits, axis=-1)
        o = jnp.einsum('bqhk,bqkhd->bqhd', probs, v_sel.astype(jnp.float32))
        return o.astype(q.dtype)

    out = lax.map(chunk_fn, (to_chunks(q), to_chunks(iq), to_chunks(iw), jnp.arange(n_chunks)))
    return out.swapaxes(0, 1).reshape(b, s, h, dh)

def hier_moe(h, w_grp, b_grp, w_rt, b_rt, w_gate, w_up, w_down):
    b, s, d = h.shape
    t = b * s
    hf = h.reshape(t, d)
    grp_logits = jnp.matmul(hf, w_grp).astype(jnp.float32) + b_grp.astype(jnp.float32)
    grp_prob = jax.nn.softmax(grp_logits, axis=-1)
    g = jnp.argmax(grp_logits, axis=-1)
    p_g = jnp.take_along_axis(grp_prob, g[:, None], axis=-1)[:, 0]
    exp_logits = (jnp.matmul(hf, w_rt).astype(jnp.float32) + b_rt.astype(jnp.float32))
    exp_logits = exp_logits.reshape(t, N_GROUPS, EXPERTS_PER_GROUP)
    in_grp = jnp.take_along_axis(exp_logits, g[:, None, None], axis=1)[:, 0]
    top_val, top_idx = lax.top_k(in_grp, EXPERT_TOPK)
    combine = p_g[:, None] * jax.nn.softmax(top_val, axis=-1)
    expert_id = g[:, None] * EXPERTS_PER_GROUP + top_idx

    a = t * EXPERT_TOPK
    e_flat = expert_id.reshape(a)
    tok_flat = jnp.repeat(jnp.arange(t), EXPERT_TOPK)
    w_flat = combine.reshape(a)
    order = jnp.argsort(e_flat)
    e_s, tok_s, w_s = e_flat[order], tok_flat[order], w_flat[order]
    counts = jnp.bincount(e_flat, length=N_EXPERTS)
    padded = ((counts + MOE_ROWS - 1) // MOE_ROWS) * MOE_ROWS
    start = jnp.cumsum(counts) - counts
    pend = jnp.cumsum(padded)
    pstart = pend - padded
    dest = pstart[e_s] + (jnp.arange(a) - start[e_s])
    n_blocks = -(-a // MOE_ROWS) + N_EXPERTS
    rows = n_blocks * MOE_ROWS
    buf_tok = jnp.full((rows,), t, dtype=jnp.int32).at[dest].set(tok_s.astype(jnp.int32))
    buf_w = jnp.zeros((rows,), jnp.float32).at[dest].set(w_s)
    blk_exp = jnp.minimum(jnp.searchsorted(pend, jnp.arange(n_blocks) * MOE_ROWS, side='right'),
                          N_EXPERTS - 1)
    h_pad = jnp.concatenate([hf, jnp.zeros((1, d), hf.dtype)], axis=0)

    def block_fn(args):
        tok_b, e_b = args
        xb = h_pad[tok_b]
        hid = jax.nn.silu(jnp.matmul(xb, w_gate[e_b])) * jnp.matmul(xb, w_up[e_b])
        return jnp.matmul(hid, w_down[e_b])

    y = lax.map(block_fn, (buf_tok.reshape(n_blocks, MOE_ROWS), blk_exp))
    y = y.reshape(rows, d).astype(jnp.float32) * buf_w[:, None]
    out = jnp.zeros((t + 1, d), jnp.float32).at[buf_tok].add(y)[:t]
    return out.reshape(b, s, d).astype(h.dtype)

def hybrid_layer(x, p_i, cos, sin, g_attn, w_in, w_br_a, w_br_b, w_out, g_ffn,
                 w_grp, b_grp, w_rt, b_rt, w_gate, w_up, w_down, g_ple, w_ple_gate, w_ple_proj):
    b, s, d = x.shape
    h = rms_norm(x, g_attn)
    z = jnp.matmul(h, w_in)
    offs = np.cumsum(IN_SPLITS)[:-1].tolist()
    qa, ka, va, qb, kb, vb, iq, ik, iw, ga, gb = jnp.split(z, offs, axis=-1)
    heads = lambda a, n: a.reshape(b, s, n, HEAD_DIM)
    qa = apply_rope(heads(qa, N_HEADS_MOBA), cos, sin)
    ka = apply_rope(heads(ka, N_HEADS_MOBA), cos, sin)
    va = heads(va, N_HEADS_MOBA)
    qb = apply_rope(heads(qb, N_HEADS_DSA), cos, sin)
    kb = apply_rope(heads(kb, N_HEADS_DSA), cos, sin)
    vb = heads(vb, N_HEADS_DSA)
    iq = apply_rope(iq.reshape(b, s, IDX_HEADS, IDX_DIM), cos, sin)
    ik = apply_rope(ik[:, :, None, :], cos, sin)[:, :, 0, :]
    o_a = moba_attention(qa, ka, va).reshape(b, s, A_W)
    o_b = dsa_attention(qb, kb, vb, iq, ik, iw).reshape(b, s, B_W)
    merged = (jax.nn.sigmoid(ga) * jnp.matmul(o_a, w_br_a)
              + jax.nn.sigmoid(gb) * jnp.matmul(o_b, w_br_b))
    x = x + jnp.matmul(merged, w_out)
    x = x + hier_moe(rms_norm(x, g_ffn), w_grp, b_grp, w_rt, b_rt, w_gate, w_up, w_down)
    gate = jax.nn.sigmoid(jnp.matmul(rms_norm(x, g_ple), w_ple_gate))
    x = x + gate * jnp.matmul(p_i, w_ple_proj)
    return x

def setup_inputs(seed: int = 0) -> dict:
    key = jax.random.key(seed)
    ks = jax.random.split(key, 20)
    f32 = jnp.float32
    nrm = lambda k, shape, fan_in: jax.random.normal(k, shape, f32) * (fan_in ** -0.5)
    gain = lambda k: 1.0 + 0.05 * jax.random.normal(k, (DEPTH, D_MODEL), f32)
    return {
        "x": jax.random.normal(ks[0], (BATCH, SEQ, D_MODEL), f32),
        "p": jax.random.normal(ks[1], (DEPTH, BATCH, SEQ, PLE_DIM), f32),
        "g_attn": gain(ks[2]),
        "w_in": nrm(ks[3], (DEPTH, D_MODEL, IN_COLS), D_MODEL),
        "w_br_a": nrm(ks[4], (DEPTH, A_W, D_MODEL), A_W),
        "w_br_b": nrm(ks[5], (DEPTH, B_W, D_MODEL), B_W),
        "w_out": nrm(ks[6], (DEPTH, D_MODEL, D_MODEL), D_MODEL),
        "g_ffn": gain(ks[7]),
        "w_grp": nrm(ks[8], (DEPTH, D_MODEL, N_GROUPS), D_MODEL),
        "b_grp": 0.01 * jax.random.normal(ks[9], (DEPTH, N_GROUPS), f32),
        "w_rt": nrm(ks[10], (DEPTH, D_MODEL, N_EXPERTS), D_MODEL),
        "b_rt": 0.01 * jax.random.normal(ks[11], (DEPTH, N_EXPERTS), f32),
        "w_gate": nrm(ks[12], (DEPTH, N_EXPERTS, D_MODEL, D_EXPERT), D_MODEL),
        "w_up": nrm(ks[13], (DEPTH, N_EXPERTS, D_MODEL, D_EXPERT), D_MODEL),
        "w_down": nrm(ks[14], (DEPTH, N_EXPERTS, D_EXPERT, D_MODEL), D_EXPERT),
        "g_ple": gain(ks[15]),
        "w_ple_gate": nrm(ks[16], (DEPTH, D_MODEL, D_MODEL), D_MODEL),
        "w_ple_proj": nrm(ks[17], (DEPTH, PLE_DIM, D_MODEL), PLE_DIM),
        "g_final": 1.0 + 0.05 * jax.random.normal(ks[18], (D_MODEL,), f32),
    }

def reference(x, p, g_attn, w_in, w_br_a, w_br_b, w_out, g_ffn, w_grp, b_grp, w_rt, b_rt,
              w_gate, w_up, w_down, g_ple, w_ple_gate, w_ple_proj, g_final):
    cos, sin = rope_tables(x.shape[1])
    for i in range(DEPTH):
        x = hybrid_layer(x, p[i], cos, sin, g_attn[i], w_in[i], w_br_a[i], w_br_b[i], w_out[i],
                         g_ffn[i], w_grp[i], b_grp[i], w_rt[i], b_rt[i], w_gate[i], w_up[i],
                         w_down[i], g_ple[i], w_ple_gate[i], w_ple_proj[i])
    return rms_norm(x, g_final)


_drawn_inputs = setup_inputs


def setup_inputs(seed=0):
    import zlib

    import numpy as np

    out = dict(_drawn_inputs(seed))
    spreads = {}
    factors = {'b_grp': 11.523, 'b_rt': 4.321, 'g_ple': 6.316}
    for name, (base, spread) in spreads.items():
        noise = np.random.default_rng([zlib.crc32(name.encode()), seed]).standard_normal(out[name].shape)
        drawn = base * np.exp(spread * noise) if base else spread * noise
        out[name] = __import__('jax').numpy.asarray(drawn.astype(out[name].dtype))
    for name, factor in factors.items():
        out[name] = (out[name] * factor).astype(out[name].dtype)
    return out
```

```python
import numpy as np

import concourse.bass as bass
from concourse import mybir

ALU = mybir.AluOpType
ACT = mybir.ActivationFunctionType
AX = mybir.AxisListType
F32 = mybir.dt.float32
I32 = mybir.dt.int32
U32 = mybir.dt.uint32

P = 128
S = 512
D = 1024
NT = S // P
KD = D // P
HD = 64
NH = 8
AW = NH * HD
ROT = HD // 4
HALF = ROT // 2
THETA = 500000.0
DSA_TOPK = min(256, S // 4)
NG, EPG = 4, 8
NE = NG * EPG
FE = 512
PLE = 256
EPS = 1e-6
NEG = -1.0e30
MARK = -3.0e38
CH = NT
SLOT = 4096
RING = 6
NOVER = 2 * S // P - 1
OOB = 1 << 20

IN_OFF = dict(qa=0, ka=AW, va=2 * AW, qb=3 * AW, kb=4 * AW, vb=5 * AW, iq=6 * AW,
              ix=7 * AW, ga=7 * AW + HD + NH, gb=7 * AW + HD + NH + D)

CONST_COLS = {}
_at = 0
for _name, _n in (("ident", P), ("before", P), ("causal", 2 * P * (NT + 1) // 2), ("cos", NT * NH * HALF),
                  ("sin", NT * NH * HALF), ("ones", P), ("desc_group", NT * NG), ("desc_expert", NT * NE),
                  ("four_e", NT * NE), ("token", NT), ("code", 1), ("limit", 1), ("iota8", 8)):
    CONST_COLS[_name] = (_at, _at + _n)
    _at += _n
NCONST = _at


def constants():
    c = np.zeros((P, NCONST), np.float32)

    def put(name, value):
        a, b = CONST_COLS[name]
        c[:, a:b] = np.asarray(value, np.float32).reshape(P, b - a)

    row = np.arange(P)
    put("ident", np.eye(P))
    put("before", row[:, None] < row[None, :])
    causal = np.zeros((P, P * (NT + 1)), np.float32)
    causal[:, P * NT:] = np.where(row[None, :] <= row[:, None], 0.0, NEG)
    put("causal", causal)
    inv = (1.0 / (np.float32(THETA) ** (np.arange(0, ROT, 2, dtype=np.float32) / np.float32(ROT)))).astype(np.float32)
    ang = np.arange(S, dtype=np.float32)[:, None] * inv[None, :]
    for name, f in (("cos", np.cos), ("sin", np.sin)):
        t = f(ang).reshape(NT, P, 1, HALF).transpose(1, 0, 2, 3)
        put(name, np.broadcast_to(t, (P, NT, NH, HALF)))
    put("ones", np.ones((P, P)))
    put("desc_group", np.broadcast_to(NG - np.arange(NG), (P, NT, NG)))
    put("desc_expert", np.broadcast_to(NE - np.arange(NE), (P, NT, NE)))
    put("four_e", np.broadcast_to(CH * np.arange(NE), (P, NT, NE)))
    put("token", np.arange(NT)[None, :] * P + row[:, None])
    put("code", row)
    put("limit", np.where(row % CH == 0, 1e9, P * (row % CH)))
    put("iota8", np.broadcast_to(np.arange(8), (P, 8)))
    return c


def attention_steps(branch):
    units = [(h, t) for h in range(NH) for t in range(NT)]
    out = []
    for u in range(len(units) + 3):
        if u < len(units):
            out.append(("scores", branch, u))
        if 2 <= u < len(units) + 2:
            out.append(("turn_p", branch, u - 2))
        if u >= 3:
            out.append(("pv", branch, u - 3))
    return out


def front_steps():
    z = lambda name: [("z", name, t) for t in range(NT)]
    turn = lambda name, n: [("turn", name, c) for c in range(n)]
    st = turn("h", KD)
    st += z("iq") + [("rope", "iq", 0)] + z("ix") + [("rope", "ix", 0)]
    st += turn("iq", NT)
    st += z("qa")[:1] + turn("ix", 1)
    for t in range(1, NT):
        st += [("rel", t, h) for h in range(NH)] + z("qa")[t:t + 1]
    st += [("topk", 0, 0), ("rope", "qa", 0)]
    st += z("ka") + [("rope", "ka", 0)] + turn("qa", NT) + z("va") + turn("ka", NT)
    st += z("qb") + [("rope", "qb", 0)] + z("kb") + [("rope", "kb", 0)]
    st += attention_steps("a")
    st += turn("qb", NT) + turn("kb", NT) + z("vb")
    st += attention_steps("b")
    st += turn("oa", NT) + turn("ob", NT)
    for n in range(2):
        for x in "ab":
            st += [(what + x, n, t) for t in range(NT) for what in ("gate_", "branch_")]
    st += turn("merged", KD)
    st += [("out", n, t) for t in range(NT) for n in range(2)]
    st += [("norm", "ffn", 0)] + turn("h2", KD) + [("router", 0, 0)]
    return st


def back_steps():
    st = [("turn", "p", c) for c in range(2)]
    st += [("norm", "ple", 0)] + [("turn", "h3", c) for c in range(KD)]
    st += [(w, n, t) for t in range(NT) for n in range(2) for w in ("ple_gate", "ple_proj")]
    st += [("norm", "final", 0)]
    return st


FRONT, BACK = front_steps(), back_steps()
NO_BANK = ("rope", "topk", "norm")


def place_banks():
    where, uses = {}, [0] * 8
    rot = {"z": 0, "turn": 0, "rel": 0, "out": 0, "gate": 0}
    for s in FRONT + BACK:
        kind = s[0]
        if kind in NO_BANK:
            continue
        if kind in ("z",):
            b = rot["z"] % 4
            rot["z"] += 1
        elif kind == "turn":
            b = 4 + rot["turn"] % 2
            rot["turn"] += 1
        elif kind == "rel":
            b = 6 + rot["rel"] % 2
            rot["rel"] += 1
        elif kind == "scores":
            b = s[2] % 3
        elif kind == "turn_p":
            b = 4 + s[2] % 2
        elif kind == "pv":
            b = 6 + s[2] % 2
        elif kind.startswith("gate_") or kind == "ple_gate":
            b = 2 * (rot["gate"] % 4)
        elif kind.startswith("branch_") or kind == "ple_proj":
            b = 2 * (rot["gate"] % 4) + 1
            rot["gate"] += 1
        elif kind == "out":
            b = rot["out"] % 8
            rot["out"] += 1
        else:
            b = 0
        uses[b] += 1
        where[s] = (b, uses[b])
    return where


BANK = place_banks()

GATES = [s for s in FRONT + BACK if s[0].startswith("gate_") or s[0] == "ple_gate"]
BRANCHES = [s for s in FRONT + BACK if s[0].startswith("branch_") or s[0] == "ple_proj"]
ROPES = ["iq", "ix", "qa", "ka", "qb", "kb"]
STAGE = {name: n % 2 for n, name in enumerate(ROPES)}


def pieces_of(s):
    kind, a, _ = s
    if kind == "z":
        return [a]
    if kind.startswith("gate_"):
        return [f"g{kind[-1]}{a}"]
    if kind.startswith("branch_"):
        return ["br_" + kind[-1]]
    return {"out": ["out0", "out1"]}.get(kind, [])


LAST_USE = {name: s for s in FRONT for name in pieces_of(s)}


def act_evacuates(s):
    return s[1] in ("iq", "ix", "qa", "ka") or s[2] % 2 == 0

PIECES = ["iq", "ix", "qa", "ka", "va", "qb", "kb", "vb", "br_a", "br_b", "ga0", "gb0", "ga1", "gb1", "out0", "out1"]
N_FRONT = len(PIECES)
N_EXP = 3 * NE
TAIL = ["ple_proj", "ple_gate0", "ple_gate1"]
PIECE = {n: i for i, n in enumerate(PIECES)}
PIECE.update({n: N_FRONT + N_EXP + i for i, n in enumerate(TAIL)})


def layer_kernel(nc, x, p, g_attn, w_in, w_br_a, w_br_b, w_out, g_ffn, w_grp, b_grp, w_rt, b_rt,
                 w_gate, w_up, w_down, g_ple, w_ple_gate, w_ple_proj, g_final, const, out):
    def sb(name, shape, dt=F32):
        return nc.alloc_sbuf_tensor(name, shape, dt)

    def sem(name):
        return nc.alloc_semaphore(name)

    ring = sb("ring", [P, RING, SLOT])
    cst = sb("cst", [P, NCONST])
    gain = sb("gain", [P, D])
    stage = sb("stage", [P, NT * D])
    wide_t = sb("wide_t", [P, KD * S])
    qt_kt = sb("qt_kt", [P, 2, NT * S])
    vals = sb("vals", [P, NT * AW])
    o_or_iq = sb("o_or_iq", [P, 2, NT * AW])
    ikt = sb("ikt", [P, S])
    work = sb("work", [P, 9 * P])
    small = sb("small", [P, 6, S])
    iws = sb("iws", [P, NT, NH])
    rope_t = sb("rope_t", [P, NT, NH, 2 * ROT])
    m8 = sb("m8", [P, NT, 8])
    stat = sb("stat", [P, 24])
    nm = sb("nm", [P, 4])
    rs = sb("rs", [P, 4])
    ri = sb("ri", [P, 4])
    wr = sb("wr", [P, KD, NG + NE])
    br = sb("br", [P, NG + NE])
    table = sb("table", [P, NE * CH + CH, 4], I32)
    slots = sb("slots", [P, 2, 4], I32)
    rt = work
    rs_small = sb("rs_small", [P, 32 * NT])
    rows = sb("rows", [P, 2 * NT, 4], I32)
    dest = sb("dest", [P, 2 * NT], I32)
    over_f = sb("over_f", [P, 32])
    over = sb("over", [P, 16], I32)

    def score(t):
        return work[:, score_at[t]:score_at[t] + (t + 1) * P]

    def turn_dst(s):
        _, a, i = s
        if a == "ix":
            return ikt[:]
        where = {"iq": iqt, "qa": qt, "qb": qt, "ka": kt_, "kb": kt_, "oa": ot["a"], "ob": ot["b"], "p": pt_in}
        return where.get(a, wide)[:, i, :]

    def c(name, *dims):
        a, b = CONST_COLS[name]
        v = cst[:, a:b]
        return v

    def c4(name, k):
        a, b = CONST_COLS[name]
        return cst[:, a:b].rearrange("p (t k) -> p t k", k=k)

    ident = c("ident")
    stage_tok = stage[:].rearrange("p (t d) -> p t d", t=NT)
    stage_z = stage[:].rearrange("p (s t n) -> p s t n", s=2, t=NT)
    wide = wide_t[:].rearrange("p (k s) -> p k s", k=KD)
    qt = qt_kt[:, 0].rearrange("p (c s) -> p c s", c=NT)
    kt_ = qt_kt[:, 1].rearrange("p (c s) -> p c s", c=NT)
    v_sb = vals[:].rearrange("p (t n) -> p t n", t=NT)
    iqt = o_or_iq[:, 0].rearrange("p (c s) -> p c s", c=NT)
    o_sb = {"a": o_or_iq[:, 0].rearrange("p (t n) -> p t n", t=NT), "b": o_or_iq[:, 1].rearrange("p (t n) -> p t n", t=NT)}
    ot = {"a": qt, "b": kt_}
    junk0 = o_or_iq[:].rearrange("p a n -> p (a n)").rearrange("p (t d) -> p t d", t=NT)
    xres = o_or_iq[:].rearrange("p a n -> p (a n)").rearrange("p (t d) -> p t d", t=NT)
    xg = wide_t[:, 0:2 * D].rearrange("p (b d) -> p b d", b=2)
    xgt = wide_t[:, 2 * D:4 * D].rearrange("p (b k s) -> p b k s", b=2, k=KD)
    y_sb = vals[:].rearrange("p (b d) -> p b d", b=2)
    y_in = qt_kt[:]
    pin = vals[:, 0:NT * PLE].rearrange("p (t d) -> p t d", t=NT)
    logits = small[:, 4, 0:NT * (NG + NE)].rearrange("p (t k) -> p t k", t=NT)
    member = rt[:, 4 * NT * NE:5 * NT * NE].rearrange("p (t e) -> p t e", t=NT)
    member_wide = small[:, 3, :].rearrange("p (t k) -> p t k", t=NT)
    score_at = {1: 0, 2: 2 * P, 3: 5 * P}
    pt_in = vals[:, NT * PLE:2 * NT * PLE].rearrange("p (c s) -> p c s", c=2)

    bank = [nc.alloc_psum_tensor(f"bank{b}", [P, S], F32) for b in range(8)]

    h2_d = nc.dram_tensor("h2_rows", [S, D], F32, kind="Internal").ap()
    pairs_d = nc.dram_tensor("pair_rows", [2 * S, D], F32, kind="Internal").ap()
    table_d = nc.dram_tensor("slot_table", [P * NE * CH, 4], I32, kind="Internal").ap()

    bank_filled = [sem(f"bank_filled_{b}") for b in range(8)]
    bank_drained = [sem(f"bank_drained_{b}") for b in range(8)]
    piece_loaded = [sem(f"piece_loaded_{b}") for b in range(RING)]
    merged_done, ple_added = sem("merged_done"), sem("ple_added")
    const_in, x_in, gain_in, small_in, p_in = sem("const_in"), sem("x_in"), sem("gain_in"), sem("small_in"), sem("p_in")
    sumsq, rvar, root, normed = sem("sumsq"), sem("rvar"), sem("root"), sem("normed")
    roped, pool_chain, dve_chain = sem("roped"), sem("pool_chain"), sem("dve_chain")
    relu_done, acc_done = sem("relu_done"), sem("acc_done")
    max_done, mark_done, selected = sem("max_done"), sem("mark_done"), sem("selected")
    exp_done = sem("exp_done")
    x_back, h2_out = sem("x_back"), sem("h2_out")
    ngmax_done, gexp_done, e2_done = sem("ngmax_done"), sem("gexp_done"), sem("e2_done")
    top_done, rank_done, count_done, list_done = sem("top_done"), sem("rank_done"), sem("count_done"), sem("list_done")
    member_f, over_list, rows_ready, fill_ready = sem("member_f"), sem("over_list"), sem("rows_ready"), sem("fill_ready")
    table_filled, table_written, table_in = sem("table_filled"), sem("table_written"), sem("table_in")
    xg_clear, slots_set, gathered, x_turned = sem("xg_clear"), sem("slots_set"), sem("gathered"), sem("x_turned")
    xt_low, xt_high, gate_done, up_done, silu_done = (sem("xt_low"), sem("xt_high"), sem("gate_done"), sem("up_done"),
                                                      sem("silu_done"))
    hid_done, hid_turned, hidt_done, down_done = sem("hid_done"), sem("hid_turned"), sem("hidt_done"), sem("down_done")
    y_low, y_high, scattered = sem("y_low"), sem("y_high"), sem("scattered")
    pairs_in, pairs_added = [sem("pairs_in_even"), sem("pairs_in_odd")], sem("pairs_added")
    ov = {n: sem("ov_" + n) for n in ("loaded", "slots", "gathered", "turned", "xt", "gate", "up", "silu", "hid",
                                      "hid_turned", "hidt", "down", "y", "scattered", "act_end", "sp_end", "pool_end")}
    out_done, pool_steps = sem("out_done"), sem("pool_steps")

    def claim(pe, step):
        b, n = BANK[step]
        if n > 1:
            pe.wait_ge(bank_drained[b], n - 1)
        return bank[b]

    def filled(eng, step):
        b, n = BANK[step]
        eng.wait_ge(bank_filled[b], n)
        return bank[b]

    def drained(eng, step):
        b, n = BANK[step]
        eng.wait_ge(bank_drained[b], n)

    def piece_slot(name):
        n = PIECE[name]
        return n % RING, n // RING + 1

    def loaded(pe, name):
        b, n = piece_slot(name)
        pe.wait_ge(piece_loaded[b], 16 * n)

    def wview(name, k):
        return ring[:, PIECE[name] % RING].rearrange("p (k n) -> p k n", k=k)

    def exp_piece(kind, j):
        n = N_FRONT + 3 * j + kind
        return n % RING, n // RING + 1

    def wait_for(eng, sem_, value):
        if not isinstance(value, int) or value > 0:
            eng.wait_ge(sem_, value)

    def unit(u):
        return u // NT, u % NT

    BR = {"a": 0, "b": 1}
    NU = NH * NT
    block = nc.Block()
    block.__enter__()

    @block.sync
    def _(sp):
        w_in_v = w_in[0].rearrange("(k p) n -> p k n", p=P)
        br_v = {"br_a": w_br_a[0], "br_b": w_br_b[0]}

        def load(name, dst, src):
            n = PIECE[name]
            if RING <= n < N_FRONT:
                filled(sp, LAST_USE[PIECES[n - RING]])
            sp.dma_start(dst, src).then_inc(piece_loaded[n % RING], 16)

        sp.dma_start(stage_tok, x[0].rearrange("(t p) d -> p t d", p=P)).then_inc(x_in, 16)
        sp.dma_start(cst[:], const).then_inc(const_in, 16)
        sp.dma_start(gain[:], g_attn[0:1, :].partition_broadcast(P)).then_inc(gain_in, 16)
        for name in PIECES:
            n = PIECE[name]
            if name in br_v:
                load(name, wview(name, AW // P), br_v[name].rearrange("(k p) n -> p k n", p=P))
            elif name.startswith("out"):
                i = int(name[-1])
                load(name, wview(name, KD // 2), w_out[0, i * (D // 2):(i + 1) * (D // 2)].rearrange("(k p) n -> p k n", p=P))
            elif name == "ix":
                w = HD + NH
                load(name, ring[:, n % RING, 0:KD * w].rearrange("p (k n) -> p k n", k=KD),
                     w_in_v[:, :, IN_OFF["ix"]:IN_OFF["ix"] + w])
            else:
                off = IN_OFF[name[:2]] + (512 * int(name[2]) if len(name) > 2 else 0)
                load(name, wview(name, KD), w_in_v[:, :, off:off + 512])
        gate_v = w_gate[0].rearrange("e (p k) f -> e p (k f)", p=P)
        up_v = w_up[0].rearrange("e (p k) f -> e p (k f)", p=P)
        down_v = w_down[0].rearrange("e (k p) d -> e p k d", p=P)

        def load_expert(j, e):
            for kind, src in enumerate((gate_v, up_v, down_v)):
                b = exp_piece(kind, j)[0]
                if isinstance(e, int):
                    filled(sp, LAST_USE[PIECES[N_FRONT + 3 * j + kind - RING]])
                else:
                    sp.wait_ge((gate_done, up_done, down_done)[kind], 2 * e - 2 if kind == 2 else e - 1)
                dst = ring[:, b]
                if kind == 2:
                    dst = dst.rearrange("p (k n) -> p k n", k=FE // P)
                sp.dma_start(dst, src[e]).then_inc(piece_loaded[b], 16)

        load_expert(0, 0)
        load_expert(1, 1)
        with sp.Fori(1, NE // 2) as i:
            for j in range(2):
                load_expert(j, 2 * i + j)
        sp.wait_ge(over_list, 1)
        n_over = sp.value_load(over[0:1, 8:9], min_val=0, max_val=NOVER)
        with sp.Fori(0, NOVER) as i:
            with sp.If(i < n_over):
                sp.wait_ge(down_done, 2 * NE)
                code = sp.value_load(over[0:1, bass.ds(i, 1)], min_val=0, max_val=NE * CH - 1)
                e = sp.snap(code // CH, min_val=0, max_val=NE - 1)
                for kind, src in enumerate((gate_v, up_v, down_v)):
                    dst = ring[:, kind]
                    if kind == 2:
                        dst = dst.rearrange("p (k n) -> p k n", k=FE // P)
                    sp.dma_start(dst, src[e]).then_inc(ov["loaded"], 16)
                sp.wait_ge(ov["scattered"], 16 * i + 16)
                sp.sem_inc(ov["sp_end"], 1)
        sp.wait_ge(scattered, 16 * NE)
        for t in range(NT):
            if t >= 2:
                sp.wait_ge(pairs_added, t - 1)
            sp.dma_start(y_in[:, t % 2, :], pairs_d[t * 2 * P:(t + 1) * 2 * P].rearrange("(p k) d -> p (k d)", k=2)
                         ).then_inc(pairs_in[t % 2], 16)
            if t == 0:
                sp.wait_ge(down_done, 2 * NE)
                load("ple_proj", ring[:, PIECE["ple_proj"] % RING, 0:2 * D].rearrange("p (k n) -> p k n", k=2),
                     w_ple_proj[0].rearrange("(k p) n -> p k n", p=P))
                for i in range(2):
                    load(f"ple_gate{i}", wview(f"ple_gate{i}", KD // 2),
                         w_ple_gate[0, i * (D // 2):(i + 1) * (D // 2)].rearrange("(k p) n -> p k n", p=P))
        out_v = out[0].rearrange("(t p) d -> p t d", p=P)
        for t in range(NT):
            sp.wait_ge(normed, 13 + t)
            sp.dma_start(out_v[:, t], stage_tok[:, t]).then_inc(out_done, 16)
        sp.wait_ge(out_done, 16 * NT)

    @block.tensor
    def _(pe):
        def transposes(step, views):
            ps = claim(pe, step)
            for n, v in enumerate(views):
                mm = pe.transpose(ps[0:v.shape[1], n * P:(n + 1) * P], v, ident)
            mm.then_inc(bank_filled[BANK[step][0]], 1)

        def product(ps, pairs):
            for n, (a, b) in enumerate(pairs):
                mm = pe.matmul(ps, a, b, start=(n == 0), stop=(n == len(pairs) - 1))
            return mm

        def front_step(s):
            kind, a, i = s
            if kind in NO_BANK:
                return
            if kind == "turn":
                if s == ("turn", "h", 0):
                    pe.wait_ge(const_in, 16)
                    pe.wait_ge(normed, NT)
                elif a == "h2" and i == 0:
                    pe.wait_ge(normed, 2 * NT)
                elif a == "h3" and i == 0:
                    pe.wait_ge(normed, 3 * NT)
                elif a in ROPES and i == 0:
                    pe.wait_ge(roped, ROPES.index(a) + 1)
                elif a == "oa" and i == 0:
                    drained(pe, ("pv", "a", NU - 1))
                elif a == "ob" and i == 0:
                    drained(pe, ("pv", "b", NU - 1))
                    drained(pe, ("pv", "b", NU - 2))
                elif a == "merged" and i == 0:
                    pe.wait_ge(merged_done, 2 * NT)
                elif a == "p" and i == 0:
                    pe.wait_ge(p_in, 16)
                if a in ("h", "merged", "h2", "h3"):
                    views = [stage_tok[:, t, i * P:(i + 1) * P] for t in range(NT)]
                elif a in ("oa", "ob"):
                    views = [o_sb[a[1]][:, t, i * P:(i + 1) * P] for t in range(NT)]
                elif a == "p":
                    views = [pin[:, t, i * P:(i + 1) * P] for t in range(NT)]
                else:
                    views = [stage_z[:, STAGE[a], t, i * P:(i + 1) * P] for t in range(NT)]
                transposes(s, views)
            elif kind == "z":
                if i == 0:
                    loaded(pe, a)
                if s == ("z", "iq", 0):
                    for k in range(KD):
                        drained(pe, ("turn", "h", k))
                ps = claim(pe, s)
                w = HD + NH if a == "ix" else 512
                rhs = (ring[:, PIECE[a] % RING, 0:KD * w].rearrange("p (k n) -> p k n", k=KD) if a == "ix"
                       else wview(a, KD))
                mm = product(ps[:, 0:w], [(wide[:, k, i * P:(i + 1) * P], rhs[:, k, :]) for k in range(KD)])
                mm.then_inc(bank_filled[BANK[s][0]], 1)
            elif kind == "rel":
                t, h = a, i
                if (t, h) == (1, 0):
                    for cc in range(NT):
                        drained(pe, ("turn", "iq", cc))
                    drained(pe, ("turn", "ix", 0))
                ps = claim(pe, s)
                lo = HD * (h % 2)
                pe.matmul(ps[:, 0:(t + 1) * P], iqt[lo:lo + HD, h // 2, t * P:(t + 1) * P],
                          ikt[lo:lo + HD, 0:(t + 1) * P], start=True, stop=True
                          ).then_inc(bank_filled[BANK[s][0]], 1)
            elif kind == "scores":
                h, t = unit(i)
                if i == 0:
                    for cc in range(NT):
                        drained(pe, ("turn", "q" + a, cc))
                        drained(pe, ("turn", "k" + a, cc))
                ps = claim(pe, s)
                lo = HD * (h % 2)
                pe.matmul(ps[:, 0:(t + 1) * P], qt[lo:lo + HD, h // 2, t * P:(t + 1) * P],
                          kt_[lo:lo + HD, h // 2, 0:(t + 1) * P], start=True, stop=True
                          ).then_inc(bank_filled[BANK[s][0]], 1)
            elif kind == "turn_p":
                h, t = unit(i)
                pe.wait_ge(exp_done, NU * BR[a] + i + 1)
                transposes(s, [small[:, 2 + i % 2, j * P:(j + 1) * P] for j in range(t + 1)])
            elif kind == "pv":
                h, t = unit(i)
                if i == 0:
                    drained(pe, ("z", "v" + a, NT - 1))
                drained(pe, ("turn_p", a, i))
                ps = claim(pe, s)
                mm = product(ps[:, 0:HD], [(small[:, 4 + i % 2, j * P:(j + 1) * P], v_sb[:, j, h * HD:(h + 1) * HD])
                                           for j in range(t + 1)])
                mm.then_inc(bank_filled[BANK[s][0]], 1)
            elif kind.startswith("gate_"):
                x_ = kind[-1]
                if i == 0:
                    loaded(pe, f"g{x_}{a}")
                ps = claim(pe, s)
                rhs = wview(f"g{x_}{a}", KD)
                product(ps[:], [(wide[:, k, i * P:(i + 1) * P], rhs[:, k, :]) for k in range(KD)]
                        ).then_inc(bank_filled[BANK[s][0]], 1)
            elif kind.startswith("branch_"):
                x_ = kind[-1]
                if i == 0 and a == 0:
                    loaded(pe, "br_" + x_)
                    for cc in range(NT):
                        drained(pe, ("turn", "o" + x_, cc))
                ps = claim(pe, s)
                rhs = wview("br_" + x_, AW // P)
                product(ps[:], [(ot[x_][:, k, i * P:(i + 1) * P], rhs[:, k, a * 512:(a + 1) * 512])
                                for k in range(AW // P)]).then_inc(bank_filled[BANK[s][0]], 1)
            elif kind == "out":
                n, t = a, i
                if (n, t) == (0, 0):
                    loaded(pe, "out0")
                    loaded(pe, "out1")
                    for k in range(KD):
                        drained(pe, ("turn", "merged", k))
                ps = claim(pe, s)
                product(ps[:], [(wide[:, k, t * P:(t + 1) * P],
                                 wview(f"out{k // 4}", KD // 2)[:, k % 4, n * 512:(n + 1) * 512]) for k in range(KD)]
                        ).then_inc(bank_filled[BANK[s][0]], 1)
            elif kind == "router":
                pe.wait_ge(small_in, 64)
                for k in range(KD):
                    drained(pe, ("turn", "h2", k))
                ps = claim(pe, s)
                w = NG + NE
                for t in range(NT):
                    mm = product(ps[:, t * w:(t + 1) * w], [(wide[:, k, t * P:(t + 1) * P], wr[:, k, :]) for k in range(KD)])
                mm.then_inc(bank_filled[BANK[s][0]], 1)
            elif kind == "ple_gate":
                n, t = a, i
                if (n, t) == (0, 0):
                    loaded(pe, "ple_gate0")
                    loaded(pe, "ple_gate1")
                    for k in range(KD):
                        drained(pe, ("turn", "h3", k))
                ps = claim(pe, s)
                product(ps[:], [(wide[:, k, t * P:(t + 1) * P],
                                 wview(f"ple_gate{k // 4}", KD // 2)[:, k % 4, n * 512:(n + 1) * 512]) for k in range(KD)]
                        ).then_inc(bank_filled[BANK[s][0]], 1)
            elif kind == "ple_proj":
                n, t = a, i
                if (n, t) == (0, 0):
                    loaded(pe, "ple_proj")
                    for k in range(2):
                        drained(pe, ("turn", "p", k))
                ps = claim(pe, s)
                rhs = ring[:, PIECE["ple_proj"] % RING, 0:2 * D].rearrange("p (k n) -> p k n", k=2)
                product(ps[:], [(pt_in[:, k, t * P:(t + 1) * P], rhs[:, k, n * 512:(n + 1) * 512]) for k in range(2)]
                        ).then_inc(bank_filled[BANK[s][0]], 1)

        for s in FRONT:
            front_step(s)

        pe.wait_ge(top_done, 2)
        for t in range(NT):
            mm = product(bank[1][:, t * NE:(t + 1) * NE],
                         [(c("ones"), member[:, u, :]) for u in range(t)] + [(c("before"), member[:, t, :])])
        mm.then_inc(rank_done, 1)
        for t in range(NT):
            mm = pe.matmul(bank[2][0:P, 0:1], member_wide[:, t, :], c("ones")[:, 0:1], start=(t == 0), stop=(t == NT - 1))
        mm.then_inc(count_done, 1)
        pe.wait_ge(member_f, 1)
        pe.matmul(bank[3][:, 0:1], c("before"), over_f[:, 0:1], start=True, stop=True).then_inc(list_done, 1)
        pe.wait_ge(member_f, 2)
        pe.matmul(bank[4][0:1, 0:8], c("code"), over_f[:, 8:16], start=True, stop=True)
        pe.matmul(bank[5][0:1, 0:1], c("ones")[:, 0:1], over_f[:, 0:1], start=True, stop=True).then_inc(list_done, 1)

        def turn_rows(src, half, sem_):
            for k in range(4 * half, 4 * half + 4):
                mm = pe.transpose(bank[half][:, (k % 4) * P:(k % 4 + 1) * P], src[:, k:D:KD], ident)
            mm.then_inc(sem_, 1)

        pe.wait_ge(gathered, 16)
        pe.wait_ge(over_list, 1)
        turn_rows(xg[:, 0], 0, x_turned)
        turn_rows(xg[:, 0], 1, x_turned)
        def expert_pair(i):
            for j in range(2):
                e = 2 * i + j
                jn = 1 - j
                slot = [exp_piece(kind, j) for kind in range(3)]
                w = [ring[:, slot[kind][0]] for kind in range(3)]
                gw, uw = (v.rearrange("p (k n) -> p k n", k=KD) for v in w[:2])
                dw = w[2].rearrange("p (k n) -> p k n", k=FE // P)
                wait_for(pe, piece_loaded[slot[0][0]], 16 * i + 16 * slot[0][1])
                wait_for(pe, xt_low, e + 1)
                wait_for(pe, xt_high, e + 1)
                wait_for(pe, silu_done, e)
                product(bank[2][:], [(xgt[:, j, k, :], gw[:, k, :]) for k in range(KD)]).then_inc(gate_done, 1)
                wait_for(pe, piece_loaded[slot[1][0]], 16 * i + 16 * slot[1][1])
                wait_for(pe, hid_done, e)
                product(bank[3][:], [(xgt[:, j, k, :], uw[:, k, :]) for k in range(KD)]).then_inc(up_done, 1)
                wait_for(pe, gathered, 16 * e + 32)
                turn_rows(xg[:, jn], 0, x_turned)
                wait_for(pe, hid_done, e + 1)
                wait_for(pe, hidt_done, e)
                for k in range(FE // P):
                    mm = pe.transpose(bank[4][:, k * P:(k + 1) * P], small[:, 1, k * P:(k + 1) * P], ident)
                mm.then_inc(hid_turned, 1)
                turn_rows(xg[:, jn], 1, x_turned)
                wait_for(pe, piece_loaded[slot[2][0]], 16 * i + 16 * slot[2][1])
                wait_for(pe, hidt_done, e + 1)
                for n in range(2):
                    wait_for(pe, (y_low, y_high)[n], e)
                    product(bank[5 + n][:], [(small[:, 2, k * P:(k + 1) * P], dw[:, k, n * 512:(n + 1) * 512])
                                             for k in range(FE // P)]).then_inc(down_done, 1)

        expert_pair(0)
        with pe.Fori(1, NE // 2) as i:
            expert_pair(i)
        n_over = pe.value_load(over[0:1, 8:9], min_val=0, max_val=NOVER)
        with pe.Fori(0, NOVER) as i:
            with pe.If(i < n_over):
                gw, uw = (ring[:, k].rearrange("p (k n) -> p k n", k=KD) for k in range(2))
                dw = ring[:, 2].rearrange("p (k n) -> p k n", k=FE // P)
                pe.wait_ge(xt_low, NE + 1)
                pe.wait_ge(xt_high, NE + 1)
                pe.wait_ge(ov["gathered"], 16 * i + 16)
                turn_rows(xg[:, 0], 0, ov["turned"])
                turn_rows(xg[:, 0], 1, ov["turned"])
                pe.wait_ge(ov["xt"], 2 * i + 2)
                pe.wait_ge(ov["loaded"], 48 * i + 48)
                product(bank[2][:], [(xgt[:, 0, k, :], gw[:, k, :]) for k in range(KD)]).then_inc(ov["gate"], 1)
                product(bank[3][:], [(xgt[:, 0, k, :], uw[:, k, :]) for k in range(KD)]).then_inc(ov["up"], 1)
                pe.wait_ge(ov["hid"], i + 1)
                for k in range(FE // P):
                    mm = pe.transpose(bank[4][:, k * P:(k + 1) * P], small[:, 1, k * P:(k + 1) * P], ident)
                mm.then_inc(ov["hid_turned"], 1)
                pe.wait_ge(ov["hidt"], i + 1)
                pe.wait_ge(y_low, NE)
                pe.wait_ge(y_high, NE)
                for n in range(2):
                    product(bank[5 + n][:], [(small[:, 2, k * P:(k + 1) * P], dw[:, k, n * 512:(n + 1) * 512])
                                             for k in range(FE // P)]).then_inc(ov["down"], 1)
                pe.wait_ge(ov["y"], 2 * i + 2)
        pe.wait_ge(xt_low, NE + 1)
        pe.wait_ge(xt_high, NE + 1)
        pe.wait_ge(y_low, NE)
        pe.wait_ge(y_high, NE)
        for s in BACK:
            front_step(s)

    @block.scalar
    def _(act):
        def square_sums(n, src, junk, wait):
            for t in range(NT):
                wait(t)
                act.activation(junk[:, t], src[:, t], ACT.Square, accum_out=stat[:, t:t + 1]).then_inc(sumsq, 1)
            act.wait_ge(rvar, n + 1)
            act.activation(stat[:, 8:12], stat[:, 4:8], ACT.Sqrt).then_inc(root, 1)

        def step(s):
            kind, a, i = s
            if s not in BANK:
                if kind == "norm" and a == "ffn":
                    def wait(t):
                        drained(act, ("out", 0, t))
                        drained(act, ("out", 1, t))
                        if t == 0:
                            for k in range(KD):
                                filled(act, ("turn", "merged", k))
                    square_sums(1, xres, stage_tok, wait)
                elif kind == "norm" and a == "ple":
                    def wait(t):
                        act.wait_ge(pairs_added, t + 1)
                        act.wait_ge(h2_out, 16)
                    square_sums(2, xres, stage_tok, wait)
                elif kind == "norm" and a == "final":
                    def wait(t):
                        act.wait_ge(ple_added, 2 * t + 2)
                        if t == 0:
                            for k in range(KD):
                                filled(act, ("turn", "h3", k))
                    square_sums(3, xres, stage_tok, wait)
                return
            b = BANK[s][0]
            if kind == "turn":
                if not act_evacuates(s):
                    return
                ps = filled(act, s)
                act.copy(turn_dst(s), ps[:]).then_inc(bank_drained[b], 1)
            elif kind == "z":
                ps = filled(act, s)
                if a in ROPES and ROPES.index(a) >= 2 and i == 0:
                    prev = ROPES[ROPES.index(a) - 2]
                    for cc in range(1 if prev == "ix" else NT):
                        filled(act, ("turn", prev, cc))
                if a == "ix":
                    act.copy(stage_z[:, 1, i, 0:HD], ps[:, 0:HD])
                    act.copy(stage_z[:, 1, i, HD:2 * HD], ps[:, 0:HD])
                    act.activation(iws[:, i, :], ps[:, HD:HD + NH], ACT.Copy, scale=float(np.float32(NH ** -0.5))
                                   ).then_inc(bank_drained[b], 1)
                elif a in ("va", "vb"):
                    if a == "vb" and i == 0:
                        filled(act, ("pv", "a", NU - 1))
                    act.copy(v_sb[:, i, :], ps[:]).then_inc(bank_drained[b], 1)
                else:
                    act.copy(stage_z[:, STAGE[a], i, :], ps[:]).then_inc(bank_drained[b], 1)
            elif kind == "rel":
                n = (a - 1) * NH + i
                ps = filled(act, s)
                if n >= 2:
                    act.wait_ge(acc_done, n - 1)
                act.activation(small[:, n % 2, 0:(a + 1) * P], ps[:, 0:(a + 1) * P], ACT.Relu, scale=HD ** -0.5
                               ).then_inc(bank_drained[b], 1)
            elif kind == "scores":
                h, t = unit(i)
                n = NU * BR[a] + i
                drained(act, s)
                if i >= 2:
                    filled(act, ("turn_p", a, i - 2))
                act.activation(small[:, 2 + i % 2, 0:(t + 1) * P], small[:, i % 2, 0:(t + 1) * P], ACT.Exp,
                               bias=nm[:, i % 4:i % 4 + 1], scale=-1.0, accum_out=rs[:, i % 4:i % 4 + 1]
                               ).then_inc(exp_done, 1)
            elif kind == "turn_p":
                if i % 2:
                    return
                h, t = unit(i)
                ps = filled(act, s)
                if i >= 2:
                    filled(act, ("pv", a, i - 2))
                act.copy(small[:, 4 + i % 2, 0:(t + 1) * P], ps[:, 0:(t + 1) * P]).then_inc(bank_drained[b], 1)
            elif kind.startswith("gate_") or kind == "ple_gate":
                n = GATES.index(s)
                ps = filled(act, s)
                if n >= 2:
                    drained(act, BRANCHES[n - 2])
                act.activation(small[:, n % 2, :], ps[:], ACT.Sigmoid).then_inc(bank_drained[b], 1)

        square_sums(0, stage_tok, junk0, lambda t: act.wait_ge(x_in, 16) if t == 0 else None)
        act.dma_start(wr[:, :, 0:NG], w_grp[0].rearrange("(k p) n -> p k n", p=P)).then_inc(small_in, 16)
        act.dma_start(wr[:, :, NG:NG + NE], w_rt[0].rearrange("(k p) n -> p k n", p=P)).then_inc(small_in, 16)
        act.dma_start(br[:, 0:NG], b_grp[0:1, :].partition_broadcast(P)).then_inc(small_in, 16)
        act.dma_start(br[:, NG:NG + NE], b_rt[0:1, :].partition_broadcast(P)).then_inc(small_in, 16)
        for s in FRONT:
            if s == ("turn", "oa", 0):
                act.wait_ge(normed, NT)
                act.dma_start(gain[:], g_ffn[0:1, :].partition_broadcast(P)).then_inc(gain_in, 16)
            if s == ("gate_a", 0, 0):
                for x_ in "ab":
                    for cc in range(NT):
                        filled(act, ("turn", "o" + x_, cc))
                act.dma_start(xres, x[0].rearrange("(t p) d -> p t d", p=P)).then_inc(x_back, 16)
            step(s)
        act.wait_ge(normed, 2 * NT)
        act.dma_start(h2_d.rearrange("(t p) d -> p t d", p=P), stage_tok).then_inc(h2_out, 16)
        act.dma_start(gain[:], g_ple[0:1, :].partition_broadcast(P)).then_inc(gain_in, 16)
        act.wait_ge(fill_ready, 1)
        act.dma_start(table_d.rearrange("(p n) w -> p (n w)", p=P), table[:, 0:NE * CH, :].rearrange("p n w -> p (n w)")
                      ).then_inc(table_filled, 16)
        act.wait_ge(ngmax_done, 1)
        for t in range(NT):
            ins = act.activation(rs_small[:, 4 * NT + NG * t:4 * NT + NG * (t + 1)], logits[:, t, 0:NG], ACT.Exp,
                                 bias=rs_small[:, t:t + 1], accum_out=rs_small[:, NT + t:NT + t + 1])
        ins.then_inc(gexp_done, 1)
        act.wait_ge(e2_done, 1)
        act.activation(rs_small[:, 3 * NT:4 * NT], rs_small[:, 2 * NT:3 * NT], ACT.Exp).then_inc(gexp_done, 1)
        act.wait_ge(table_written, 16 * 2 * NT)
        act.dma_start(table[:, 0:NE * CH, :].rearrange("p n w -> p (n w)"), table_d.rearrange("(p n) w -> p (n w)", p=P)
                      ).then_inc(table_in, 16)

        act.wait_ge(x_turned, 1)
        act.copy(xgt[:, 0, 0:4, :].rearrange("p k s -> p (k s)"), bank[0][:]).then_inc(xt_low, 1)
        def expert_pair(i):
            for j in range(2):
                e = 2 * i + j
                wait_for(act, gate_done, e + 1)
                wait_for(act, hid_done, e)
                act.activation(small[:, 0, :], bank[2][:], ACT.Silu).then_inc(silu_done, 1)
                wait_for(act, x_turned, 2 * e + 3)
                wait_for(act, up_done, e)
                act.copy(xgt[:, 1 - j, 0:4, :].rearrange("p k s -> p (k s)"), bank[0][:]).then_inc(xt_low, 1)
                wait_for(act, down_done, 2 * e + 1)
                wait_for(act, scattered, 16 * e)
                act.activation(y_sb[:, j, 0:512], bank[5][:], ACT.Copy, scale=slots[:, j, 2:3].bitcast(F32)
                               ).then_inc(y_low, 1)

        expert_pair(0)
        with act.Fori(1, NE // 2) as i:
            expert_pair(i)
        act.wait_ge(over_list, 1)
        n_over = act.value_load(over[0:1, 8:9], min_val=0, max_val=NOVER)
        with act.Fori(0, NOVER) as i:
            with act.If(i < n_over):
                act.wait_ge(ov["turned"], 2 * i + 1)
                act.copy(xgt[:, 0, 0:4, :].rearrange("p k s -> p (k s)"), bank[0][:]).then_inc(ov["xt"], 1)
                act.wait_ge(ov["gate"], i + 1)
                act.activation(small[:, 0, :], bank[2][:], ACT.Silu).then_inc(ov["silu"], 1)
                act.wait_ge(ov["down"], 2 * i + 1)
                act.activation(y_sb[:, 0, 0:512], bank[5][:], ACT.Copy, scale=slots[:, 0, 2:3].bitcast(F32)
                               ).then_inc(ov["y"], 1)
                act.wait_ge(ov["scattered"], 16 * i + 16)
                act.sem_inc(ov["act_end"], 1)
        act.wait_ge(scattered, 16 * NE)
        act.dma_start(pin, p[0, 0].rearrange("(t p) d -> p t d", p=P)).then_inc(p_in, 16)
        for s in BACK:
            if s == ("turn", "h3", 0):
                act.wait_ge(normed, 3 * NT)
                act.dma_start(gain[:], g_final.rearrange("(a d) -> a d", a=1).partition_broadcast(P)).then_inc(gain_in, 16)
            step(s)

    @block.vector
    def _(dve):
        chain = [0]

        def link(ins):
            chain[0] += 1
            ins.then_inc(dve_chain, 1)
            dve.wait_ge(dve_chain, chain[0])

        def norm(n, src, dst, wait):
            dve.wait_ge(sumsq, NT * (n + 1))
            ms, v, y, a, b2 = (stat[:, 4 * k:4 * k + 4] for k in (0, 3, 2, 4, 5))
            link(dve.tensor_scalar(v, ms, 1.0 / D, EPS, ALU.mult, ALU.add))
            dve.reciprocal(stat[:, 4:8], v).then_inc(rvar, 1)
            dve.wait_ge(root, n + 1)
            link(dve.tensor_tensor(a, y, y, ALU.mult))
            link(dve.tensor_tensor(b2, a, v, ALU.mult))
            link(dve.tensor_scalar(a, b2, -0.5, 1.5, ALU.mult, ALU.add))
            link(dve.tensor_tensor(b2, y, a, ALU.mult))
            dve.wait_ge(gain_in, 16 * (n + 1))
            wait()
            for t in range(NT):
                dve.scalar_tensor_tensor(out=dst[:, t], in0=src[:, t], scalar=stat[:, 20 + t:21 + t], in1=gain[:],
                                         op0=ALU.mult, op1=ALU.mult).then_inc(normed, 1)

        def step(s):
            kind, a, i = s
            if kind == "norm":
                if a == "ffn":
                    norm(1, xres, stage_tok, lambda: None)
                elif a == "ple":
                    norm(2, xres, stage_tok, lambda: None)
                else:
                    norm(3, xres, stage_tok, lambda: None)
                return
            if kind == "topk":
                topk()
                return
            if s not in BANK:
                return
            b = BANK[s][0]
            if kind == "turn":
                if act_evacuates(s):
                    return
                ps = filled(dve, s)
                dve.tensor_copy(turn_dst(s), ps[:]).then_inc(bank_drained[b], 1)
            elif kind == "rel":
                t, h = a, i
                n = (t - 1) * NH + h
                w = (t + 1) * P
                drained(dve, s)
                if h == 0:
                    base = c("causal")[:, (NT - t) * P:(NT + 1) * P]
                else:
                    base = score(t)
                    dve.wait_ge(acc_done, n)
                dve.scalar_tensor_tensor(out=score(t), in0=small[:, n % 2, 0:w], scalar=iws[:, t, h:h + 1],
                                         in1=base, op0=ALU.mult, op1=ALU.add).then_inc(acc_done, 1)
            elif kind == "scores":
                h, t = unit(i)
                w = (t + 1) * P
                n = NU * BR[a] + i
                ps = filled(dve, s)
                if i >= 2:
                    dve.wait_ge(exp_done, n - 1)
                bias = score(t) if a == "b" and t else c("causal")[:, (NT - t) * P:(NT + 1) * P]
                dve.tensor_tensor_reduce(out=small[:, i % 2, 0:w], in0=ps[:, 0:w], in1=bias, scale=-HD ** -0.5,
                                         scalar=3.0e38, op0=ALU.add, op1=ALU.min, accum_out=nm[:, i % 4:i % 4 + 1]
                                         ).then_inc(bank_drained[b], 1)
            elif kind == "turn_p":
                if not i % 2:
                    return
                h, t = unit(i)
                ps = filled(dve, s)
                if i >= 2:
                    filled(dve, ("pv", a, i - 2))
                dve.tensor_copy(small[:, 4 + i % 2, 0:(t + 1) * P], ps[:, 0:(t + 1) * P]).then_inc(bank_drained[b], 1)
            elif kind == "pv":
                h, t = unit(i)
                link(dve.reciprocal(ri[:, i % 4:i % 4 + 1], rs[:, i % 4:i % 4 + 1]))
                ps = filled(dve, s)
                dve.tensor_scalar(o_sb[a][:, t, h * HD:(h + 1) * HD], ps[:, 0:HD], ri[:, i % 4:i % 4 + 1], None, ALU.mult
                                  ).then_inc(bank_drained[b], 1)
            elif kind.startswith("branch_"):
                x_ = kind[-1]
                n = BRANCHES.index(s)
                drained(dve, ("gate_" + x_, a, i))
                ps = filled(dve, s)
                g = small[:, n % 2, :]
                dst = stage_tok[:, i, a * 512:(a + 1) * 512]
                if x_ == "a":
                    dve.tensor_tensor(dst, g, ps[:], ALU.mult).then_inc(bank_drained[b], 1)
                else:
                    dve.tensor_tensor(small[:, 2 + n % 2, :], g, ps[:], ALU.mult).then_inc(bank_drained[b], 1)
                    drained(dve, s)
                    drained(dve, ("branch_a", a, i))
                    dve.tensor_tensor(dst, dst, small[:, 2 + n % 2, :], ALU.add).then_inc(merged_done, 1)
            elif kind == "out":
                n, t = a, i
                ps = filled(dve, s)
                dve.wait_ge(x_back, 16)
                dst = xres[:, t, n * 512:(n + 1) * 512]
                dve.tensor_tensor(dst, dst, ps[:], ALU.add).then_inc(bank_drained[b], 1)
            elif kind == "ple_proj":
                n = BRANCHES.index(s)
                nn, t = a, i
                drained(dve, ("ple_gate", a, i))
                ps = filled(dve, s)
                dve.tensor_tensor(small[:, 2 + n % 2, :], small[:, n % 2, :], ps[:], ALU.mult).then_inc(bank_drained[b], 1)
                drained(dve, s)
                dst = xres[:, t, nn * 512:(nn + 1) * 512]
                dve.tensor_tensor(dst, dst, small[:, 2 + n % 2, :], ALU.add).then_inc(ple_added, 1)

        def topk():
            rounds = DSA_TOPK // 8
            dve.wait_ge(acc_done, (NT - 1) * NH)
            for r in range(rounds):
                for t in range(1, NT):
                    if r:
                        dve.wait_ge(mark_done, (NT - 1) * (r - 1) + t)
                    dve.max(m8[:, t, :], score(t)).then_inc(max_done, 1)
                for t in range(1, NT):
                    dve.wait_ge(max_done, (NT - 1) * r + t)
                    dve.match_replace(score(t), m8[:, t, :], score(t), MARK).then_inc(mark_done, 1)
            for t in range(1, NT):
                dve.wait_ge(mark_done, (NT - 1) * (rounds - 1) + t)
                dve.tensor_scalar(score(t), score(t), 0.9 * MARK, NEG, ALU.is_gt, ALU.mult).then_inc(selected, 1)
            dve.wait_ge(selected, NT - 1)

        def route():
            def small_col(n):
                return rs_small[:, n * NT:(n + 1) * NT]

            def spread(v, k):
                return v.unsqueeze(2).to_broadcast([P, NT, k])

            def first_largest(dst, src, top, desc, k, tmp):
                link(dve.tensor_reduce(top, src, AX.X, ALU.max))
                link(dve.tensor_tensor(tmp, src, spread(top, k), ALU.is_equal))
                link(dve.tensor_tensor(tmp, tmp, desc, ALU.mult))
                link(dve.tensor_reduce(small_col(9), tmp, AX.X, ALU.max))
                link(dve.tensor_tensor(dst, tmp, spread(small_col(9), k), ALU.is_equal))

            def block_(n, k=NE):
                return rt[:, n * NT * NE:n * NT * NE + NT * k].rearrange("p (t k) -> p t k", t=NT)

            masked, m1, m2, tmp, group, pen = block_(0), block_(1), block_(2), block_(3), block_(5, NG), block_(6, NG)
            gmax, v1, v2 = small_col(8), small_col(10), small_col(11)
            r_ = BANK[("router", 0, 0)][0]
            ps = filled(dve, ("router", 0, 0))
            dve.wait_ge(small_in, 64)
            dve.tensor_tensor(logits, ps[:, 0:NT * (NG + NE)].rearrange("p (t k) -> p t k", t=NT),
                              br[:].unsqueeze(1).to_broadcast([P, NT, NG + NE]), ALU.add).then_inc(bank_drained[r_], 1)
            drained(dve, ("router", 0, 0))
            first_largest(group, logits[:, :, 0:NG], gmax, c4("desc_group", NG), NG, block_(7, NG))
            dve.tensor_scalar(small_col(0), gmax, -1.0, None, ALU.mult).then_inc(ngmax_done, 1)
            link(dve.tensor_scalar(pen, group, -1.0, -NEG, ALU.add, ALU.mult))
            for g in range(NG):
                ins = dve.tensor_tensor(masked[:, :, g * EPG:(g + 1) * EPG],
                                        logits[:, :, NG + g * EPG:NG + (g + 1) * EPG],
                                        pen[:, :, g:g + 1].to_broadcast([P, NT, EPG]), ALU.add)
            link(ins)
            first_largest(m1, masked, v1, c4("desc_expert", NE), NE, tmp)
            link(dve.scalar_tensor_tensor(out=masked, in0=m1, scalar=NEG, in1=masked, op0=ALU.mult, op1=ALU.add))
            first_largest(m2, masked, v2, c4("desc_expert", NE), NE, tmp)
            dve.tensor_tensor(small_col(2), v2, v1, ALU.subtract).then_inc(e2_done, 1)
            dve.tensor_tensor(member, m1, m2, ALU.add).then_inc(top_done, 1)
            dve.wait_ge(top_done, 1)
            dve.tensor_copy(member_wide.rearrange("p t (e c) -> p (t e) c", c=CH),
                            member.rearrange("p t e -> p (t e)").unsqueeze(2).to_broadcast([P, NT * NE, CH])
                            ).then_inc(top_done, 1)
            dve.wait_ge(fill_ready, 2)
            dve.wait_ge(gexp_done, 2)
            link(dve.tensor_scalar(small_col(12), small_col(3), 1.0, None, ALU.add))
            link(dve.reciprocal(small_col(13), small_col(12)))
            link(dve.reciprocal(small_col(14), small_col(1)))
            wv = [rows[:, k * NT:(k + 1) * NT, 2].bitcast(F32) for k in range(2)]
            link(dve.tensor_tensor(wv[0], small_col(13), small_col(14), ALU.mult))
            link(dve.tensor_tensor(wv[1], wv[0], small_col(3), ALU.mult))
            dve.wait_ge(rank_done, 1)
            nec = NE * CH
            for k, m in enumerate((m1, m2)):
                rank, chunk, at = small_col(16 + 4 * k), small_col(17 + 4 * k), small_col(18 + 4 * k)
                link(dve.tensor_tensor(tmp, m, bank[1][:, 0:NT * NE].rearrange("p (t e) -> p t e", t=NT), ALU.mult))
                link(dve.tensor_reduce(rank, tmp, AX.X, ALU.add))
                link(dve.tensor_tensor(tmp, m, c4("four_e", NE), ALU.mult))
                link(dve.tensor_reduce(at, tmp, AX.X, ALU.add))
                link(dve.tensor_scalar(chunk, rank, float(P), None, ALU.is_ge))
                for cc in range(2, CH):
                    link(dve.scalar_tensor_tensor(out=chunk, in0=rank, scalar=float(cc * P), in1=chunk,
                                                  op0=ALU.is_ge, op1=ALU.add))
                link(dve.scalar_tensor_tensor(out=at, in0=rank, scalar=float(nec), in1=at, op0=ALU.mult, op1=ALU.add))
                link(dve.scalar_tensor_tensor(out=at, in0=chunk, scalar=float(1 - P * nec), in1=at,
                                              op0=ALU.mult, op1=ALU.add))
                link(dve.tensor_copy(dest[:, k * NT:(k + 1) * NT], at))
                link(dve.tensor_copy(rows[:, k * NT:(k + 1) * NT, 0], c("token")))
                link(dve.tensor_scalar(rows[:, k * NT:(k + 1) * NT, 1], c("token"), 2.0, float(k), ALU.mult, ALU.add))
            dve.sem_inc(rows_ready, 1)
            dve.wait_ge(count_done, 1)
            dve.tensor_tensor(over_f[:, 0:1], bank[2][:, 0:1], c("limit"), ALU.is_gt).then_inc(member_f, 1)
            dve.wait_ge(list_done, 1)
            link(dve.tensor_copy(over_f[:, 1:2], bank[3][:, 0:1]))
            dve.tensor_scalar(over_f[:, 8:16], c("iota8"), over_f[:, 1:2], over_f[:, 0:1], ALU.is_equal, ALU.mult
                              ).then_inc(member_f, 1)
            dve.wait_ge(list_done, 2)
            link(dve.tensor_copy(over[0:1, 0:8], bank[4][0:1, 0:8]))
            dve.tensor_copy(over[0:1, 8:9], bank[5][0:1, 0:1]).then_inc(over_list, 1)

        dve.memset(table[:], OOB).then_inc(fill_ready, 1)
        dve.memset(rows[:], 0).then_inc(fill_ready, 1)
        norm(0, stage_tok, stage_tok, lambda: None)
        for s in FRONT:
            step(s)
        route()
        dve.wait_ge(x_turned, 2)
        dve.tensor_copy(xgt[:, 0, 4:8, :].rearrange("p k s -> p (k s)"), bank[1][:]).then_inc(xt_high, 1)
        def expert_pair(i):
            for j in range(2):
                e = 2 * i + j
                wait_for(dve, silu_done, e + 1)
                wait_for(dve, up_done, e + 1)
                wait_for(dve, hid_turned, e)
                dve.tensor_tensor(small[:, 1, :], small[:, 0, :], bank[3][:], ALU.mult).then_inc(hid_done, 1)
                wait_for(dve, hid_turned, e + 1)
                wait_for(dve, down_done, 2 * e)
                dve.tensor_copy(small[:, 2, :], bank[4][:]).then_inc(hidt_done, 1)
                wait_for(dve, x_turned, 2 * e + 4)
                dve.tensor_copy(xgt[:, 1 - j, 4:8, :].rearrange("p k s -> p (k s)"), bank[1][:]).then_inc(xt_high, 1)
                wait_for(dve, down_done, 2 * e + 2)
                wait_for(dve, scattered, 16 * e)
                dve.tensor_scalar(y_sb[:, j, 512:1024], bank[6][:], slots[:, j, 2:3].bitcast(F32), None, ALU.mult
                                  ).then_inc(y_high, 1)

        expert_pair(0)
        with dve.Fori(1, NE // 2) as i:
            expert_pair(i)
        dve.wait_ge(over_list, 1)
        n_over = dve.value_load(over[0:1, 8:9], min_val=0, max_val=NOVER)
        with dve.Fori(0, NOVER) as i:
            with dve.If(i < n_over):
                dve.wait_ge(ov["turned"], 2 * i + 2)
                dve.tensor_copy(xgt[:, 0, 4:8, :].rearrange("p k s -> p (k s)"), bank[1][:]).then_inc(ov["xt"], 1)
                dve.wait_ge(ov["silu"], i + 1)
                dve.wait_ge(ov["up"], i + 1)
                dve.tensor_tensor(small[:, 1, :], small[:, 0, :], bank[3][:], ALU.mult).then_inc(ov["hid"], 1)
                dve.wait_ge(ov["hid_turned"], i + 1)
                dve.tensor_copy(small[:, 2, :], bank[4][:]).then_inc(ov["hidt"], 1)
                dve.wait_ge(ov["down"], 2 * i + 2)
                dve.tensor_scalar(y_sb[:, 0, 512:1024], bank[6][:], slots[:, 0, 2:3].bitcast(F32), None, ALU.mult
                                  ).then_inc(ov["y"], 1)
        for t in range(NT):
            dve.wait_ge(pairs_in[t % 2], 16 * (t // 2 + 1))
            link(dve.tensor_tensor(y_in[:, t % 2, 0:D], y_in[:, t % 2, 0:D], y_in[:, t % 2, D:2 * D], ALU.add))
            dve.tensor_tensor(xres[:, t], xres[:, t], y_in[:, t % 2, 0:D], ALU.add).then_inc(pairs_added, 1)
        for s in BACK:
            step(s)

    @block.gpsimd
    def _(pool):
        chain = [0]

        def link(ins):
            chain[0] += 1
            ins.then_inc(pool_chain, 1)
            pool.wait_ge(pool_chain, chain[0])

        def rope(name):
            heads = 2 if name == "ix" else NH
            z = stage_z[:, STAGE[name]].rearrange("p t (h d) -> p t h d", d=HD)[:, :, 0:heads]
            x1, x2 = z[:, :, :, 0:HALF], z[:, :, :, HALF:ROT]
            cos, sin = (c(n).rearrange("p (t h d) -> p t h d", t=NT, h=NH)[:, :, 0:heads] for n in ("cos", "sin"))
            part = [rope_t[:, :, 0:heads, k * HALF:(k + 1) * HALF] for k in range(4)]
            for t in range(NT):
                drained(pool, ("z", name, t))
            for k, (xx, f) in enumerate(((x1, cos), (x2, sin), (x2, cos), (x1, sin))):
                link(pool.tensor_tensor(part[k], xx, f, ALU.mult))
            link(pool.tensor_tensor(x1, part[0], part[1], ALU.subtract))
            link(pool.tensor_tensor(x2, part[2], part[3], ALU.add))
            pool.sem_inc(roped, 1)

        pool.wait_ge(const_in, 16)
        for s in FRONT:
            if s[0] == "rope":
                rope(s[1])
        filled(pool, ("router", 0, 0))
        link(pool.memset(wide_t[:, 0:2 * D], 0.0))
        pool.wait_ge(rows_ready, 1)
        pool.wait_ge(table_filled, 16)
        for n in range(2 * NT):
            pool.indirect_dma_start(out=table_d, out_offset=bass.IndirectOffsetOnAxis(ap=dest[:, n:n + 1], axis=0),
                                    in_=rows[:, n, :], in_offset=None, bounds_check=P * NE * CH - 1,
                                    oob_is_err=False).then_inc(table_written, 16)

        def gather(b, done):
            pool.sem_inc(pool_steps, 1)
            pool.indirect_dma_start(out=xg[:, b], out_offset=None, in_=h2_d,
                                    in_offset=bass.IndirectOffsetOnAxis(ap=slots[:, b, 0:1], axis=0),
                                    bounds_check=S - 1, oob_is_err=False).then_inc(done, 16)

        def scatter(b, done):
            pool.sem_inc(pool_steps, 1)
            pool.indirect_dma_start(out=pairs_d, out_offset=bass.IndirectOffsetOnAxis(ap=slots[:, b, 1:2], axis=0),
                                    in_=y_sb[:, b], in_offset=None,
                                    bounds_check=2 * S - 1, oob_is_err=False).then_inc(done, 16)

        pool.wait_ge(table_in, 16)
        pool.wait_ge(h2_out, 16)
        pool.tensor_copy(slots[:, 0, :], table[:, 0, :]).then_inc(slots_set, 1)
        pool.wait_ge(slots_set, 1)
        gather(0, gathered)
        def expert_pair(i):
            for j in range(2):
                e = 2 * i + j
                wait_for(pool, scattered, 16 * e)
                col = CH * (e + 1)
                pool.tensor_copy(slots[:, 1 - j, :].unsqueeze(1), table[:, bass.ds(col, 1), :]).then_inc(slots_set, 1)
                wait_for(pool, slots_set, e + 2)
                wait_for(pool, gathered, 16 * e + 16)
                wait_for(pool, x_turned, 2 * e)
                gather(1 - j, gathered)
                wait_for(pool, y_low, e + 1)
                wait_for(pool, y_high, e + 1)
                scatter(j, scattered)

        expert_pair(0)
        with pool.Fori(1, NE // 2) as i:
            expert_pair(i)
        pool.wait_ge(over_list, 1)
        n_over = pool.value_load(over[0:1, 8:9], min_val=0, max_val=NOVER)
        with pool.Fori(0, NOVER) as i:
            with pool.If(i < n_over):
                pool.wait_ge(scattered, 16 * NE)
                pool.wait_ge(x_turned, 2 * NE + 2)
                code = pool.value_load(over[0:1, bass.ds(i, 1)], min_val=0, max_val=NE * CH - 1)
                pool.tensor_copy(slots[:, 0, :].unsqueeze(1), table[:, bass.ds(code, 1), :]).then_inc(ov["slots"], 1)
                pool.wait_ge(ov["slots"], i + 1)
                gather(0, ov["gathered"])
                pool.wait_ge(ov["y"], 2 * i + 2)
                scatter(0, ov["scattered"])
                pool.wait_ge(ov["scattered"], 16 * i + 16)
                pool.sem_inc(ov["pool_end"], 1)

    block.__exit__(None, None, None)


_INS = ["x", "p", "g_attn", "w_in", "w_br_a", "w_br_b", "w_out", "g_ffn", "w_grp", "b_grp", "w_rt", "b_rt",
        "w_gate", "w_up", "w_down", "g_ple", "w_ple_gate", "w_ple_proj", "g_final"]


def kernel(**inputs):
    import concourse.bacc as bacc
    from concourse.bass_utils import run_bass_kernel_spmd

    nc = bacc.Bacc("TRN2", target_bir_lowering=False, num_devices=1)
    arrays, args = {}, []
    for name in _INS:
        a = np.ascontiguousarray(inputs[name])
        arrays[f"in_{name}"] = a
        args.append(nc.dram_tensor(f"in_{name}", a.shape, mybir.dt.from_np(a.dtype), kind="ExternalInput").ap())
    arrays["constants"] = constants()
    args.append(nc.dram_tensor("constants", (P, NCONST), F32, kind="ExternalInput").ap())
    out = nc.dram_tensor("out", (1, S, D), F32, kind="ExternalOutput").ap()
    layer_kernel(nc, *args, out)
    r = run_bass_kernel_spmd(nc, [arrays], core_ids=[0])
    return r.results[0]["out"]
```

```python
import numpy as np

import concourse.bass as bass
from concourse import mybir

ALU = mybir.AluOpType
ACT = mybir.ActivationFunctionType
AX = mybir.AxisListType
F32 = mybir.dt.float32
I32 = mybir.dt.int32
F32R = mybir.dt.float32r

P = 128
S = 512
D = 1024
NT = S // P
KD = D // P
HD = 64
NH = 8
AW = NH * HD
ROT = HD // 4
HALF = ROT // 2
THETA = 500000.0
DSA_TOPK = min(256, S // 4)
NG, EPG = 4, 8
NE = NG * EPG
FE = 512
PLE = 256
EPS = 1e-6
NEG = -1.0e30
MARK = -3.0e38
CH = NT
HALF_W = 2048
RAW = 4
SPLIT = 3
AHEAD = 2
FIRST = 64
NOVER = 4 * S // (P + 1)
OOB = 1 << 20

IN_OFF = dict(qa=0, ka=AW, va=2 * AW, qb=3 * AW, kb=4 * AW, vb=5 * AW, iq=6 * AW,
              ix=7 * AW, ga=7 * AW + HD + NH, gb=7 * AW + HD + NH + D)

CONST_COLS = {}
_at = 0
for _name, _n in (("ident", P), ("before", P), ("causal", 2 * P * (NT + 1) // 2), ("cos", NT * NH * HALF),
                  ("sin", NT * NH * HALF), ("ones", P), ("desc_group", NT * NG), ("desc_expert", NT * NE),
                  ("four_e", NT * NE), ("token", NT), ("code", 1), ("limit", 1), ("places", 16)):
    CONST_COLS[_name] = (_at, _at + _n)
    _at += _n
NCONST = _at


def constants():
    c = np.zeros((P, NCONST), np.float32)

    def put(name, value):
        a, b = CONST_COLS[name]
        c[:, a:b] = np.asarray(value, np.float32).reshape(P, b - a)

    row = np.arange(P)
    put("ident", np.eye(P))
    put("before", row[:, None] < row[None, :])
    causal = np.zeros((P, P * (NT + 1)), np.float32)
    causal[:, P * NT:] = np.where(row[None, :] <= row[:, None], 0.0, NEG)
    put("causal", causal)
    inv = (1.0 / (np.float32(THETA) ** (np.arange(0, ROT, 2, dtype=np.float32) / np.float32(ROT)))).astype(np.float32)
    ang = np.arange(S, dtype=np.float32)[:, None] * inv[None, :]
    for name, f in (("cos", np.cos), ("sin", np.sin)):
        t = f(ang).reshape(NT, P, 1, HALF).transpose(1, 0, 2, 3)
        put(name, np.broadcast_to(t, (P, NT, NH, HALF)))
    put("ones", np.ones((P, P)))
    put("desc_group", np.broadcast_to(NG - np.arange(NG), (P, NT, NG)))
    put("desc_expert", np.broadcast_to(NE - np.arange(NE), (P, NT, NE)))
    put("four_e", np.broadcast_to(CH * np.arange(NE), (P, NT, NE)))
    put("token", np.arange(NT)[None, :] * P + row[:, None])
    put("code", row)
    put("limit", np.where(row % CH == 0, FIRST, P * (row % CH)))
    put("places", np.broadcast_to(np.arange(16), (P, 16)))
    return c


def attention_steps(branch):
    units = [(h, t) for h in range(NH) for t in range(NT)]
    out = []
    for u in range(len(units) + 3):
        if u < len(units):
            out.append(("scores", branch, u))
        if 2 <= u < len(units) + 2:
            out.append(("turn_p", branch, u - 2))
        if u >= 3:
            out.append(("pv", branch, u - 3))
    return out


def front_steps():
    z = lambda name: [("z", name, i) for i in range(1 if name == "ix" else 2)]
    turn = lambda name, n: [("turn", name, c) for c in range(n)]
    rel = lambda t: [("rel", t, h) for h in range(NH)]
    st = turn("h", KD)
    st += z("iq") + [("rope", "iq", 0)] + z("ix") + [("rope", "ix", 0)]
    st += z("qa")[:1] + turn("iq", NT) + turn("ix", 1) + rel(1)
    st += z("qa")[1:] + [("rope", "qa", 0)] + rel(2)
    st += z("ka")[:1] + rel(3) + z("ka")[1:] + [("rope", "ka", 0)] + turn("qa", NT)
    rounds = [("topk", r, 0) for r in range(DSA_TOPK // 8)]
    for n, w in enumerate(z("va") + z("qb") + z("kb")):
        st += [w] + rounds[3 * n:3 * n + 3]
        if n == 0:
            st += turn("ka", NT)
        if w == ("z", "qb", 1):
            st += [("rope", "qb", 0)]
    st += [("select", 0, 0), ("rope", "kb", 0)]
    st += attention_steps("a")
    st += turn("qb", NT) + turn("kb", NT) + z("vb")
    st += attention_steps("b")
    st += turn("oa", NT) + turn("ob", NT)
    for n in range(2):
        for x in "ab":
            st += [("gate_" + x, n, 0), ("gate_" + x, n, 1), ("branch_" + x, n, 0)]
    st += turn("merged", KD)
    st += [("out", n, i) for n in range(2) for i in range(2)]
    st += [("norm", "ffn", 0)] + turn("p", PLE // P) + turn("h2", KD) + [("router", 0, 0)]
    return st


def back_steps():
    st = [("norm", "ple", 0)] + [("turn", "h3", c) for c in range(KD)]
    for n in range(2):
        st += [("ple_gate", n, 0), ("ple_gate", n, 1), ("ple_proj", n, 0)]
    st += [("norm", "final", 0)]
    return st


FRONT, BACK = front_steps(), back_steps()
WEIGHTS = ("z", "gate_a", "gate_b", "branch_a", "branch_b", "out", "ple_gate", "ple_proj")
N_EXP = 6 * NE
HALVES = [s for s in FRONT if s[0] in WEIGHTS]
N_FRONT = len(HALVES)
TAIL = [s for s in BACK if s[0] in WEIGHTS]
HALF_OF = {s: n for n, s in enumerate(HALVES)}
HALF_OF.update({s: N_FRONT + N_EXP + n for n, s in enumerate(TAIL)})
N_ALL = N_FRONT + N_EXP + len(TAIL)
LAST_OF = {"z": 1, "gate_a": 1, "gate_b": 1, "branch_a": 0, "branch_b": 0, "out": 1, "ple_gate": 1, "ple_proj": 0}


def last_half(s):
    return s[2] == (0 if s[1] == "ix" else LAST_OF[s[0]])


def place_banks():
    where, uses = {}, [0] * 8
    turns = rels = outs = 0
    for s in FRONT + BACK:
        kind = s[0]
        if kind in ("rope", "topk", "select", "norm"):
            continue
        if kind in WEIGHTS:
            if s[2] == 0:
                first = {"z": 0, "gate_a": 0, "gate_b": 0, "branch_a": 4, "branch_b": 4, "out": 4 * (s[1] == 1),
                         "ple_gate": 0, "ple_proj": 4}[kind]
                for t in range(NT):
                    uses[first + t] += 1
                    where[(kind, s[1], "tile", t)] = (first + t, uses[first + t])
            continue
        if kind == "turn":
            b = 4 + turns % 2
            turns += 1
        elif kind == "rel":
            b = 6 + rels % 2
            rels += 1
        elif kind == "scores":
            b = s[2] % 3
        elif kind == "turn_p":
            b = 4 + s[2] % 2
        elif kind == "pv":
            b = 6 + s[2] % 2
        else:
            b = 0
        uses[b] += 1
        where[s] = (b, uses[b])
    return where


BANK = place_banks()

GATES = [(s[0], s[1], t) for s in FRONT + BACK if s[0] in ("gate_a", "gate_b", "ple_gate") and s[2] for t in range(NT)]
BRANCHES = [(s[0], s[1], t) for s in FRONT + BACK if s[0] in ("branch_a", "branch_b", "ple_proj") for t in range(NT)]
ROPES = ["iq", "ix", "qa", "ka", "qb", "kb"]
STAGE = {name: n % 2 for n, name in enumerate(ROPES)}


SPLIT_TURNS = ("h", "oa", "ob", "merged", "h2", "h3", "p")


ROW_TURNS = ("h", "merged", "h2", "h3")


def tile_and_half(a, i):
    return (i % NT, i // NT) if a == "merged" else (i // 2, i % 2)


def raw_turn(n):
    return n % RAW, n // RAW + 1


def layer_kernel(nc, x, p, g_attn, w_in, w_br_a, w_br_b, w_out, g_ffn, w_grp, b_grp, w_rt, b_rt,
                 w_gate, w_up, w_down, g_ple, w_ple_gate, w_ple_proj, g_final, const, out):
    K = 1024
    base = (nc.sbuf_base + 31) // 32 * 32
    size = {"cst": 4 * NCONST, "raw": RAW * 8 * K, "whi": SPLIT * 8 * K, "wlo": SPLIT * 8 * K, "gain": 4 * K,
            "stage": 16 * K, "hi": 16 * K, "lo": 16 * K, "qk": 16 * K, "v": 8 * K, "rope": 4 * K, "work": 4 * K + 512,
            "o": 16 * K, "small": 12 * K, "ik": 2 * K, "misc": 6 * K}
    start = {}
    for name, n in size.items():
        start[name] = base
        base += (n + 31) // 32 * 32
    assert base <= nc.sbuf_usable_end, base

    def sb(name, region, shape, dt=F32, skip=0):
        return nc.alloc_sbuf_tensor_at(name, shape, dt, offset=start[region] + skip)

    misc_at = [0]

    def tiny(name, shape, dt=F32):
        n = 4 * int(np.prod(shape[1:]))
        at = misc_at[0]
        misc_at[0] += (n + 31) // 32 * 32
        assert misc_at[0] <= size["misc"], name
        return nc.alloc_sbuf_tensor_at(name, shape, dt, offset=start["misc"] + at)

    def sem(name):
        return nc.alloc_semaphore(name)

    cst = sb("cst", "cst", [P, NCONST])
    raw = sb("raw", "raw", [P, RAW, HALF_W])
    w_hi = sb("w_hi", "whi", [P, SPLIT, HALF_W], F32R)
    w_lo = sb("w_lo", "wlo", [P, SPLIT, HALF_W], F32R)
    gain = sb("gain", "gain", [P, D])
    stage_tok = sb("rows_tok", "stage", [P, NT, D])[:]
    stage_z = sb("z_chunks", "stage", [P, 2, NT, AW])[:]
    act_hi = sb("act_hi", "hi", [P, KD, S], F32R)
    act_lo = sb("act_lo", "lo", [P, KD, S], F32R)
    qt = sb("qt", "qk", [P, NT, S])[:]
    kt_ = sb("kt", "qk", [P, NT, S], skip=8 * K)[:]
    v_sb = sb("v", "v", [P, NT, AW])[:]
    rope_t = sb("rope_t", "rope", [P, NT, NH, 2 * ROT])
    work = sb("work", "work", [P, 9 * P])
    o_sb = {"a": sb("o_a", "o", [P, NT, AW])[:], "b": sb("o_b", "o", [P, NT, AW], skip=8 * K)[:]}
    iqt = sb("iqt", "o", [P, NT, S], skip=8 * K)[:]
    ikt = sb("ikt", "ik", [P, S])
    small = sb("small", "small", [P, 6, S])
    ot_hi = {x_: sb(f"ot_{x_}_hi", "qk", [P, NT, S], F32R, skip=8 * K * n)[:] for n, x_ in enumerate("ab")}
    ot_lo = {x_: sb(f"ot_{x_}_lo", "v", [P, NT, S], F32R, skip=8 * K * n)[:] for n, x_ in enumerate("ab")}
    xres = sb("x_after", "o", [P, NT, D])[:]
    junk0 = sb("squares", "o", [P, NT, D])[:]
    rt = sb("rt", "work", [P, 8 * NT * NE])
    xg = sb("xg", "stage", [P, 2, D])[:]
    y_sb = sb("y", "stage", [P, 2, D], skip=8 * K)[:]
    xt_hi = sb("xt_hi", "hi", [P, 2, KD, P], F32R)[:]
    xt_lo = sb("xt_lo", "hi", [P, 2, KD, P], F32R, skip=8 * K)[:]
    ht_hi = sb("ht_hi", "lo", [P, FE // P, P], F32R)[:]
    ht_lo = sb("ht_lo", "lo", [P, FE // P, P], F32R, skip=2 * K)[:]
    y_in = sb("y_in", "qk", [P, 2, 2 * D])[:]
    pin = sb("p_rows", "v", [P, NT, PLE])[:]
    pt_hi = sb("pt_hi", "v", [P, 2, S], F32R, skip=4 * K)[:]
    pt_lo = sb("pt_lo", "v", [P, 2, S], F32R, skip=8 * K)[:]

    iws = tiny("iws", [P, NT, NH])
    m8 = tiny("m8", [P, NT, 8])
    stat = tiny("stat", [P, 24])
    eps = tiny("eps", [P, 1])
    nm = tiny("nm", [P, 4])
    rs = tiny("rs", [P, 4])
    ri = tiny("ri", [P, 4])
    br = tiny("br", [P, NG + NE])
    table = tiny("table", [P, NE * CH + 2 * CH, 4], I32)
    row_of = tiny("row_of", [P, 2, 4], I32)
    pair_of = tiny("pair_of", [P, 2, 4], I32)
    rs_small = tiny("rs_small", [P, 32 * NT])
    rows = tiny("rows", [P, 2 * NT, 4], I32)
    dest = tiny("dest", [P, 2 * NT], I32)
    over_f = tiny("over_f", [P, 32])
    over = tiny("over", [P, 32], I32)
    wr = sb("wr", "ik", [P, KD, NG + NE])
    wr_hi = tiny("wr_hi", [P, KD, NG + NE], F32R)
    wr_lo = tiny("wr_lo", [P, KD, NG + NE], F32R)

    logits = small[:, 4, 0:NT * (NG + NE)].rearrange("p (t k) -> p t k", t=NT)
    member = rt[:, 4 * NT * NE:5 * NT * NE].rearrange("p (t e) -> p t e", t=NT)
    member_wide = small[:, 3, :].rearrange("p (t k) -> p t k", t=NT)
    score_at = {1: 0, 2: 2 * P, 3: 5 * P}

    def score(t):
        return work[:, score_at[t]:score_at[t] + (t + 1) * P]

    def turn_dst(s):
        _, a, i = s
        if a == "ix":
            return ikt[:]
        if a in ("iq", "qa", "qb", "ka", "kb"):
            return {"iq": iqt, "qa": qt, "qb": qt, "ka": kt_, "kb": kt_}[a][:, i, :]
        if a in ROW_TURNS:
            t, h = tile_and_half(a, i)
            return [v[:, 4 * h:4 * h + 4, t * P:(t + 1) * P] for v in (act_hi, act_lo)]
        hi, lo = {"oa": (ot_hi["a"], ot_lo["a"]), "ob": (ot_hi["b"], ot_lo["b"]), "p": (pt_hi, pt_lo)}[a]
        return hi[:, i, :], lo[:, i, :]

    def c(name):
        a, b = CONST_COLS[name]
        return cst[:, a:b]

    def c4(name, k):
        return c(name).rearrange("p (t k) -> p t k", k=k)

    ident = c("ident")

    psum = nc.alloc_psum_tensor("psum", [P, 8, S], F32)
    bank = [psum[:, b, :] for b in range(8)]

    h2_d = nc.dram_tensor("h2_rows", [S, D], F32, kind="Internal").ap()
    pairs_d = nc.dram_tensor("pair_rows", [2 * S, D], F32, kind="Internal").ap()
    table_d = nc.dram_tensor("slot_table", [P * NE * CH, 4], I32, kind="Internal").ap()

    bank_filled = [sem(f"bank_filled_{b}") for b in range(8)]
    bank_drained = [sem(f"bank_drained_{b}") for b in range(8)]
    raw_loaded = [sem(f"raw_loaded_{b}") for b in range(RAW)]
    hi_done, lo_done = sem("hi_done"), sem("lo_done")
    half_started = sem("half_started")
    turn_hi = sem("turn_hi")
    logits_t = sem("logits_t")
    wr_split, eps_set = sem("wr_split"), sem("eps_set")
    merged_done, ple_added = sem("merged_done"), sem("ple_added")
    ident_in, const_in, x_in = sem("ident_in"), sem("const_in"), [sem(f"x_in_{t}") for t in range(NT)]
    gain_in, small_in, p_in = sem("gain_in"), sem("small_in"), sem("p_in")
    sumsq, root, normed = sem("sumsq"), sem("root"), sem("normed")
    roped, pool_chain, dve_chain = sem("roped"), sem("pool_chain"), sem("dve_chain")
    relu_done, acc_done = sem("relu_done"), sem("acc_done")
    max_done, mark_done, selected = sem("max_done"), sem("mark_done"), sem("selected")
    exp_done = sem("exp_done")
    x_back, h2_out = sem("x_back"), sem("h2_out")
    ngmax_done, gexp_done, e2_done = sem("ngmax_done"), sem("gexp_done"), sem("e2_done")
    top_done, rank_done, count_done, list_done = sem("top_done"), sem("rank_done"), sem("count_done"), sem("list_done")
    member_f, over_list, rows_ready, fill_ready = sem("member_f"), sem("over_list"), sem("rows_ready"), sem("fill_ready")
    table_filled, table_written, table_in = sem("table_filled"), sem("table_written"), sem("table_in")
    rows_set, pairs_set, gathered, x_turned = sem("rows_set"), sem("pairs_set"), sem("gathered"), sem("x_turned")
    xt_hi_done, xt_done, gate_done, up_done = sem("xt_hi_done"), sem("xt_done"), sem("gate_done"), sem("up_done")
    silu_done, hid_done, hid_turned = sem("silu_done"), sem("hid_done"), sem("hid_turned")
    ht_hi_done, ht_done, down_done, y_done, scattered = (sem("ht_hi_done"), sem("ht_done"), sem("down_done"),
                                                         sem("y_done"), sem("scattered"))
    pairs_in, pairs_added = [sem("pairs_in_even"), sem("pairs_in_odd")], sem("pairs_added")
    ov = {n: sem("ov_" + n) for n in ("loaded", "hi", "lo", "started", "rows", "pairs", "gathered", "turned", "xt_hi", "xt",
                                      "gate", "up", "silu", "hid", "hid_turned", "ht_hi", "ht", "down", "y", "scattered",
                                      "act_end", "sp_end", "pool_end", "pe_end")}
    out_done, pool_steps, sp_steps, pe_steps = sem("out_done"), sem("pool_steps"), sem("sp_steps"), sem("pe_steps")

    def claim(pe, step):
        b, n = BANK[step]
        if n > 1:
            pe.wait_ge(bank_drained[b], n - 1)
        return bank[b]

    def filled(eng, step):
        b, n = BANK[step]
        eng.wait_ge(bank_filled[b], n)
        return bank[b]

    def drained(eng, step):
        b, n = BANK[step]
        eng.wait_ge(bank_drained[b], n)

    def tile_of(s, t):
        return (s[0], s[1], "tile", t)

    def half_view(buf, n, k):
        w = HD + NH if n == HALF_OF[("z", "ix", 0)] else HALF_W // 4
        return buf[:, 0:k * w].rearrange("p (k n) -> p k n", k=k)

    def tiles_in(s):
        return KD if s[1] == "ix" else PLE // P if s[0] == "ple_proj" else 4

    def columns_of(n):
        if n == HALF_OF[("z", "ix", 0)]:
            return KD * (HD + NH)
        return HALF_W // 2 if n in (HALF_OF[("ple_proj", 0, 0)], HALF_OF[("ple_proj", 1, 0)]) else HALF_W

    def x_turns(n_rows):
        return psum[:, 0:2, :].rearrange("p b (k s) -> p (b k) s", k=4)[:, :, 0:n_rows]

    def h_turns(n_rows):
        return bank[4].rearrange("p (k s) -> p k s", k=FE // P)[:, :, 0:n_rows]

    def split_high(act, n, i=0):
        b, turns = raw_turn(n)
        act.wait_ge(raw_loaded[b], 16 * turns + 48 * i)
        if n >= SPLIT:
            act.wait_ge(half_started, n - 1 + 12 * i)
        w = columns_of(n)
        act.copy(w_hi[:, n % SPLIT, 0:w], raw[:, b, 0:w]).then_inc(hi_done, 1)

    def split_low(dve, n, i=0):
        dve.wait_ge(hi_done, n + 1 + 12 * i)
        w = columns_of(n)
        dve.tensor_tensor(w_lo[:, n % SPLIT, 0:w], raw[:, n % RAW, 0:w], w_hi[:, n % SPLIT, 0:w].bitcast(F32),
                          ALU.subtract).then_inc(lo_done, 1)

    EXPERT_HALVES = ("up0", "up1", "gate0", "gate1", "down0", "down1")
    LAST_HALVES = ("up0", "up1", "down0", "down1")
    OVER_HALVES = ("gate0", "gate1", "up0", "up1", "down0", "down1")
    BASE_E = N_FRONT + 2

    def wait_for(eng, sem_, value):
        if not isinstance(value, int) or value > 0:
            eng.wait_ge(sem_, value)

    def unit(u):
        return u // NT, u % NT

    BR = {"a": 0, "b": 1}
    NU = NH * NT
    block = nc.Block()
    block.__enter__()

    @block.sync
    def _(sp):
        w_in_v = w_in[0].rearrange("(k p) n -> p k n", p=P)
        x_v = x[0].rearrange("(t p) d -> p t d", p=P)
        by_rows = lambda w: w.rearrange("(k p) n -> p k n", p=P)

        def load(n, src, i=0):
            if n >= RAW:
                sp.wait_ge(lo_done, n - RAW + 1 + 12 * i)
                if not isinstance(i, int):
                    sp.sem_inc(sp_steps, 1)
            w = columns_of(n)
            k = src.shape[1]
            sp.dma_start(raw[:, n % RAW, 0:w].rearrange("p (k n) -> p k n", k=k), src).then_inc(raw_loaded[n % RAW], 16)

        def source(s):
            kind, a, i = s
            if kind == "z":
                if a == "ix":
                    return w_in_v[:, :, IN_OFF[a]:IN_OFF[a] + HD + NH]
                return w_in_v[:, 4 * i:4 * i + 4, IN_OFF[a]:IN_OFF[a] + 512]
            if kind in ("gate_a", "gate_b"):
                off = IN_OFF["g" + kind[-1]] + 512 * a
                return w_in_v[:, 4 * i:4 * i + 4, off:off + 512]
            w = {"branch_a": w_br_a, "branch_b": w_br_b, "out": w_out, "ple_gate": w_ple_gate, "ple_proj": w_ple_proj}[kind]
            k = tiles_in(s)
            return by_rows(w[0])[:, k * i:k * (i + 1), a * 512:(a + 1) * 512]

        sp.dma_start(stage_tok[:, 0], x_v[:, 0]).then_inc(x_in[0], 16)
        sp.dma_start(gain[:], g_attn[0:1, :].partition_broadcast(P)).then_inc(gain_in, 16)
        sp.dma_start(cst[:, 0:P], const[:, 0:P]).then_inc(ident_in, 16)
        for t in range(1, NT):
            sp.dma_start(stage_tok[:, t], x_v[:, t]).then_inc(x_in[t], 16)
        for n, s in enumerate(HALVES):
            load(n, source(s))
            if n == 1:
                sp.dma_start(cst[:, P:], const[:, P:]).then_inc(const_in, 16)
        views = {"gate": w_gate[0].rearrange("e (p k) f -> e p k f", p=P),
                 "up": w_up[0].rearrange("e (p k) f -> e p k f", p=P),
                 "down": w_down[0].rearrange("e (k p) d -> e p k d", p=P)}

        def expert_source(name, e):
            what, h = name[:-1], int(name[-1])
            v = views[what][e]
            return v[:, :, h * 512:(h + 1) * 512] if what == "down" else v[:, 4 * h:4 * h + 4, :]

        def load_expert(e0, i=0):
            e = e0 + 2 * i
            names = EXPERT_HALVES if e0 != NE - 1 else LAST_HALVES
            for r, name in enumerate(names):
                load(BASE_E + 6 * e0 + r, expert_source(name, e + 1 if name.startswith("gate") else e), i)

        load(N_FRONT, expert_source("gate0", 0))
        load(N_FRONT + 1, expert_source("gate1", 0))
        load_expert(0)
        with sp.Fori(0, NE // 2 - 1) as i:
            load_expert(1, i)
            load_expert(2, i)
        load_expert(NE - 1)
        sp.wait_ge(over_list, 1)
        n_over = sp.value_load(over[0:1, 16:17], min_val=0, max_val=NOVER)
        with sp.Fori(0, NOVER) as i:
            with sp.If(i < n_over):
                sp.wait_ge(lo_done, N_FRONT + N_EXP)
                code = sp.value_load(over[0:1, bass.ds(i, 1)], min_val=0, max_val=NE * CH - 1)
                e = sp.snap(code // CH, min_val=0, max_val=NE - 1)
                for r, name in enumerate(OVER_HALVES):
                    if r >= RAW:
                        sp.wait_ge(ov["lo"], 6 * i + (r - RAW + 1))
                        sp.sem_inc(sp_steps, 1)
                    if r:
                        sp.wait_ge(ov["loaded"], 96 * i + 16 * r)
                        sp.sem_inc(sp_steps, 1)
                    sp.dma_start(raw[:, r % RAW, :].rearrange("p (k n) -> p k n", k=4), expert_source(name, e)
                                 ).then_inc(ov["loaded"], 16)
                sp.wait_ge(ov["scattered"], 16 * i + 16)
                sp.sem_inc(ov["sp_end"], 1)
        sp.wait_ge(scattered, 16 * NE)
        for t in range(NT):
            if t >= 2:
                sp.wait_ge(pairs_added, t - 1)
            sp.dma_start(y_in[:, t % 2, :], pairs_d[t * 2 * P:(t + 1) * 2 * P].rearrange("(p k) d -> p (k d)", k=2)
                         ).then_inc(pairs_in[t % 2], 16)
            if t == 0:
                for n, s in enumerate(TAIL[:RAW]):
                    load(N_FRONT + N_EXP + n, source(s))
        for n, s in enumerate(TAIL[RAW:]):
            load(N_FRONT + N_EXP + RAW + n, source(s))
        out_v = out[0].rearrange("(t p) d -> p t d", p=P)
        for t in range(NT):
            sp.wait_ge(normed, 3 * NT + 1 + t)
            sp.dma_start(out_v[:, t], stage_tok[:, t]).then_inc(out_done, 16)
        sp.wait_ge(out_done, 16 * NT)

    @block.tensor
    def _(pe):
        def transposes(step, views):
            ps = claim(pe, step)
            for n, v in enumerate(views):
                mm = pe.transpose(ps[0:v.shape[1], n * P:(n + 1) * P], v, ident)
            mm.then_inc(bank_filled[BANK[step][0]], 1)

        def product(ps, pairs):
            for n, (a, b) in enumerate(pairs):
                mm = pe.matmul(ps, a, b, start=(n == 0), stop=(n == len(pairs) - 1))
            return mm

        def three(ps, left, right, first, last):
            ops = [(left[0], right[0]), (left[1], right[0]), (left[0], right[1])]
            mms = [pe.matmul(ps, a, b, start=first and n == 0, stop=last and n == 2) for n, (a, b) in enumerate(ops)]
            return mms[0], mms[2]

        def half_product(s, left, k0):
            n, k_n, last = HALF_OF[s], tiles_in(s), last_half(s)
            pe.wait_ge(lo_done, n + 1)
            hi, lo = half_view(w_hi[:, n % SPLIT], n, k_n), half_view(w_lo[:, n % SPLIT], n, k_n)
            w = hi.shape[2]
            for t in range(NT):
                b = BANK[tile_of(s, t)][0]
                if s[2] == 0:
                    claim(pe, tile_of(s, t))
                for k in range(k_n):
                    l_ = [v[:, k0 + k, t * P:(t + 1) * P] for v in left]
                    m0, m1 = three(bank[b][:, 0:w], l_, (hi[:, k, :], lo[:, k, :]), s[2] == 0 and k == 0,
                                   last and k == k_n - 1)
                    if t == 0 and k == 0:
                        m0.then_inc(half_started, 1)
                if last:
                    m1.then_inc(bank_filled[b], 1)

        def front_step(s):
            kind, a, i = s
            if kind in ("rope", "topk", "select", "norm"):
                return
            if kind == "turn":
                if s == ("turn", "h", 0):
                    pe.wait_ge(ident_in, 16)
                if a in ("h", "h2", "h3"):
                    pe.wait_ge(normed, NT * ("h", "h2", "h3").index(a) + tile_and_half(a, i)[0] + 1)
                elif a in ROPES and i == 0:
                    pe.wait_ge(roped, ROPES.index(a) + 1)
                elif a == "oa" and i == 0:
                    drained(pe, ("pv", "a", NU - 1))
                elif a == "ob" and i == 0:
                    drained(pe, ("pv", "b", NU - 1))
                    drained(pe, ("pv", "b", NU - 2))
                elif a == "merged":
                    pe.wait_ge(merged_done, i + 1)
                elif a == "p" and i == 0:
                    pe.wait_ge(p_in, 16)
                if a in ROW_TURNS:
                    t, h = tile_and_half(a, i)
                    views = [stage_tok[:, t, k * P:(k + 1) * P] for k in range(4 * h, 4 * h + 4)]
                elif a in ("oa", "ob"):
                    views = [o_sb[a[1]][:, t, i * P:(i + 1) * P] for t in range(NT)]
                elif a == "p":
                    views = [pin[:, t, i * P:(i + 1) * P] for t in range(NT)]
                else:
                    views = [stage_z[:, STAGE[a], t, i * P:(i + 1) * P] for t in range(NT)]
                transposes(s, views)
            elif kind == "z":
                if s == ("z", "iq", 0):
                    for k in range(KD):
                        drained(pe, ("turn", "h", k))
                half_product(s, (act_hi, act_lo), 4 * i)
            elif kind == "rel":
                t, h = a, i
                if (t, h) == (1, 0):
                    for cc in range(NT):
                        drained(pe, ("turn", "iq", cc))
                    drained(pe, ("turn", "ix", 0))
                ps = claim(pe, s)
                lo = HD * (h % 2)
                pe.matmul(ps[:, 0:(t + 1) * P], iqt[lo:lo + HD, h // 2, t * P:(t + 1) * P],
                          ikt[lo:lo + HD, 0:(t + 1) * P], start=True, stop=True
                          ).then_inc(bank_filled[BANK[s][0]], 1)
            elif kind == "scores":
                h, t = unit(i)
                if i == 0:
                    for cc in range(NT):
                        drained(pe, ("turn", "q" + a, cc))
                        drained(pe, ("turn", "k" + a, cc))
                ps = claim(pe, s)
                lo = HD * (h % 2)
                pe.matmul(ps[:, 0:(t + 1) * P], qt[lo:lo + HD, h // 2, t * P:(t + 1) * P],
                          kt_[lo:lo + HD, h // 2, 0:(t + 1) * P], start=True, stop=True
                          ).then_inc(bank_filled[BANK[s][0]], 1)
            elif kind == "turn_p":
                h, t = unit(i)
                pe.wait_ge(exp_done, NU * BR[a] + i + 1)
                transposes(s, [small[:, 2 + i % 2, j * P:(j + 1) * P] for j in range(t + 1)])
            elif kind == "pv":
                h, t = unit(i)
                if i == 0:
                    for tt in range(NT):
                        drained(pe, ("z", "v" + a, "tile", tt))
                drained(pe, ("turn_p", a, i))
                ps = claim(pe, s)
                mm = product(ps[:, 0:HD], [(small[:, 4 + i % 2, j * P:(j + 1) * P], v_sb[:, j, h * HD:(h + 1) * HD])
                                           for j in range(t + 1)])
                mm.then_inc(bank_filled[BANK[s][0]], 1)
            elif kind in ("gate_a", "gate_b"):
                half_product(s, (act_hi, act_lo), 4 * i)
            elif kind in ("branch_a", "branch_b"):
                x_ = kind[-1]
                if a == 0:
                    for cc in range(NT):
                        drained(pe, ("turn", "o" + x_, cc))
                half_product(s, (ot_hi[x_], ot_lo[x_]), 0)
            elif kind == "out":
                if (a, i) == (0, 0):
                    for k in range(KD):
                        drained(pe, ("turn", "merged", k))
                half_product(s, (act_hi, act_lo), 4 * i)
            elif kind == "router":
                pe.wait_ge(wr_split, 2)
                for k in range(KD):
                    drained(pe, ("turn", "h2", k))
                w = NG + NE
                for k in range(KD):
                    _, mm = three(bank[1][0:w, :], (wr_hi[:, k, :], wr_lo[:, k, :]), (act_hi[:, k, :], act_lo[:, k, :]),
                                  k == 0, k == KD - 1)
                mm.then_inc(logits_t, 1)
                pe.wait_ge(logits_t, 2)
                ps = claim(pe, s)
                for t in range(NT):
                    mm = pe.transpose(ps[:, t * w:(t + 1) * w], small[0:w, 5, t * P:(t + 1) * P], ident[0:w, 0:w])
                mm.then_inc(bank_filled[BANK[s][0]], 1)
            elif kind == "ple_gate":
                if (a, i) == (0, 0):
                    for k in range(KD):
                        drained(pe, ("turn", "h3", k))
                half_product(s, (act_hi, act_lo), 4 * i)
            elif kind == "ple_proj":
                if a == 0:
                    for k in range(PLE // P):
                        drained(pe, ("turn", "p", k))
                half_product(s, (pt_hi, pt_lo), 0)

        for s in FRONT:
            front_step(s)

        pe.wait_ge(top_done, 2)
        for t in range(NT):
            mm = product(bank[1][:, t * NE:(t + 1) * NE],
                         [(c("ones"), member[:, u, :]) for u in range(t)] + [(c("before"), member[:, t, :])])
        mm.then_inc(rank_done, 1)
        for t in range(NT):
            mm = pe.matmul(bank[2][0:P, 0:1], member_wide[:, t, :], c("ones")[:, 0:1], start=(t == 0), stop=(t == NT - 1))
        mm.then_inc(count_done, 1)
        pe.wait_ge(member_f, 1)
        pe.matmul(bank[3][:, 0:1], c("before"), over_f[:, 0:1], start=True, stop=True).then_inc(list_done, 1)
        pe.wait_ge(member_f, 2)
        pe.matmul(bank[4][0:1, 0:16], c("code"), over_f[:, 8:24], start=True, stop=True)
        pe.matmul(bank[5][0:1, 0:1], c("ones")[:, 0:1], over_f[:, 0:1], start=True, stop=True).then_inc(list_done, 1)

        def turn_rows(b, done, n_rows=FIRST):
            pe.sem_inc(pe_steps, 1)
            for k in range(KD):
                mm = pe.transpose(x_turns(n_rows)[:, k, :], xg[0:n_rows, b, k:D:KD], ident[0:n_rows, 0:n_rows])
            mm.then_inc(done, 1)

        def turn_hidden(done, n_rows=FIRST):
            pe.sem_inc(pe_steps, 1)
            for k in range(FE // P):
                mm = pe.transpose(h_turns(n_rows)[:, k, :], small[0:n_rows, 1, k * P:(k + 1) * P],
                                  ident[0:n_rows, 0:n_rows])
            mm.then_inc(done, 1)

        def expert_half(name, b, slot, started, n_rows=FIRST):
            what, h = name[:-1], int(name[-1])
            hi, lo = (v[:, slot].rearrange("p (k n) -> p k n", k=4) for v in (w_hi, w_lo))
            for k in range(4):
                if what == "down":
                    ps = bank[5 + h]
                    left = [v[:, k, 0:n_rows] for v in (ht_hi, ht_lo)]
                    first, last = k == 0, k == 3
                else:
                    ps = bank[2 if what == "gate" else 3]
                    left = [v[:, b, 4 * h + k, 0:n_rows] for v in (xt_hi, xt_lo)]
                    first, last = h == 0 and k == 0, h == 1 and k == 3
                m0, m1 = three(ps[0:n_rows, :], left, (hi[:, k, :], lo[:, k, :]), first, last)
                if k == 0:
                    m0.then_inc(started, 1)
            return m1

        def half_at(name, n, b, i=0):
            pe.wait_ge(lo_done, n + 1 + 12 * i)
            return expert_half(name, b, n % SPLIT, half_started)

        pe.wait_ge(over_list, 1)
        pe.wait_ge(gathered, 16)
        turn_rows(0, x_turned)
        pe.wait_ge(xt_done, 1)
        half_at("gate0", N_FRONT, 0)
        half_at("gate1", N_FRONT + 1, 0).then_inc(gate_done, 1)

        def expert(e0, i=0):
            e, b, n = e0 + 2 * i, e0 % 2, BASE_E + 6 * e0
            more = e0 != NE - 1
            wait_for(pe, hid_done, e)
            half_at("up0", n, b, i)
            if more:
                pe.wait_ge(gathered, 16 * e + 32)
                pe.wait_ge(xt_done, e + 1)
                turn_rows(1 - b, x_turned)
            half_at("up1", n + 1, b, i).then_inc(up_done, 1)
            if more:
                pe.wait_ge(xt_done, e + 2)
                pe.wait_ge(silu_done, e + 1)
                half_at("gate0", n + 2, 1 - b, i)
            pe.wait_ge(hid_done, e + 1)
            wait_for(pe, ht_done, e)
            turn_hidden(hid_turned)
            if more:
                half_at("gate1", n + 3, 1 - b, i).then_inc(gate_done, 1)
                n += 2
            pe.wait_ge(ht_done, e + 1)
            wait_for(pe, y_done, e)
            half_at("down0", n + 2, b, i)
            half_at("down1", n + 3, b, i).then_inc(down_done, 1)

        expert(0)
        with pe.Fori(0, NE // 2 - 1) as i:
            expert(1, i)
            expert(2, i)
        expert(NE - 1)
        n_over = pe.value_load(over[0:1, 16:17], min_val=0, max_val=NOVER)
        with pe.Fori(0, NOVER) as i:
            with pe.If(i < n_over):
                pe.wait_ge(y_done, NE)
                pe.wait_ge(ov["gathered"], 16 * i + 16)
                turn_rows(0, ov["turned"], P)
                pe.wait_ge(ov["xt"], i + 1)
                for r, name in enumerate(OVER_HALVES):
                    if name == "down0":
                        pe.wait_ge(ov["hid"], i + 1)
                        turn_hidden(ov["hid_turned"], P)
                        pe.wait_ge(ov["ht"], i + 1)
                    pe.wait_ge(ov["lo"], 6 * i + r + 1)
                    mm = expert_half(name, 0, r % SPLIT, ov["started"], P)
                    if r % 2:
                        mm.then_inc(ov[name[:-1]], 1)
                pe.wait_ge(ov["y"], i + 1)
                pe.sem_inc(ov["pe_end"], 1)
        pe.wait_ge(y_done, NE)
        for s in BACK:
            front_step(s)

    @block.scalar
    def _(act):
        def square_sums(n, src, junk, wait):
            for t in range(NT):
                if n:
                    act.wait_ge(normed, NT * (n - 1) + t + 1)
                wait(t)
                act.activation(junk[:, t], src[:, t], ACT.Square, accum_out=stat[:, t:t + 1]).then_inc(sumsq, 1)
                act.wait_ge(sumsq, NT * n + t + 1)
                act.activation(stat[:, 4 + t:5 + t], stat[:, t:t + 1], ACT.Sqrt, scale=1.0 / D, bias=eps[:, 0:1]
                               ).then_inc(root, 1)

        def step(s):
            kind, a, i = s
            if kind in WEIGHTS and HALF_OF[s] + AHEAD < N_ALL:
                split_high(act, HALF_OF[s] + AHEAD)
            if kind == "norm":
                if a == "ffn":
                    def wait(t):
                        for n in range(2):
                            drained(act, ("out", n, "tile", t))
                        if t == 0:
                            for k in range(KD):
                                filled(act, ("turn", "merged", k))
                    square_sums(1, xres, stage_tok, wait)
                elif a == "ple":
                    square_sums(2, xres, stage_tok, lambda t: act.wait_ge(pairs_added, t + 1))
                elif a == "final":
                    def wait(t):
                        act.wait_ge(ple_added, NT + t + 1)
                        if t == 0:
                            for k in range(KD):
                                filled(act, ("turn", "h3", k))
                    square_sums(3, xres, stage_tok, wait)
                return
            if kind == "turn":
                ps = filled(act, s)
                b = BANK[s][0]
                if a in SPLIT_TURNS:
                    if a in ROW_TURNS:
                        ps = ps.rearrange("p (k s) -> p k s", k=4)
                    act.copy(turn_dst(s)[0], ps).then_inc(turn_hi, 1)
                else:
                    act.copy(turn_dst(s), ps).then_inc(bank_drained[b], 1)
            elif kind == "z":
                if not last_half(s):
                    return
                if a in ROPES and ROPES.index(a) >= 2:
                    prev = ROPES[ROPES.index(a) - 2]
                    for cc in range(1 if prev == "ix" else NT):
                        filled(act, ("turn", prev, cc))
                for t in range(NT):
                    tile = tile_of(s, t)
                    ps, b = filled(act, tile), BANK[tile][0]
                    if a == "ix":
                        act.copy(stage_z[:, 1, t, 0:HD], ps[:, 0:HD])
                        act.copy(stage_z[:, 1, t, HD:2 * HD], ps[:, 0:HD])
                        act.activation(iws[:, t, :], ps[:, HD:HD + NH], ACT.Copy, scale=float(np.float32(NH ** -0.5))
                                       ).then_inc(bank_drained[b], 1)
                    elif a in ("va", "vb"):
                        act.copy(v_sb[:, t, :], ps[:]).then_inc(bank_drained[b], 1)
                    else:
                        act.copy(stage_z[:, STAGE[a], t, :], ps[:]).then_inc(bank_drained[b], 1)
            elif kind == "router":
                act.wait_ge(logits_t, 1)
                act.copy(small[0:NG + NE, 5, :], bank[1][0:NG + NE, :]).then_inc(logits_t, 1)
            elif kind in ("gate_a", "gate_b", "ple_gate"):
                if not last_half(s):
                    return
                for t in range(NT):
                    n = GATES.index((kind, a, t))
                    ps, b = filled(act, tile_of(s, t)), BANK[tile_of(s, t)][0]
                    if n >= NT:
                        kk, aa, tt = BRANCHES[n - NT]
                        drained(act, (kk, aa, "tile", tt))
                    act.activation(small[:, t, :], ps[:], ACT.Sigmoid).then_inc(bank_drained[b], 1)
            elif kind == "rel":
                n = (a - 1) * NH + i
                ps = filled(act, s)
                b = BANK[s][0]
                if n >= 2:
                    act.wait_ge(acc_done, n - 1)
                act.activation(small[:, n % 2, 0:(a + 1) * P], ps[:, 0:(a + 1) * P], ACT.Relu, scale=HD ** -0.5
                               ).then_inc(bank_drained[b], 1)
            elif kind == "scores":
                h, t = unit(i)
                n = NU * BR[a] + i
                drained(act, s)
                if i >= 2:
                    filled(act, ("turn_p", a, i - 2))
                act.activation(small[:, 2 + i % 2, 0:(t + 1) * P], small[:, i % 2, 0:(t + 1) * P], ACT.Exp,
                               bias=nm[:, i % 4:i % 4 + 1], scale=-1.0, accum_out=rs[:, i % 4:i % 4 + 1]
                               ).then_inc(exp_done, 1)
            elif kind == "turn_p":
                if i % 2:
                    return
                h, t = unit(i)
                b = BANK[s][0]
                ps = filled(act, s)
                if i >= 2:
                    filled(act, ("pv", a, i - 2))
                act.copy(small[:, 4 + i % 2, 0:(t + 1) * P], ps[:, 0:(t + 1) * P]).then_inc(bank_drained[b], 1)
        act.wait_ge(eps_set, 1)
        square_sums(0, stage_tok, junk0, lambda t: act.wait_ge(x_in[t], 16))
        act.dma_start(br[:, 0:NG], b_grp[0:1, :].partition_broadcast(P)).then_inc(small_in, 16)
        act.dma_start(br[:, NG:NG + NE], b_rt[0:1, :].partition_broadcast(P)).then_inc(small_in, 16)
        for s in FRONT:
            if s == ("turn", "oa", 0):
                act.wait_ge(normed, NT)
                act.dma_start(gain[:], g_ffn[0:1, :].partition_broadcast(P)).then_inc(gain_in, 16)
            if s == ("scores", "a", 0):
                filled(act, ("rel", NT - 1, NH - 1))
                act.dma_start(wr[:, :, 0:NG], w_grp[0].rearrange("(k p) n -> p k n", p=P)).then_inc(small_in, 16)
                act.dma_start(wr[:, :, NG:NG + NE], w_rt[0].rearrange("(k p) n -> p k n", p=P)).then_inc(small_in, 16)
            if s == ("turn", "oa", 0):
                act.wait_ge(small_in, 64)
                act.copy(wr_hi[:], wr[:]).then_inc(wr_split, 1)
            if s == ("norm", "ffn", 0):
                for t in range(NT):
                    filled(act, ("branch_b", 1, "tile", t))
                act.dma_start(pin, p[0, 0].rearrange("(t p) d -> p t d", p=P)).then_inc(p_in, 16)
            if s == ("gate_a", 0, 0):
                for x_ in "ab":
                    for cc in range(NT):
                        filled(act, ("turn", "o" + x_, cc))
                act.dma_start(xres, x[0].rearrange("(t p) d -> p t d", p=P)).then_inc(x_back, 16)
            step(s)
            if s in (("turn", "h", 3), ("turn", "h", KD - 1)):
                split_high(act, 0 if s[2] == 3 else 1)
        act.wait_ge(normed, 2 * NT)
        act.dma_start(h2_d.rearrange("(t p) d -> p t d", p=P), stage_tok).then_inc(h2_out, 16)
        act.dma_start(gain[:], g_ple[0:1, :].partition_broadcast(P)).then_inc(gain_in, 16)
        act.wait_ge(fill_ready, 1)
        act.dma_start(table_d.rearrange("(p n) w -> p (n w)", p=P), table[:, 0:NE * CH, :].rearrange("p n w -> p (n w)")
                      ).then_inc(table_filled, 16)
        act.wait_ge(ngmax_done, 1)
        for t in range(NT):
            ins = act.activation(rs_small[:, 4 * NT + NG * t:4 * NT + NG * (t + 1)], logits[:, t, 0:NG], ACT.Exp,
                                 bias=rs_small[:, t:t + 1], accum_out=rs_small[:, NT + t:NT + t + 1])
        ins.then_inc(gexp_done, 1)
        act.wait_ge(e2_done, 1)
        act.activation(rs_small[:, 3 * NT:4 * NT], rs_small[:, 2 * NT:3 * NT], ACT.Exp).then_inc(gexp_done, 1)
        act.wait_ge(table_written, 16 * 2 * NT)
        act.dma_start(table[:, 0:NE * CH, :].rearrange("p n w -> p (n w)"), table_d.rearrange("(p n) w -> p (n w)", p=P)
                      ).then_inc(table_in, 16)

        def rows_high(b, done, n_rows=FIRST):
            act.copy(xt_hi[:, b, :, 0:n_rows], x_turns(n_rows)).then_inc(done, 1)

        def silu(done, n_rows=FIRST):
            act.activation(small[0:n_rows, 0, :], bank[2][0:n_rows, :], ACT.Silu).then_inc(done, 1)

        def hidden_high(done, n_rows=FIRST):
            act.copy(ht_hi[:, :, 0:n_rows], h_turns(n_rows)).then_inc(done, 1)

        def weigh(b, done, n_rows=FIRST):
            act.activation(y_sb[0:n_rows, b], psum[0:n_rows, 5:7, :].rearrange("p b s -> p (b s)"), ACT.Copy,
                           scale=pair_of[0:n_rows, b, 2:3].bitcast(F32)).then_inc(done, 1)

        act.wait_ge(x_turned, 1)
        rows_high(0, xt_hi_done)
        split_high(act, N_FRONT + 2)
        split_high(act, N_FRONT + 3)
        act.wait_ge(gate_done, 1)
        silu(silu_done)

        def expert(e0, i=0):
            e, b, n = e0 + 2 * i, e0 % 2, BASE_E + 6 * e0
            more = e0 != NE - 1
            split_high(act, n + 2, i)
            if more:
                act.wait_ge(x_turned, e + 2)
                wait_for(act, up_done, e)
                rows_high(1 - b, xt_hi_done)
            split_high(act, n + 3, i)
            if more:
                split_high(act, n + 4, i)
            act.wait_ge(hid_turned, e + 1)
            wait_for(act, down_done, e)
            hidden_high(ht_hi_done)
            if more:
                split_high(act, n + 5, i)
                if e0 + 2 < NE:
                    split_high(act, n + 6, i)
                act.wait_ge(gate_done, e + 2)
                act.wait_ge(hid_done, e + 1)
                silu(silu_done)
                split_high(act, n + 7, i)
            act.wait_ge(down_done, e + 1)
            wait_for(act, scattered, 16 * e)
            act.wait_ge(pairs_set, e + 1)
            weigh(b, y_done)

        expert(0)
        with act.Fori(0, NE // 2 - 1) as i:
            expert(1, i)
            expert(2, i)
        expert(NE - 1)
        act.wait_ge(over_list, 1)
        n_over = act.value_load(over[0:1, 16:17], min_val=0, max_val=NOVER)
        with act.Fori(0, NOVER) as i:
            with act.If(i < n_over):
                act.wait_ge(ov["turned"], i + 1)
                rows_high(0, ov["xt_hi"], P)
                for r, name in enumerate(OVER_HALVES):
                    if name == "down0":
                        act.wait_ge(ov["gate"], i + 1)
                        silu(ov["silu"], P)
                    act.wait_ge(ov["loaded"], 96 * i + 16 * r + 16)
                    if r >= SPLIT:
                        act.wait_ge(ov["started"], 6 * i + r - 1)
                    else:
                        act.wait_ge(half_started, N_FRONT + N_EXP)
                        act.wait_ge(down_done, NE)
                    act.copy(w_hi[:, r % SPLIT, :], raw[:, r % RAW, :]).then_inc(ov["hi"], 1)
                act.wait_ge(ov["hid_turned"], i + 1)
                hidden_high(ov["ht_hi"], P)
                act.wait_ge(ov["down"], i + 1)
                act.wait_ge(ov["pairs"], i + 1)
                weigh(0, ov["y"], P)
                act.wait_ge(ov["scattered"], 16 * i + 16)
                act.sem_inc(ov["act_end"], 1)
        for n in range(AHEAD):
            split_high(act, N_FRONT + N_EXP + n)
        for s in BACK:
            if s == ("turn", "h3", 0):
                act.wait_ge(normed, 3 * NT)
                act.dma_start(gain[:], g_final.rearrange("(a d) -> a d", a=1).partition_broadcast(P)).then_inc(gain_in, 16)
            step(s)

    @block.vector
    def _(dve):
        chain = [0]

        def link(ins):
            chain[0] += 1
            ins.then_inc(dve_chain, 1)
            dve.wait_ge(dve_chain, chain[0])

        def norm(n, src, t):
            dve.wait_ge(root, NT * n + t + 1)
            ms, sq, v, y, a, inv = (stat[:, 4 * k + t:4 * k + t + 1] for k in range(6))
            dve.tensor_scalar(v, ms, 1.0 / D, EPS, ALU.mult, ALU.add)
            link(dve.reciprocal(y, sq))
            link(dve.tensor_tensor(a, y, y, ALU.mult))
            link(dve.tensor_tensor(a, a, v, ALU.mult))
            link(dve.tensor_scalar(a, a, -0.5, 1.5, ALU.mult, ALU.add))
            link(dve.tensor_tensor(inv, a, y, ALU.mult))
            if t == 0:
                dve.wait_ge(gain_in, 16 * (n + 1))
            dve.scalar_tensor_tensor(out=stage_tok[:, t], in0=src[:, t], scalar=inv, in1=gain[:],
                                     op0=ALU.mult, op1=ALU.mult).then_inc(normed, 1)

        def step(s):
            kind, a, i = s
            if kind in WEIGHTS and HALF_OF[s] + AHEAD < N_ALL:
                split_low(dve, HALF_OF[s] + AHEAD)
            if kind == "norm":
                if a == "ple":
                    for t in range(NT):
                        dve.wait_ge(pairs_in[t % 2], 16 * (t // 2 + 1))
                        link(dve.tensor_tensor(y_in[:, t % 2, 0:D], y_in[:, t % 2, 0:D], y_in[:, t % 2, D:2 * D], ALU.add))
                        dve.tensor_tensor(xres[:, t], xres[:, t], y_in[:, t % 2, 0:D], ALU.add).then_inc(pairs_added, 1)
                        if t:
                            norm(2, xres, t - 1)
                norm({"ffn": 1, "ple": 2, "final": 3}[a], xres, NT - 1)
                return
            if kind == "topk":
                topk_round(a)
                return
            if kind == "select":
                select()
                return
            b = BANK[s][0] if s in BANK else None
            if kind == "turn":
                if a not in SPLIT_TURNS:
                    return
                if a == "h" and i % 2 == 0 and i // 2 + 1 < NT:
                    norm(0, stage_tok, i // 2 + 1)
                n_turned[0] += 1
                dve.wait_ge(turn_hi, n_turned[0])
                hi, lo = turn_dst(s)
                ps = bank[b].rearrange("p (k s) -> p k s", k=4) if a in ROW_TURNS else bank[b]
                dve.tensor_tensor(lo, ps, hi.bitcast(F32), ALU.subtract).then_inc(bank_drained[b], 1)
            elif kind == "rel":
                t, h = a, i
                n = (t - 1) * NH + h
                w = (t + 1) * P
                drained(dve, s)
                if n == 0:
                    dve.wait_ge(const_in, 16)
                if h == 0:
                    base = c("causal")[:, (NT - t) * P:(NT + 1) * P]
                else:
                    base = score(t)
                    dve.wait_ge(acc_done, n)
                dve.scalar_tensor_tensor(out=score(t), in0=small[:, n % 2, 0:w], scalar=iws[:, t, h:h + 1],
                                         in1=base, op0=ALU.mult, op1=ALU.add).then_inc(acc_done, 1)
            elif kind == "scores":
                h, t = unit(i)
                w = (t + 1) * P
                n = NU * BR[a] + i
                ps = filled(dve, s)
                if i >= 2:
                    dve.wait_ge(exp_done, n - 1)
                bias = score(t) if a == "b" and t else c("causal")[:, (NT - t) * P:(NT + 1) * P]
                dve.tensor_tensor_reduce(out=small[:, i % 2, 0:w], in0=ps[:, 0:w], in1=bias, scale=-HD ** -0.5,
                                         scalar=3.0e38, op0=ALU.add, op1=ALU.min, accum_out=nm[:, i % 4:i % 4 + 1]
                                         ).then_inc(bank_drained[b], 1)
            elif kind == "turn_p":
                if not i % 2:
                    return
                h, t = unit(i)
                ps = filled(dve, s)
                if i >= 2:
                    filled(dve, ("pv", a, i - 2))
                dve.tensor_copy(small[:, 4 + i % 2, 0:(t + 1) * P], ps[:, 0:(t + 1) * P]).then_inc(bank_drained[b], 1)
            elif kind == "pv":
                h, t = unit(i)
                link(dve.reciprocal(ri[:, i % 4:i % 4 + 1], rs[:, i % 4:i % 4 + 1]))
                ps = filled(dve, s)
                dve.tensor_scalar(o_sb[a][:, t, h * HD:(h + 1) * HD], ps[:, 0:HD], ri[:, i % 4:i % 4 + 1], None, ALU.mult
                                  ).then_inc(bank_drained[b], 1)
            elif kind in ("branch_a", "branch_b"):
                gate = "gate_" + kind[-1]
                for t in range(NT):
                    tile = tile_of(s, t)
                    drained(dve, (gate, a, "tile", t))
                    ps, b = filled(dve, tile), BANK[tile][0]
                    dst = stage_tok[:, t, a * 512:(a + 1) * 512]
                    if kind == "branch_a":
                        dve.tensor_tensor(dst, small[:, t, :], ps[:], ALU.mult).then_inc(bank_drained[b], 1)
                    else:
                        tmp = small[:, 4 + t % 2, :]
                        dve.tensor_tensor(tmp, small[:, t, :], ps[:], ALU.mult).then_inc(bank_drained[b], 1)
                        drained(dve, tile)
                        drained(dve, ("branch_a", a, "tile", t))
                        dve.tensor_tensor(dst, dst, tmp, ALU.add).then_inc(merged_done, 1)
            elif kind == "out":
                if not last_half(s):
                    return
                for t in range(NT):
                    tile = tile_of(s, t)
                    ps, b = filled(dve, tile), BANK[tile][0]
                    dve.wait_ge(x_back, 16)
                    dst = xres[:, t, a * 512:(a + 1) * 512]
                    dve.tensor_tensor(dst, dst, ps[:], ALU.add).then_inc(bank_drained[b], 1)
                    if a and t:
                        norm(1, xres, t - 1)
            elif kind == "ple_proj":
                for t in range(NT):
                    tile = tile_of(s, t)
                    drained(dve, ("ple_gate", a, "tile", t))
                    ps, b = filled(dve, tile), BANK[tile][0]
                    tmp = small[:, 4 + t % 2, :]
                    dve.tensor_tensor(tmp, small[:, t, :], ps[:], ALU.mult).then_inc(bank_drained[b], 1)
                    drained(dve, tile)
                    dst = xres[:, t, a * 512:(a + 1) * 512]
                    dve.tensor_tensor(dst, dst, tmp, ALU.add).then_inc(ple_added, 1)
                    if a and t:
                        norm(3, xres, t - 1)

        n_turned = [0]

        def topk_round(r):
            if r == 0:
                dve.wait_ge(acc_done, (NT - 1) * NH)
            for t in range(1, NT):
                if r:
                    dve.wait_ge(mark_done, (NT - 1) * (r - 1) + t)
                dve.max(m8[:, t, :], score(t)).then_inc(max_done, 1)
            for t in range(1, NT):
                dve.wait_ge(max_done, (NT - 1) * r + t)
                dve.match_replace(score(t), m8[:, t, :], score(t), MARK).then_inc(mark_done, 1)

        def select():
            for t in range(1, NT):
                dve.wait_ge(mark_done, (NT - 1) * (DSA_TOPK // 8 - 1) + t)
                dve.tensor_scalar(score(t), score(t), 0.9 * MARK, NEG, ALU.is_gt, ALU.mult).then_inc(selected, 1)
            dve.wait_ge(selected, NT - 1)

        def route():
            def small_col(n):
                return rs_small[:, n * NT:(n + 1) * NT]

            def spread(v, k):
                return v.unsqueeze(2).to_broadcast([P, NT, k])

            def first_largest(dst, src, top, desc, k, tmp):
                link(dve.tensor_reduce(top, src, AX.X, ALU.max))
                link(dve.tensor_tensor(tmp, src, spread(top, k), ALU.is_equal))
                link(dve.tensor_tensor(tmp, tmp, desc, ALU.mult))
                link(dve.tensor_reduce(small_col(9), tmp, AX.X, ALU.max))
                link(dve.tensor_tensor(dst, tmp, spread(small_col(9), k), ALU.is_equal))

            def block_(n, k=NE):
                return rt[:, n * NT * NE:n * NT * NE + NT * k].rearrange("p (t k) -> p t k", t=NT)

            masked, m1, m2, tmp, group, pen = block_(0), block_(1), block_(2), block_(3), block_(5, NG), block_(6, NG)
            gmax, v1, v2 = small_col(8), small_col(10), small_col(11)
            r_ = BANK[("router", 0, 0)][0]
            ps = filled(dve, ("router", 0, 0))
            dve.wait_ge(small_in, 64)
            dve.tensor_tensor(logits, ps[:, 0:NT * (NG + NE)].rearrange("p (t k) -> p t k", t=NT),
                              br[:].unsqueeze(1).to_broadcast([P, NT, NG + NE]), ALU.add).then_inc(bank_drained[r_], 1)
            drained(dve, ("router", 0, 0))
            first_largest(group, logits[:, :, 0:NG], gmax, c4("desc_group", NG), NG, block_(7, NG))
            dve.tensor_scalar(small_col(0), gmax, -1.0, None, ALU.mult).then_inc(ngmax_done, 1)
            link(dve.tensor_scalar(pen, group, -1.0, -NEG, ALU.add, ALU.mult))
            for g in range(NG):
                ins = dve.tensor_tensor(masked[:, :, g * EPG:(g + 1) * EPG],
                                        logits[:, :, NG + g * EPG:NG + (g + 1) * EPG],
                                        pen[:, :, g:g + 1].to_broadcast([P, NT, EPG]), ALU.add)
            link(ins)
            first_largest(m1, masked, v1, c4("desc_expert", NE), NE, tmp)
            link(dve.scalar_tensor_tensor(out=masked, in0=m1, scalar=NEG, in1=masked, op0=ALU.mult, op1=ALU.add))
            first_largest(m2, masked, v2, c4("desc_expert", NE), NE, tmp)
            dve.tensor_tensor(small_col(2), v2, v1, ALU.subtract).then_inc(e2_done, 1)
            dve.tensor_tensor(member, m1, m2, ALU.add).then_inc(top_done, 1)
            dve.wait_ge(top_done, 1)
            dve.tensor_copy(member_wide.rearrange("p t (e c) -> p (t e) c", c=CH),
                            member.rearrange("p t e -> p (t e)").unsqueeze(2).to_broadcast([P, NT * NE, CH])
                            ).then_inc(top_done, 1)
            dve.wait_ge(fill_ready, 2)
            dve.wait_ge(gexp_done, 2)
            link(dve.tensor_scalar(small_col(12), small_col(3), 1.0, None, ALU.add))
            link(dve.reciprocal(small_col(13), small_col(12)))
            link(dve.reciprocal(small_col(14), small_col(1)))
            wv = [rows[:, k * NT:(k + 1) * NT, 2].bitcast(F32) for k in range(2)]
            link(dve.tensor_tensor(wv[0], small_col(13), small_col(14), ALU.mult))
            link(dve.tensor_tensor(wv[1], wv[0], small_col(3), ALU.mult))
            dve.wait_ge(rank_done, 1)
            nec = NE * CH
            for k, m in enumerate((m1, m2)):
                rank, chunk, at = small_col(16 + 4 * k), small_col(17 + 4 * k), small_col(18 + 4 * k)
                link(dve.tensor_tensor(tmp, m, bank[1][:, 0:NT * NE].rearrange("p (t e) -> p t e", t=NT), ALU.mult))
                link(dve.tensor_reduce(rank, tmp, AX.X, ALU.add))
                link(dve.tensor_tensor(tmp, m, c4("four_e", NE), ALU.mult))
                link(dve.tensor_reduce(at, tmp, AX.X, ALU.add))
                link(dve.tensor_scalar(chunk, rank, float(P), None, ALU.is_ge))
                for cc in range(2, CH):
                    link(dve.scalar_tensor_tensor(out=chunk, in0=rank, scalar=float(cc * P), in1=chunk,
                                                  op0=ALU.is_ge, op1=ALU.add))
                link(dve.scalar_tensor_tensor(out=at, in0=rank, scalar=float(nec), in1=at, op0=ALU.mult, op1=ALU.add))
                link(dve.scalar_tensor_tensor(out=at, in0=chunk, scalar=float(1 - P * nec), in1=at,
                                              op0=ALU.mult, op1=ALU.add))
                link(dve.tensor_copy(dest[:, k * NT:(k + 1) * NT], at))
                link(dve.tensor_copy(rows[:, k * NT:(k + 1) * NT, 0], c("token")))
                link(dve.tensor_scalar(rows[:, k * NT:(k + 1) * NT, 1], c("token"), 2.0, float(k), ALU.mult, ALU.add))
            dve.sem_inc(rows_ready, 1)
            dve.wait_ge(count_done, 1)
            dve.tensor_tensor(over_f[:, 0:1], bank[2][:, 0:1], c("limit"), ALU.is_gt).then_inc(member_f, 1)
            dve.wait_ge(list_done, 1)
            link(dve.tensor_copy(over_f[:, 1:2], bank[3][:, 0:1]))
            dve.tensor_scalar(over_f[:, 8:24], c("places"), over_f[:, 1:2], over_f[:, 0:1], ALU.is_equal, ALU.mult
                              ).then_inc(member_f, 1)
            dve.wait_ge(list_done, 2)
            link(dve.tensor_copy(over[0:1, 0:16], bank[4][0:1, 0:16]))
            dve.tensor_copy(over[0:1, 16:17], bank[5][0:1, 0:1]).then_inc(over_list, 1)

        dve.memset(eps[:], EPS).then_inc(eps_set, 1)
        dve.memset(table[:], OOB).then_inc(fill_ready, 1)
        dve.memset(rows[:], 0).then_inc(fill_ready, 1)
        norm(0, stage_tok, 0)
        for s in FRONT:
            if s == ("turn", "oa", 0):
                dve.wait_ge(wr_split, 1)
                dve.tensor_tensor(wr_lo[:], wr[:], wr_hi[:].bitcast(F32), ALU.subtract).then_inc(wr_split, 1)
            step(s)
            if s in (("turn", "h", 3), ("turn", "h", KD - 1)):
                split_low(dve, 0 if s[2] == 3 else 1)
        route()
        def rows_low(b, done, n_rows=FIRST):
            dve.tensor_tensor(xt_lo[:, b, :, 0:n_rows], x_turns(n_rows), xt_hi[:, b, :, 0:n_rows].bitcast(F32),
                              ALU.subtract).then_inc(done, 1)

        def hidden(done, n_rows=FIRST):
            dve.tensor_tensor(small[0:n_rows, 1, :], small[0:n_rows, 0, :], bank[3][0:n_rows, :], ALU.mult
                              ).then_inc(done, 1)

        def hidden_low(done, n_rows=FIRST):
            dve.tensor_tensor(ht_lo[:, :, 0:n_rows], h_turns(n_rows), ht_hi[:, :, 0:n_rows].bitcast(F32), ALU.subtract
                              ).then_inc(done, 1)

        dve.wait_ge(xt_hi_done, 1)
        rows_low(0, xt_done)
        split_low(dve, N_FRONT + 2)
        split_low(dve, N_FRONT + 3)

        def expert(e0, i=0):
            e, b, n = e0 + 2 * i, e0 % 2, BASE_E + 6 * e0
            more = e0 != NE - 1
            split_low(dve, n + 2, i)
            if more:
                dve.wait_ge(xt_hi_done, e + 2)
                rows_low(1 - b, xt_done)
            split_low(dve, n + 3, i)
            dve.wait_ge(silu_done, e + 1)
            dve.wait_ge(up_done, e + 1)
            wait_for(dve, hid_turned, e)
            hidden(hid_done)
            if more:
                split_low(dve, n + 4, i)
            dve.wait_ge(ht_hi_done, e + 1)
            hidden_low(ht_done)
            if more:
                split_low(dve, n + 5, i)
                split_low(dve, n + 6, i)
                split_low(dve, n + 7, i)

        expert(0)
        with dve.Fori(0, NE // 2 - 1) as i:
            expert(1, i)
            expert(2, i)
        expert(NE - 1)
        dve.wait_ge(over_list, 1)
        n_over = dve.value_load(over[0:1, 16:17], min_val=0, max_val=NOVER)
        with dve.Fori(0, NOVER) as i:
            with dve.If(i < n_over):
                dve.wait_ge(ov["xt_hi"], i + 1)
                rows_low(0, ov["xt"], P)
                for r, name in enumerate(OVER_HALVES):
                    dve.wait_ge(ov["hi"], 6 * i + r + 1)
                    dve.tensor_tensor(w_lo[:, r % SPLIT, :], raw[:, r % RAW, :], w_hi[:, r % SPLIT, :].bitcast(F32),
                                      ALU.subtract).then_inc(ov["lo"], 1)
                dve.wait_ge(ov["silu"], i + 1)
                dve.wait_ge(ov["up"], i + 1)
                hidden(ov["hid"], P)
                dve.wait_ge(ov["ht_hi"], i + 1)
                hidden_low(ov["ht"], P)
        for n in range(AHEAD):
            split_low(dve, N_FRONT + N_EXP + n)
        for s in BACK:
            step(s)

    @block.gpsimd
    def _(pool):
        chain = [0]

        def link(ins):
            chain[0] += 1
            ins.then_inc(pool_chain, 1)
            pool.wait_ge(pool_chain, chain[0])

        def rope(name):
            heads = 2 if name == "ix" else NH
            z = stage_z[:, STAGE[name]].rearrange("p t (h d) -> p t h d", d=HD)[:, :, 0:heads]
            x1, x2 = z[:, :, :, 0:HALF], z[:, :, :, HALF:ROT]
            cos, sin = (c(n).rearrange("p (t h d) -> p t h d", t=NT, h=NH)[:, :, 0:heads] for n in ("cos", "sin"))
            part = [rope_t[:, :, 0:heads, k * HALF:(k + 1) * HALF] for k in range(4)]
            for t in range(NT):
                drained(pool, ("z", name, "tile", t))
            for k, (xx, f) in enumerate(((x1, cos), (x2, sin), (x2, cos), (x1, sin))):
                link(pool.tensor_tensor(part[k], xx, f, ALU.mult))
            link(pool.tensor_tensor(x1, part[0], part[1], ALU.subtract))
            link(pool.tensor_tensor(x2, part[2], part[3], ALU.add))
            pool.sem_inc(roped, 1)

        pool.wait_ge(const_in, 16)
        for s in FRONT:
            if s[0] == "rope":
                rope(s[1])
        pool.wait_ge(h2_out, 16)
        for k in range(KD):
            filled(pool, ("turn", "h2", k))
        link(pool.memset(xg, 0.0))
        pool.wait_ge(rows_ready, 1)
        pool.wait_ge(table_filled, 16)
        for n in range(2 * NT):
            pool.indirect_dma_start(out=table_d, out_offset=bass.IndirectOffsetOnAxis(ap=dest[:, n:n + 1], axis=0),
                                    in_=rows[:, n, :], in_offset=None, bounds_check=P * NE * CH - 1,
                                    oob_is_err=False).then_inc(table_written, 16)

        def gather(b, done, n_rows=FIRST):
            pool.sem_inc(pool_steps, 1)
            pool.indirect_dma_start(out=xg[0:n_rows, b], out_offset=None, in_=h2_d,
                                    in_offset=bass.IndirectOffsetOnAxis(ap=row_of[0:n_rows, b, 0:1], axis=0),
                                    bounds_check=S - 1, oob_is_err=False).then_inc(done, 16)

        def scatter(b, done, n_rows=FIRST):
            pool.sem_inc(pool_steps, 1)
            pool.indirect_dma_start(out=pairs_d,
                                    out_offset=bass.IndirectOffsetOnAxis(ap=pair_of[0:n_rows, b, 1:2], axis=0),
                                    in_=y_sb[0:n_rows, b], in_offset=None,
                                    bounds_check=2 * S - 1, oob_is_err=False).then_inc(done, 16)

        pool.wait_ge(table_in, 16)
        for e in range(2):
            pool.tensor_copy(row_of[:, e, :], table[:, CH * e, :]).then_inc(rows_set, 1)
        for e in range(2):
            pool.wait_ge(rows_set, e + 1)
            if e:
                pool.wait_ge(gathered, 16)
            gather(e, gathered)

        def expert(e0, i=0):
            e, b = e0 + 2 * i, e0 % 2
            if e0 != NE - 1:
                pool.wait_ge(gathered, 16 * e + 32)
                pool.tensor_copy(row_of[:, b, :].unsqueeze(1), table[:, bass.ds(CH * (e + 2), 1), :]
                                 ).then_inc(rows_set, 1)
                pool.wait_ge(rows_set, e + 3)
                pool.wait_ge(x_turned, e + 1)
                gather(b, gathered)
            wait_for(pool, scattered, 16 * e)
            pool.tensor_copy(pair_of[:, b, :].unsqueeze(1), table[:, bass.ds(CH * e, 1), :]).then_inc(pairs_set, 1)
            pool.wait_ge(pairs_set, e + 1)
            pool.wait_ge(y_done, e + 1)
            scatter(b, scattered)

        expert(0)
        with pool.Fori(0, NE // 2 - 1) as i:
            expert(1, i)
            expert(2, i)
        expert(NE - 1)
        pool.wait_ge(over_list, 1)
        n_over = pool.value_load(over[0:1, 16:17], min_val=0, max_val=NOVER)
        with pool.Fori(0, NOVER) as i:
            with pool.If(i < n_over):
                pool.wait_ge(scattered, 16 * NE)
                pool.wait_ge(gathered, 16 * NE + 16)
                code = pool.value_load(over[0:1, bass.ds(i, 1)], min_val=0, max_val=NE * CH - 1)
                pool.tensor_copy(row_of[:, 0, :].unsqueeze(1), table[:, bass.ds(code, 1), :]).then_inc(ov["rows"], 1)
                pool.tensor_copy(pair_of[:, 0, :].unsqueeze(1), table[:, bass.ds(code, 1), :]).then_inc(ov["pairs"], 1)
                pool.wait_ge(ov["rows"], i + 1)
                pool.wait_ge(ov["pairs"], i + 1)
                gather(0, ov["gathered"], P)
                pool.wait_ge(ov["y"], i + 1)
                scatter(0, ov["scattered"], P)
                pool.wait_ge(ov["scattered"], 16 * i + 16)
                pool.sem_inc(ov["pool_end"], 1)

    block.__exit__(None, None, None)


_INS = ["x", "p", "g_attn", "w_in", "w_br_a", "w_br_b", "w_out", "g_ffn", "w_grp", "b_grp", "w_rt", "b_rt",
        "w_gate", "w_up", "w_down", "g_ple", "w_ple_gate", "w_ple_proj", "g_final"]


def kernel(**inputs):
    import concourse.bacc as bacc
    from concourse.bass_utils import run_bass_kernel_spmd

    nc = bacc.Bacc("TRN2", target_bir_lowering=False, num_devices=1)
    arrays, args = {}, []
    for name in _INS:
        a = np.ascontiguousarray(inputs[name])
        arrays[f"in_{name}"] = a
        args.append(nc.dram_tensor(f"in_{name}", a.shape, mybir.dt.from_np(a.dtype), kind="ExternalInput").ap())
    arrays["constants"] = constants()
    args.append(nc.dram_tensor("constants", (P, NCONST), F32, kind="ExternalInput").ap())
    out = nc.dram_tensor("out", (1, S, D), F32, kind="ExternalOutput").ap()
    layer_kernel(nc, *args, out)
    r = run_bass_kernel_spmd(nc, [arrays], core_ids=[0])
    return r.results[0]["out"]
```

```python
import numpy as np

import concourse.bass as bass
from concourse import mybir

ALU = mybir.AluOpType
ACT = mybir.ActivationFunctionType
AX = mybir.AxisListType
F32 = mybir.dt.float32
I32 = mybir.dt.int32
F32R = mybir.dt.float32r

P = 128
S = 512
D = 1024
NT = S // P
KD = D // P
HD = 64
NH = 8
AW = NH * HD
ROT = HD // 4
HALF = ROT // 2
THETA = 500000.0
DSA_TOPK = min(256, S // 4)
NG, EPG = 4, 8
NE = NG * EPG
FE = 512
PLE = 256
EPS = 1e-6
NEG = -1.0e30
MARK = -3.0e38
CH = NT
HALF_W = 2048
RAW, RAW_E = 4, 6
SPLIT, SPLIT_E = 3, 4
AHEAD = 2
FIRST = 64
NOVER = 4 * S // (P + 1)
OOB = 1 << 20

IN_OFF = dict(qa=0, ka=AW, va=2 * AW, qb=3 * AW, kb=4 * AW, vb=5 * AW, iq=6 * AW,
              ix=7 * AW, ga=7 * AW + HD + NH, gb=7 * AW + HD + NH + D)

CONST_COLS = {}
_at = 0
for _name, _n in (("ident", P), ("before", P), ("causal", 2 * P * (NT + 1) // 2), ("cos", NT * NH * HALF),
                  ("sin", NT * NH * HALF), ("ones", P), ("desc_group", NT * NG), ("desc_expert", NT * NE),
                  ("four_e", NT * NE), ("token", NT), ("code", 1), ("limit", 1), ("places", 16)):
    CONST_COLS[_name] = (_at, _at + _n)
    _at += _n
NCONST = _at


def constants():
    c = np.zeros((P, NCONST), np.float32)

    def put(name, value):
        a, b = CONST_COLS[name]
        c[:, a:b] = np.asarray(value, np.float32).reshape(P, b - a)

    row = np.arange(P)
    put("ident", np.eye(P))
    put("before", row[:, None] < row[None, :])
    causal = np.zeros((P, P * (NT + 1)), np.float32)
    causal[:, P * NT:] = np.where(row[None, :] <= row[:, None], 0.0, NEG)
    put("causal", causal)
    inv = (1.0 / (np.float32(THETA) ** (np.arange(0, ROT, 2, dtype=np.float32) / np.float32(ROT)))).astype(np.float32)
    ang = np.arange(S, dtype=np.float32)[:, None] * inv[None, :]
    for name, f in (("cos", np.cos), ("sin", np.sin)):
        t = f(ang).reshape(NT, P, 1, HALF).transpose(1, 0, 2, 3)
        put(name, np.broadcast_to(t, (P, NT, NH, HALF)))
    put("ones", np.ones((P, P)))
    put("desc_group", np.broadcast_to(NG - np.arange(NG), (P, NT, NG)))
    put("desc_expert", np.broadcast_to(NE - np.arange(NE), (P, NT, NE)))
    put("four_e", np.broadcast_to(CH * np.arange(NE), (P, NT, NE)))
    put("token", np.arange(NT)[None, :] * P + row[:, None])
    put("code", row)
    put("limit", np.where(row % CH == 0, FIRST, P * (row % CH)))
    put("places", np.broadcast_to(np.arange(16), (P, 16)))
    return c


def attention_steps(branch):
    units = [(h, t) for h in range(NH) for t in range(NT)]
    out = []
    for u in range(len(units) + 3):
        if 2 <= u < len(units):
            out.append(("scores", branch, u))
        if 2 <= u < len(units) + 2:
            out.append(("turn_p", branch, u - 2))
        if u >= 3:
            out.append(("pv", branch, u - 3))
    return out


def front_steps():
    z = lambda name: [("z", name, i) for i in range(1 if name == "ix" else 2)]
    turn = lambda name, n: [("turn", name, c) for c in range(n)]
    rel = lambda t: [("rel", t, h) for h in range(NH)]
    st = turn("h", KD)
    st += z("iq") + [("rope", "iq", 0)] + z("ix")
    st += z("qa")[:1] + [("ix_back", 0, 0), ("rope", "ix", 0)] + turn("iq", NT) + turn("ix", 1) + rel(1)
    st += z("qa")[1:] + [("rope", "qa", 0)] + rel(2)
    st += z("ka")[:1] + rel(3) + z("ka")[1:] + [("rope", "ka", 0)] + turn("qa", NT)
    rounds = [("topk", r, 0) for r in range(DSA_TOPK // 8)]
    for n, w in enumerate(z("va") + z("qb") + z("kb")):
        if w == ("z", "kb", 1):
            st += [("scores", "a", 0), ("scores", "a", 1)]
        st += [w] + rounds[3 * n:3 * n + 3]
        if n == 0:
            st += turn("ka", NT)
        if w == ("z", "qb", 1):
            st += [("rope", "qb", 0)]
    st += [("select", 0, 0), ("rope", "kb", 0)]
    st += attention_steps("a")
    st += turn("qb", NT) + turn("kb", NT) + z("vb")[:1] + [("scores", "b", 0), ("scores", "b", 1)] + z("vb")[1:]
    st += attention_steps("b")
    st += turn("oa", NT) + turn("ob", NT)
    for n in range(2):
        for x in "ab":
            st += [("gate_" + x, n, 0), ("gate_" + x, n, 1)]
            if (n, x) == (1, "b"):
                st += turn("merged", KD)[:NT]
            st += [("branch_" + x, n, 0)]
    st += turn("merged", KD)[NT:] + [("out", 0, 0), ("out", 0, 1)] + turn("p", PLE // P)
    st += [("out", 1, 0), ("out", 1, 1), ("norm", "ffn", 0)] + turn("h2", KD) + [("router", 0, 0)]
    return st


def back_steps():
    st = [("ple_proj", n, 0) for n in range(2)]
    st += [("norm", "ple", 0)] + [("turn", "h3", c) for c in range(KD)]
    st += [("ple_gate", n, i) for n in range(2) for i in range(2)]
    st += [("norm", "final", 0)]
    return st


FRONT, BACK = front_steps(), back_steps()
WEIGHTS = ("z", "gate_a", "gate_b", "branch_a", "branch_b", "out", "ple_gate", "ple_proj")
N_EXP = 6 * NE
HALVES = [s for s in FRONT if s[0] in WEIGHTS]
N_FRONT = len(HALVES)
TAIL = [s for s in BACK if s[0] in WEIGHTS]
HALF_OF = {s: n for n, s in enumerate(HALVES)}
HALF_OF.update({s: N_FRONT + N_EXP + n for n, s in enumerate(TAIL)})
N_ALL = N_FRONT + N_EXP + len(TAIL)
LAST_OF = {"z": 1, "gate_a": 1, "gate_b": 1, "branch_a": 0, "branch_b": 0, "out": 1, "ple_gate": 1, "ple_proj": 0}


def last_half(s):
    return s[2] == (0 if s[1] == "ix" else LAST_OF[s[0]])


def place_banks():
    where, uses = {}, [0] * 8
    turns = rels = outs = 0
    for s in FRONT + BACK:
        kind = s[0]
        if kind in ("rope", "topk", "select", "norm"):
            continue
        if kind in WEIGHTS:
            if s[2] == 0 and s[1] != "ix":
                first = {"z": 4 * (s[1] in ("kb", "vb")), "gate_a": 0, "gate_b": 0, "branch_a": 4, "branch_b": 4, "out": 4 * (s[1] == 1),
                         "ple_gate": 4 * (s[1] == 1), "ple_proj": 4 * (s[1] == 1)}[kind]
                for t in range(NT):
                    uses[first + t] += 1
                    where[(kind, s[1], "tile", t)] = (first + t, uses[first + t])
            continue
        if kind == "turn" and s[1] in ("h", "h3"):
            b = s[2]
        elif kind == "turn" and s[1] in ("merged", "h2"):
            b = s[2] % 4
        elif kind == "turn":
            b = 4 + turns % 2
            turns += 1
        elif kind == "rel":
            b = 6 + rels % 2
            rels += 1
        elif kind == "scores":
            b = s[2] % 3
        elif kind == "turn_p":
            b = 4 + s[2] % 2
        elif kind == "pv":
            b = 6 + s[2] % 2
        elif kind == "ix_back":
            b = 6
        else:
            b = 0
        uses[b] += 1
        where[s] = (b, uses[b])
    return where


BANK = place_banks()

GATES = [(s[0], s[1], t) for s in FRONT + BACK if s[0] in ("gate_a", "gate_b", "ple_gate") and s[2] for t in range(NT)]
BRANCHES = [(s[0], s[1], t) for s in FRONT + BACK if s[0] in ("branch_a", "branch_b", "ple_proj") for t in range(NT)]
ROPES = ["iq", "ix", "qa", "ka", "qb", "kb"]
STAGE = {name: n % 2 for n, name in enumerate(ROPES)}


SPLIT_TURNS = ("h", "oa", "ob", "merged", "h2", "h3", "p")


ROW_TURNS = ("h", "merged", "h2", "h3")


def tile_and_half(a, i):
    return (i % NT, i // NT) if a == "merged" else (i // 2, i % 2)


def raw_turn(n):
    if n < N_FRONT:
        return n % RAW, 0, n // RAW + 1
    m = n - N_FRONT
    if m < N_EXP:
        k = m % RAW_E
        return ((N_FRONT + k) % RAW if k < RAW else k), 1, m // RAW_E + 1
    return raw_turn(N_FRONT + (m - N_EXP) % RAW)[0], 2, (m - N_EXP) // RAW + 1


def raw_before(n):
    if n < N_FRONT + RAW:
        return n - RAW
    m = n - N_FRONT
    if m < N_EXP:
        return n - RAW_E
    return N_FRONT + N_EXP - RAW_E + m - N_EXP if m < N_EXP + RAW else n - RAW


def split_slot(n):
    if n < N_FRONT:
        return n % SPLIT
    m = n - N_FRONT
    if m < N_EXP:
        return (N_FRONT + m % SPLIT_E) % SPLIT if m % SPLIT_E < SPLIT else SPLIT
    return split_slot(N_FRONT + (m - N_EXP) % SPLIT)


def split_before(n):
    if n < N_FRONT + SPLIT:
        return n - SPLIT
    m = n - N_FRONT
    if m < N_EXP:
        return n - SPLIT_E
    return N_FRONT + N_EXP - SPLIT_E + m - N_EXP if m < N_EXP + SPLIT else n - SPLIT


assert N_EXP % RAW_E == 0 and N_EXP % SPLIT_E == 0 and 12 % RAW_E == 0 and 12 % SPLIT_E == 0


def layer_kernel(nc, x, p, g_attn, w_in, w_br_a, w_br_b, w_out, g_ffn, w_grp, b_grp, w_rt, b_rt,
                 w_gate, w_up, w_down, g_ple, w_ple_gate, w_ple_proj, g_final, const, out):
    K = 1024
    base = (nc.sbuf_base + 31) // 32 * 32
    size = {"cst": 4 * NCONST, "raw": RAW * 8 * K, "whi": SPLIT * 8 * K, "wlo": SPLIT * 8 * K, "gain": 4 * K,
            "stage": 16 * K, "hi": 16 * K, "lo": 16 * K, "qk": 16 * K, "v": 8 * K, "rope": 4 * K, "work": 4 * K + 512,
            "o": 16 * K, "small": 12 * K, "ik": 2 * K, "misc": 6 * K}
    start = {}
    for name, n in size.items():
        start[name] = base
        base += (n + 31) // 32 * 32
    assert base <= nc.sbuf_usable_end, base

    def sb(name, region, shape, dt=F32, skip=0):
        return nc.alloc_sbuf_tensor_at(name, shape, dt, offset=start[region] + skip)

    misc_at = [0]

    def tiny(name, shape, dt=F32):
        n = 4 * int(np.prod(shape[1:]))
        at = misc_at[0]
        misc_at[0] += (n + 31) // 32 * 32
        assert misc_at[0] <= size["misc"], name
        return nc.alloc_sbuf_tensor_at(name, shape, dt, offset=start["misc"] + at)

    def sem(name):
        return nc.alloc_semaphore(name)

    cst = sb("cst", "cst", [P, NCONST])
    raw = sb("raw", "raw", [P, RAW, HALF_W])
    w_hi = sb("w_hi", "whi", [P, SPLIT, HALF_W], F32R)
    w_lo = sb("w_lo", "wlo", [P, SPLIT, HALF_W], F32R)
    raw_more = [sb(f"raw_more_{r}", r, [P, HALF_W]) for r in ("hi", "lo")]
    w_hi_more = sb("w_hi_more", "qk", [P, HALF_W], F32R)
    w_lo_more = sb("w_lo_more", "qk", [P, HALF_W], F32R, skip=8 * K)
    raw_at = [raw[:, k, :] for k in range(RAW)] + [v[:] for v in raw_more]
    w_hi_at = [w_hi[:, k, :] for k in range(SPLIT)] + [w_hi_more[:]]
    w_lo_at = [w_lo[:, k, :] for k in range(SPLIT)] + [w_lo_more[:]]
    gain = sb("gain", "gain", [P, D])
    stage_tok = sb("rows_tok", "stage", [P, NT, D])[:]
    stage_z = sb("z_chunks", "stage", [P, 2, NT, AW])[:]
    act_hi = sb("act_hi", "hi", [P, KD, S], F32R)
    act_lo = sb("act_lo", "lo", [P, KD, S], F32R)
    qt = sb("qt", "qk", [P, NT, S])[:]
    kt_ = sb("kt", "qk", [P, NT, S], skip=8 * K)[:]
    v_sb = sb("v", "v", [P, NT, AW])[:]
    rope_t = sb("rope_t", "rope", [P, NT, NH, 2 * ROT])
    work = sb("work", "work", [P, 9 * P])
    o_sb = {"a": sb("o_a", "o", [P, NT, AW])[:], "b": sb("o_b", "o", [P, NT, AW], skip=8 * K)[:]}
    iqt = sb("iqt", "o", [P, NT, S], skip=8 * K)[:]
    ikt = sb("ikt", "ik", [P, S])
    small = sb("small", "small", [P, 6, S])
    ot_hi = {x_: sb(f"ot_{x_}_hi", "qk", [P, NT, S], F32R, skip=8 * K * n)[:] for n, x_ in enumerate("ab")}
    ot_lo = {x_: sb(f"ot_{x_}_lo", "v", [P, NT, S], F32R, skip=8 * K * n)[:] for n, x_ in enumerate("ab")}
    xres = sb("x_after", "o", [P, NT, D])[:]
    squares = sb("squares", "o", [P, NT, D])[:]
    rt = sb("rt", "work", [P, 8 * NT * NE])
    xg = sb("xg", "stage", [P, 2, D])[:]
    y_sb = sb("y", "stage", [P, 2, D], skip=8 * K)[:]
    xt_hi = sb("xt_hi", "hi", [P, KD * P], F32R, skip=8 * K)[:]
    xt_lo = sb("xt_lo", "hi", [P, KD * P], F32R, skip=12 * K)[:]
    assert 2 * FIRST == P
    ht_hi = sb("ht_hi", "lo", [P, FE // P, P], F32R, skip=8 * K)[:]
    ht_lo = sb("ht_lo", "lo", [P, FE // P, P], F32R, skip=10 * K)[:]
    y_in = sb("y_in", "qk", [P, 2, 2 * D])[:]
    proj_sb = sb("ple_projected", "v", [P, 2, NT, 512])[:]
    assert size["v"] + size["rope"] + size["work"] >= 16 * K
    pin = sb("p_rows", "v", [P, NT, PLE])[:]
    pt_hi = sb("pt_hi", "v", [P, 2, S], F32R, skip=4 * K)[:]
    pt_lo = sb("pt_lo", "v", [P, 2, S], F32R, skip=8 * K)[:]

    iws = tiny("iws", [P, NT, NH])
    m8 = tiny("m8", [P, NT, 8])
    stat = tiny("stat", [P, 24])
    eps = tiny("eps", [P, 1])
    nm = tiny("nm", [P, 4])
    rs = tiny("rs", [P, 4])
    ri = tiny("ri", [P, 4])
    br = tiny("br", [P, NG + NE])
    table = tiny("table", [P, NE * CH + 2 * CH, 4], I32)
    row_of = tiny("row_of", [P, 2, 4], I32)
    pair_of = tiny("pair_of", [P, 2, 4], I32)
    rs_small = tiny("rs_small", [P, 32 * NT])
    rows = tiny("rows", [P, 2 * NT, 4], I32)
    dest = tiny("dest", [P, 2 * NT], I32)
    over_f = tiny("over_f", [P, 32])
    over = tiny("over", [P, 32], I32)
    wr = sb("wr", "ik", [P, KD, NG + NE])
    wr_hi = tiny("wr_hi", [P, KD, NG + NE], F32R)
    wr_lo = tiny("wr_lo", [P, KD, NG + NE], F32R)

    logits = small[:, 4, 0:NT * (NG + NE)].rearrange("p (t k) -> p t k", t=NT)
    member = rt[:, 4 * NT * NE:5 * NT * NE].rearrange("p (t e) -> p t e", t=NT)
    member_wide = small[:, 3, :].rearrange("p (t k) -> p t k", t=NT)
    score_at = {1: 0, 2: 2 * P, 3: 5 * P}

    def score(t):
        return work[:, score_at[t]:score_at[t] + (t + 1) * P]

    def turn_dst(s):
        _, a, i = s
        if a == "ix":
            return ikt[:]
        if a in ("iq", "qa", "qb", "ka", "kb"):
            return {"iq": iqt, "qa": qt, "qb": qt, "ka": kt_, "kb": kt_}[a][:, i, :]
        if a in ROW_TURNS:
            t, h = tile_and_half(a, i)
            return [v[:, 4 * h:4 * h + 4, t * P:(t + 1) * P] for v in (act_hi, act_lo)]
        hi, lo = {"oa": (ot_hi["a"], ot_lo["a"]), "ob": (ot_hi["b"], ot_lo["b"]), "p": (pt_hi, pt_lo)}[a]
        return hi[:, i, :], lo[:, i, :]

    def c(name):
        a, b = CONST_COLS[name]
        return cst[:, a:b]

    def c4(name, k):
        return c(name).rearrange("p (t k) -> p t k", k=k)

    ident = c("ident")

    psum = nc.alloc_psum_tensor("psum", [P, 8, S], F32)
    bank = [psum[:, b, :] for b in range(8)]

    h2_d = nc.dram_tensor("h2_rows", [S, D], F32, kind="Internal").ap()
    pairs_d = nc.dram_tensor("pair_rows", [2 * S, D], F32, kind="Internal").ap()
    table_d = nc.dram_tensor("slot_table", [P * NE * CH, 4], I32, kind="Internal").ap()

    bank_filled = [sem(f"bank_filled_{b}") for b in range(8)]
    bank_drained = [sem(f"bank_drained_{b}") for b in range(8)]
    raw_loaded = [[sem(f"{phase}_loaded_{b}") for b in range(n)]
                  for phase, n in (("front", RAW), ("expert", RAW_E), ("tail", RAW))]
    hi_done, lo_done = sem("hi_done"), sem("lo_done")
    half_started = sem("half_started")
    turn_hi = sem("turn_hi")
    ix_t = sem("ix_t")
    logits_t = sem("logits_t")
    wr_split, eps_set = sem("wr_split"), sem("eps_set")
    merged_done, ple_added = sem("merged_done"), sem("ple_added")
    ident_in, const_in, x_in = sem("ident_in"), sem("const_in"), [sem(f"x_in_{t}") for t in range(NT)]
    gain_in, small_in, p_in = sem("gain_in"), sem("small_in"), sem("p_in")
    sumsq, root, normed = sem("sumsq"), sem("root"), sem("normed")
    roped, pool_chain, dve_chain = sem("roped"), sem("pool_chain"), sem("dve_chain")
    acc_done = sem("acc_done")
    max_done, mark_done, selected = sem("max_done"), sem("mark_done"), sem("selected")
    exp_done = sem("exp_done")
    x_back, h2_out = sem("x_back"), sem("h2_out")
    ngmax_done, gexp_done, e2_done = sem("ngmax_done"), sem("gexp_done"), sem("e2_done")
    top_done, rank_done, count_done, list_done = sem("top_done"), sem("rank_done"), sem("count_done"), sem("list_done")
    member_f, over_list, rows_ready, fill_ready = sem("member_f"), sem("over_list"), sem("rows_ready"), sem("fill_ready")
    table_filled, table_written, table_in = sem("table_filled"), sem("table_written"), sem("table_in")
    rows_set, pairs_set, gathered, x_turned = sem("rows_set"), sem("pairs_set"), sem("gathered"), sem("x_turned")
    xt_hi_done, xt_done, gate_done, up_done = sem("xt_hi_done"), sem("xt_done"), sem("gate_done"), sem("up_done")
    silu_done, hid_done, hid_turned = sem("silu_done"), sem("hid_done"), sem("hid_turned")
    ht_hi_done, ht_done, down_done, y_done, scattered = (sem("ht_hi_done"), sem("ht_done"), sem("down_done"),
                                                         sem("y_done"), sem("scattered"))
    pairs_in, pairs_added = [sem("pairs_in_even"), sem("pairs_in_odd")], sem("pairs_added")
    ov = {n: sem("ov_" + n) for n in ("loaded", "hi", "lo", "started", "rows", "pairs", "gathered", "turned", "xt_hi", "xt",
                                      "gate", "up", "silu", "hid", "hid_turned", "ht_hi", "ht", "down", "y", "scattered",
                                      "act_end", "sp_end", "pool_end", "pe_end")}
    out_done, pool_steps, sp_steps, pe_steps = sem("out_done"), sem("pool_steps"), sem("sp_steps"), sem("pe_steps")

    def claim(pe, step):
        b, n = BANK[step]
        if n > 1:
            pe.wait_ge(bank_drained[b], n - 1)
        return bank[b]

    def filled(eng, step):
        b, n = BANK[step]
        eng.wait_ge(bank_filled[b], n)
        return bank[b]

    def drained(eng, step):
        b, n = BANK[step]
        eng.wait_ge(bank_drained[b], n)

    def tile_of(s, t):
        return (s[0], s[1], "tile", t)

    def half_view(buf, n, k):
        w = HD + NH if n == HALF_OF[("z", "ix", 0)] else HALF_W // 4
        return buf[:, 0:k * w].rearrange("p (k n) -> p k n", k=k)

    def tiles_in(s):
        return KD if s[1] == "ix" else PLE // P if s[0] == "ple_proj" else 4

    def columns_of(n):
        if n == HALF_OF[("z", "ix", 0)]:
            return KD * (HD + NH)
        return HALF_W // 2 if n in (HALF_OF[("ple_proj", 0, 0)], HALF_OF[("ple_proj", 1, 0)]) else HALF_W

    def x_turns(n_rows):
        return psum[:, 0:2, :].rearrange("p b (k s) -> p (b k) s", k=4)[:, :, 0:n_rows]

    def h_turns(n_rows):
        return bank[4].rearrange("p (k s) -> p k s", k=FE // P)[:, :, 0:n_rows]

    def split_high(act, n, i=0):
        b, group, turns = raw_turn(n)
        act.wait_ge(raw_loaded[group][b], 16 * turns + 16 * (12 // RAW_E) * i)
        if split_before(n) == N_FRONT - 1:
            filled(act, ("out", 1, "tile", NT - 1))
        elif split_before(n) >= (0 if n < N_FRONT + SPLIT else N_FRONT):
            act.wait_ge(half_started, split_before(n) + 2 + 12 * i)
        elif n >= N_FRONT:
            for t in range(NT):
                filled(act, ("branch_b", 1, "tile", t))
        w = columns_of(n)
        act.copy(w_hi_at[split_slot(n)][:, 0:w], raw_at[b][:, 0:w]).then_inc(hi_done, 1)

    def split_low(dve, n, i=0):
        dve.wait_ge(hi_done, n + 1 + 12 * i)
        w, k = columns_of(n), split_slot(n)
        dve.tensor_tensor(w_lo_at[k][:, 0:w], raw_at[raw_turn(n)[0]][:, 0:w], w_hi_at[k][:, 0:w].bitcast(F32),
                          ALU.subtract).then_inc(lo_done, 1)

    def xt_view(v, b, n_rows):
        return v[:, b * KD * n_rows:(b + 1) * KD * n_rows].rearrange("p (k s) -> p k s", k=KD)

    EXPERT_HALVES = ("up0", "up1", "gate0", "gate1", "down0", "down1")
    LAST_HALVES = ("up0", "up1", "down0", "down1")
    OVER_HALVES = ("gate0", "gate1", "up0", "up1", "down0", "down1")
    BASE_E = N_FRONT + 2

    def wait_for(eng, sem_, value):
        if not isinstance(value, int) or value > 0:
            eng.wait_ge(sem_, value)

    def unit(u):
        return u // NT, u % NT

    BR = {"a": 0, "b": 1}
    NU = NH * NT
    block = nc.Block()
    block.__enter__()

    @block.sync
    def _(sp):
        w_in_v = w_in[0].rearrange("(k p) n -> p k n", p=P)
        x_v = x[0].rearrange("(t p) d -> p t d", p=P)
        by_rows = lambda w: w.rearrange("(k p) n -> p k n", p=P)

        def load(n, src, i=0):
            before = raw_before(n)
            if before >= (0 if n < N_FRONT + RAW else N_FRONT):
                sp.wait_ge(lo_done, before + 1 + 12 * i)
                if not isinstance(i, int):
                    sp.sem_inc(sp_steps, 1)
            elif n >= N_FRONT:
                sp.wait_ge(logits_t, 1)
            w = columns_of(n)
            k = src.shape[1]
            b, group, _ = raw_turn(n)
            sp.dma_start(raw_at[b][:, 0:w].rearrange("p (k n) -> p k n", k=k), src).then_inc(raw_loaded[group][b], 16)

        def source(s):
            kind, a, i = s
            if kind == "z":
                if a == "ix":
                    return w_in_v[:, :, IN_OFF[a]:IN_OFF[a] + HD + NH]
                return w_in_v[:, 4 * i:4 * i + 4, IN_OFF[a]:IN_OFF[a] + 512]
            if kind in ("gate_a", "gate_b"):
                off = IN_OFF["g" + kind[-1]] + 512 * a
                return w_in_v[:, 4 * i:4 * i + 4, off:off + 512]
            w = {"branch_a": w_br_a, "branch_b": w_br_b, "out": w_out, "ple_gate": w_ple_gate, "ple_proj": w_ple_proj}[kind]
            k = tiles_in(s)
            return by_rows(w[0])[:, k * i:k * (i + 1), a * 512:(a + 1) * 512]

        sp.dma_start(stage_tok[:, 0], x_v[:, 0]).then_inc(x_in[0], 16)
        sp.dma_start(gain[:], g_attn[0:1, :].partition_broadcast(P)).then_inc(gain_in, 16)
        sp.dma_start(cst[:, 0:P], const[:, 0:P]).then_inc(ident_in, 16)
        for t in range(1, NT):
            sp.dma_start(stage_tok[:, t], x_v[:, t]).then_inc(x_in[t], 16)
        for n, s in enumerate(HALVES):
            load(n, source(s))
            if n == 1:
                sp.dma_start(cst[:, P:], const[:, P:]).then_inc(const_in, 16)
        views = {"gate": w_gate[0].rearrange("e (p k) f -> e p k f", p=P),
                 "up": w_up[0].rearrange("e (p k) f -> e p k f", p=P),
                 "down": w_down[0].rearrange("e (k p) d -> e p k d", p=P)}

        def expert_source(name, e):
            what, h = name[:-1], int(name[-1])
            v = views[what][e]
            return v[:, :, h * 512:(h + 1) * 512] if what == "down" else v[:, 4 * h:4 * h + 4, :]

        def load_expert(e0, i=0):
            e = e0 + 2 * i
            names = EXPERT_HALVES if e0 != NE - 1 else LAST_HALVES
            for r, name in enumerate(names):
                load(BASE_E + 6 * e0 + r, expert_source(name, e + 1 if name.startswith("gate") else e), i)

        load(N_FRONT, expert_source("gate0", 0))
        load(N_FRONT + 1, expert_source("gate1", 0))
        load_expert(0)
        sp.wait_ge(gathered, 32)
        sp.sem_inc(sp_steps, 1)
        with sp.Fori(0, NE // 2 - 1) as i:
            load_expert(1, i)
            load_expert(2, i)
        load_expert(NE - 1)
        sp.wait_ge(over_list, 1)
        n_over = sp.value_load(over[0:1, 16:17], min_val=0, max_val=NOVER)
        with sp.If(n_over > 0):
            with sp.Fori(0, NOVER) as i:
                with sp.If(i < n_over):
                    sp.wait_ge(lo_done, N_FRONT + N_EXP)
                    code = sp.value_load(over[0:1, bass.ds(i, 1)], min_val=0, max_val=NE * CH - 1)
                    e = sp.snap(code // CH, min_val=0, max_val=NE - 1)
                    for r, name in enumerate(OVER_HALVES):
                        if r >= RAW:
                            sp.wait_ge(ov["lo"], 6 * i + (r - RAW + 1))
                            sp.sem_inc(sp_steps, 1)
                        if r:
                            sp.wait_ge(ov["loaded"], 96 * i + 16 * r)
                            sp.sem_inc(sp_steps, 1)
                        sp.dma_start(raw[:, r % RAW, :].rearrange("p (k n) -> p k n", k=4), expert_source(name, e)
                                     ).then_inc(ov["loaded"], 16)
                    sp.wait_ge(ov["scattered"], 16 * i + 16)
                    sp.sem_inc(ov["sp_end"], 1)
        for n, s in enumerate(TAIL[:RAW]):
            load(N_FRONT + N_EXP + n, source(s))
        sp.wait_ge(scattered, 16 * NE)
        for t in range(NT):
            if t >= 2:
                sp.wait_ge(pairs_added, t - 1)
            sp.dma_start(y_in[:, t % 2, :], pairs_d[t * 2 * P:(t + 1) * 2 * P].rearrange("(p k) d -> p (k d)", k=2)
                         ).then_inc(pairs_in[t % 2], 16)
        for n, s in enumerate(TAIL[RAW:]):
            load(N_FRONT + N_EXP + RAW + n, source(s))
        out_v = out[0].rearrange("(t p) d -> p t d", p=P)
        for t in range(NT):
            sp.wait_ge(normed, 3 * NT + 1 + t)
            sp.dma_start(out_v[:, t], stage_tok[:, t]).then_inc(out_done, 16)
        sp.wait_ge(out_done, 16 * NT)

    @block.tensor
    def _(pe):
        def transposes(step, views):
            ps = claim(pe, step)
            for n, v in enumerate(views):
                mm = pe.transpose(ps[0:v.shape[1], n * P:(n + 1) * P], v, ident)
            mm.then_inc(bank_filled[BANK[step][0]], 1)

        def product(ps, pairs):
            for n, (a, b) in enumerate(pairs):
                mm = pe.matmul(ps, a, b, start=(n == 0), stop=(n == len(pairs) - 1))
            return mm

        def three(ps, left, right, first, last):
            ops = [(left[0], right[0]), (left[1], right[0]), (left[0], right[1])]
            mms = [pe.matmul(ps, a, b, start=first and n == 0, stop=last and n == 2) for n, (a, b) in enumerate(ops)]
            return mms[0], mms[2]

        def half_product(s, left, k0):
            n, k_n, last = HALF_OF[s], tiles_in(s), last_half(s)
            pe.wait_ge(lo_done, n + 1)
            hi, lo = [half_view(v[split_slot(n)], n, k_n) for v in (w_hi_at, w_lo_at)]
            w = hi.shape[2]
            for t in range(NT):
                b = BANK[tile_of(s, t)][0]
                if s[2] == 0:
                    claim(pe, tile_of(s, t))
                for k in range(k_n):
                    l_ = [v[:, k0 + k, t * P:(t + 1) * P] for v in left]
                    m0, m1 = three(bank[b][:, 0:w], l_, (hi[:, k, :], lo[:, k, :]), s[2] == 0 and k == 0,
                                   last and k == k_n - 1)
                    if t == 0 and k == 0:
                        m0.then_inc(half_started, 1)
                if last:
                    m1.then_inc(bank_filled[b], 1)

        def front_step(s):
            kind, a, i = s
            if kind in ("rope", "topk", "select", "norm"):
                return
            if kind == "turn":
                if s == ("turn", "h", 0):
                    pe.wait_ge(ident_in, 16)
                if a in ("h", "h2", "h3"):
                    pe.wait_ge(normed, NT * ("h", "h2", "h3").index(a) + tile_and_half(a, i)[0] + 1)
                elif a in ROPES and i == 0:
                    pe.wait_ge(roped, ROPES.index(a) + 1)
                elif a == "oa" and i == 0:
                    drained(pe, ("pv", "a", NU - 1))
                elif a == "ob" and i == 0:
                    drained(pe, ("pv", "b", NU - 1))
                    drained(pe, ("pv", "b", NU - 2))
                elif a == "merged":
                    pe.wait_ge(merged_done, i + 1)
                elif a == "p" and i == 0:
                    pe.wait_ge(p_in, 16)
                if a in ROW_TURNS:
                    t, h = tile_and_half(a, i)
                    views = [stage_tok[:, t, k * P:(k + 1) * P] for k in range(4 * h, 4 * h + 4)]
                elif a in ("oa", "ob"):
                    views = [o_sb[a[1]][:, t, i * P:(i + 1) * P] for t in range(NT)]
                elif a == "p":
                    views = [pin[:, t, i * P:(i + 1) * P] for t in range(NT)]
                else:
                    views = [stage_z[:, STAGE[a], t, i * P:(i + 1) * P] for t in range(NT)]
                transposes(s, views)
            elif kind == "z":
                if s == ("z", "iq", 0):
                    for k in range(KD):
                        drained(pe, ("turn", "h", k))
                if a != "ix":
                    half_product(s, (act_hi, act_lo), 4 * i)
                    return
                n, w = HALF_OF[s], HD + NH
                pe.wait_ge(lo_done, n + 1)
                parts = [half_view(v[split_slot(n)], n, KD) for v in (w_hi_at, w_lo_at)]
                for k in range(KD):
                    m0, m1 = three(bank[7][0:w, :], [v[:, k, :] for v in parts], (act_hi[:, k, :], act_lo[:, k, :]),
                                   k == 0, k == KD - 1)
                    if k == 0:
                        m0.then_inc(half_started, 1)
                m1.then_inc(ix_t, 1)
            elif kind == "ix_back":
                pe.wait_ge(ix_t, 2)
                ps, w = claim(pe, s), HD + NH
                for t in range(NT):
                    mm = pe.transpose(ps[:, t * w:(t + 1) * w], small[0:w, 5, t * P:(t + 1) * P], ident[0:w, 0:w])
                mm.then_inc(bank_filled[BANK[s][0]], 1)
            elif kind == "rel":
                t, h = a, i
                if (t, h) == (1, 0):
                    for cc in range(NT):
                        drained(pe, ("turn", "iq", cc))
                    drained(pe, ("turn", "ix", 0))
                ps = claim(pe, s)
                lo = HD * (h % 2)
                pe.matmul(ps[:, 0:(t + 1) * P], iqt[lo:lo + HD, h // 2, t * P:(t + 1) * P],
                          ikt[lo:lo + HD, 0:(t + 1) * P], start=True, stop=True
                          ).then_inc(bank_filled[BANK[s][0]], 1)
            elif kind == "scores":
                h, t = unit(i)
                if i == 0:
                    for cc in range(NT):
                        drained(pe, ("turn", "q" + a, cc))
                        drained(pe, ("turn", "k" + a, cc))
                ps = claim(pe, s)
                lo = HD * (h % 2)
                pe.matmul(ps[:, 0:(t + 1) * P], qt[lo:lo + HD, h // 2, t * P:(t + 1) * P],
                          kt_[lo:lo + HD, h // 2, 0:(t + 1) * P], start=True, stop=True
                          ).then_inc(bank_filled[BANK[s][0]], 1)
            elif kind == "turn_p":
                h, t = unit(i)
                pe.wait_ge(exp_done, NU * BR[a] + i + 1)
                transposes(s, [small[:, 2 + i % 2, j * P:(j + 1) * P] for j in range(t + 1)])
            elif kind == "pv":
                h, t = unit(i)
                if i == 0:
                    for tt in range(NT):
                        drained(pe, ("z", "v" + a, "tile", tt))
                drained(pe, ("turn_p", a, i))
                ps = claim(pe, s)
                mm = product(ps[:, 0:HD], [(small[:, 4 + i % 2, j * P:(j + 1) * P], v_sb[:, j, h * HD:(h + 1) * HD])
                                           for j in range(t + 1)])
                mm.then_inc(bank_filled[BANK[s][0]], 1)
            elif kind in ("gate_a", "gate_b"):
                half_product(s, (act_hi, act_lo), 4 * i)
            elif kind in ("branch_a", "branch_b"):
                x_ = kind[-1]
                if a == 0:
                    for cc in range(NT):
                        drained(pe, ("turn", "o" + x_, cc))
                half_product(s, (ot_hi[x_], ot_lo[x_]), 0)
            elif kind == "out":
                if (a, i) == (0, 0):
                    for k in range(KD):
                        drained(pe, ("turn", "merged", k))
                half_product(s, (act_hi, act_lo), 4 * i)
            elif kind == "router":
                pe.wait_ge(wr_split, 2)
                for k in range(KD):
                    drained(pe, ("turn", "h2", k))
                w = NG + NE
                for k in range(KD):
                    _, mm = three(bank[1][0:w, :], (wr_hi[:, k, :], wr_lo[:, k, :]), (act_hi[:, k, :], act_lo[:, k, :]),
                                  k == 0, k == KD - 1)
                mm.then_inc(logits_t, 1)
                pe.wait_ge(logits_t, 2)
                ps = claim(pe, s)
                for t in range(NT):
                    mm = pe.transpose(ps[:, t * w:(t + 1) * w], small[0:w, 5, t * P:(t + 1) * P], ident[0:w, 0:w])
                mm.then_inc(bank_filled[BANK[s][0]], 1)
            elif kind == "ple_gate":
                if (a, i) == (0, 0):
                    for k in range(KD):
                        drained(pe, ("turn", "h3", k))
                half_product(s, (act_hi, act_lo), 4 * i)
            elif kind == "ple_proj":
                if a == 0:
                    for k in range(PLE // P):
                        drained(pe, ("turn", "p", k))
                half_product(s, (pt_hi, pt_lo), 0)

        for s in FRONT:
            front_step(s)

        pe.wait_ge(top_done, 2)
        pe.matmul(bank[1][:, 0:NT * NE], c("before"), member.rearrange("p t e -> p (t e)"), start=True, stop=False)
        for u in range(NT - 1):
            mm = pe.matmul(bank[1][:, (u + 1) * NE:NT * NE].rearrange("p (t e) -> p t e", e=NE), c("ones"),
                           member[:, u:u + 1, :].to_broadcast([P, NT - 1 - u, NE]), start=False, stop=(u == NT - 2))
        mm.then_inc(rank_done, 1)
        for t in range(NT):
            mm = pe.matmul(bank[2][0:P, 0:1], member_wide[:, t, :], c("ones")[:, 0:1], start=(t == 0), stop=(t == NT - 1))
        mm.then_inc(count_done, 1)
        pe.wait_ge(member_f, 1)
        pe.matmul(bank[3][:, 0:1], c("before"), over_f[:, 0:1], start=True, stop=True).then_inc(list_done, 1)
        pe.wait_ge(member_f, 2)
        pe.matmul(bank[4][0:1, 0:16], c("code"), over_f[:, 8:24], start=True, stop=True)
        pe.matmul(bank[5][0:1, 0:1], c("ones")[:, 0:1], over_f[:, 0:1], start=True, stop=True).then_inc(list_done, 1)

        def turn_rows(b, done, n_rows=FIRST):
            pe.sem_inc(pe_steps, 1)
            for k in range(KD):
                mm = pe.transpose(x_turns(n_rows)[:, k, :], xg[0:n_rows, b, k:D:KD], ident[0:n_rows, 0:n_rows])
            mm.then_inc(done, 1)

        def turn_hidden(done, n_rows=FIRST):
            pe.sem_inc(pe_steps, 1)
            for k in range(FE // P):
                mm = pe.transpose(h_turns(n_rows)[:, k, :], small[0:n_rows, 1, k * P:(k + 1) * P],
                                  ident[0:n_rows, 0:n_rows])
            mm.then_inc(done, 1)

        def expert_half(name, b, slot, started, n_rows=FIRST):
            what, h = name[:-1], int(name[-1])
            hi, lo = (v[slot].rearrange("p (k n) -> p k n", k=4) for v in (w_hi_at, w_lo_at))
            for k in range(4):
                if what == "down":
                    ps = bank[5 + h]
                    left = [v[:, k, 0:n_rows] for v in (ht_hi, ht_lo)]
                    first, last = k == 0, k == 3
                else:
                    ps = bank[2 if what == "gate" else 3]
                    left = [xt_view(v, b, n_rows)[:, 4 * h + k, :] for v in (xt_hi, xt_lo)]
                    first, last = h == 0 and k == 0, h == 1 and k == 3
                m0, m1 = three(ps[0:n_rows, :], left, (hi[:, k, :], lo[:, k, :]), first, last)
                if k == 0:
                    m0.then_inc(started, 1)
            return m1

        def half_at(name, n, b, i=0):
            pe.wait_ge(lo_done, n + 1 + 12 * i)
            return expert_half(name, b, split_slot(n), half_started)

        pe.wait_ge(over_list, 1)
        pe.wait_ge(gathered, 16)
        turn_rows(0, x_turned)
        pe.wait_ge(xt_done, 1)
        half_at("gate0", N_FRONT, 0)
        half_at("gate1", N_FRONT + 1, 0).then_inc(gate_done, 1)

        def expert(e0, i=0):
            e, b, n = e0 + 2 * i, e0 % 2, BASE_E + 6 * e0
            more = e0 != NE - 1
            wait_for(pe, hid_done, e)
            half_at("up0", n, b, i)
            if more:
                pe.wait_ge(gathered, 16 * e + 32)
                pe.wait_ge(xt_done, e + 1)
                turn_rows(1 - b, x_turned)
            half_at("up1", n + 1, b, i).then_inc(up_done, 1)
            if more:
                pe.wait_ge(xt_done, e + 2)
                pe.wait_ge(silu_done, e + 1)
                half_at("gate0", n + 2, 1 - b, i)
            pe.wait_ge(hid_done, e + 1)
            wait_for(pe, ht_done, e)
            turn_hidden(hid_turned)
            if more:
                half_at("gate1", n + 3, 1 - b, i).then_inc(gate_done, 1)
                n += 2
            pe.wait_ge(ht_done, e + 1)
            wait_for(pe, y_done, e)
            half_at("down0", n + 2, b, i)
            half_at("down1", n + 3, b, i).then_inc(down_done, 1)

        expert(0)
        with pe.Fori(0, NE // 2 - 1) as i:
            expert(1, i)
            expert(2, i)
        expert(NE - 1)
        n_over = pe.value_load(over[0:1, 16:17], min_val=0, max_val=NOVER)
        with pe.If(n_over > 0):
            with pe.Fori(0, NOVER) as i:
                with pe.If(i < n_over):
                    pe.wait_ge(y_done, NE)
                    pe.wait_ge(ov["gathered"], 16 * i + 16)
                    turn_rows(0, ov["turned"], P)
                    pe.wait_ge(ov["xt"], i + 1)
                    for r, name in enumerate(OVER_HALVES):
                        if name == "down0":
                            pe.wait_ge(ov["hid"], i + 1)
                            turn_hidden(ov["hid_turned"], P)
                            pe.wait_ge(ov["ht"], i + 1)
                        pe.wait_ge(ov["lo"], 6 * i + r + 1)
                        mm = expert_half(name, 0, r % SPLIT, ov["started"], P)
                        if r % 2:
                            mm.then_inc(ov[name[:-1]], 1)
                    pe.wait_ge(ov["y"], i + 1)
                    pe.sem_inc(ov["pe_end"], 1)
        pe.wait_ge(y_done, NE)
        for s in BACK:
            front_step(s)

    @block.scalar
    def _(act):
        def projected():
            for m in range(2):
                for t in range(NT):
                    tile = ("ple_proj", m, "tile", t)
                    filled(act, ("ple_proj", 1, "tile", NT - 1))
                    act.copy(proj_sb[:, m, t, :], filled(act, tile)).then_inc(bank_drained[BANK[tile][0]], 1)

        def square(n, t, junk):
            if n == 0:
                act.wait_ge(x_in[t], 16)
            if n:
                act.wait_ge(normed, NT * (n - 1) + t + 1)
            if n == 1:
                for m in range(2):
                    drained(act, ("out", m, "tile", t))
            if n == 2:
                act.wait_ge(pairs_added, t + 1)
            if n == 3:
                act.wait_ge(ple_added, NT + t + 1)
            if n and t == 0:
                before = {1: "merged", 2: "h2", 3: "h3"}[n]
                for k in range(KD):
                    filled(act, ("turn", before, k))
            act.activation(junk[:, t], (stage_tok if n == 0 else xres)[:, t], ACT.Square, accum_out=stat[:, t:t + 1]
                           ).then_inc(sumsq, 1)

        def square_root(n, t):
            act.wait_ge(sumsq, NT * n + t + 1)
            act.activation(stat[:, 4 + t:5 + t], stat[:, t:t + 1], ACT.Sqrt, scale=1.0 / D, bias=eps[:, 0:1]
                           ).then_inc(root, 1)

        def step(s):
            kind, a, i = s
            if kind in WEIGHTS and HALF_OF[s] + AHEAD < N_ALL:
                split_high(act, HALF_OF[s] + AHEAD)
            if kind == "norm":
                n = {"ffn": 1, "ple": 2, "final": 3}[a]
                for t in range(NT):
                    if n == 3 and t < NT - 1:
                        square_root(n, t)
                        continue
                    square(n, t, stage_tok)
                    square_root(n, t)
                    if (n, t) == (2, 0):
                        projected()
                return
            if kind == "turn":
                ps = filled(act, s)
                b = BANK[s][0]
                if a in SPLIT_TURNS:
                    if a in ROW_TURNS:
                        ps = ps.rearrange("p (k s) -> p k s", k=4)
                    act.copy(turn_dst(s)[0], ps).then_inc(turn_hi, 1)
                else:
                    act.copy(turn_dst(s), ps).then_inc(bank_drained[b], 1)
            elif kind == "z":
                if not last_half(s):
                    return
                if a == "ix":
                    act.wait_ge(ix_t, 1)
                    act.copy(small[0:HD + NH, 5, :], bank[7][0:HD + NH, :]).then_inc(ix_t, 1)
                    return
                if a in ROPES and ROPES.index(a) >= 2:
                    prev = ROPES[ROPES.index(a) - 2]
                    for cc in range(1 if prev == "ix" else NT):
                        filled(act, ("turn", prev, cc))
                for t in range(NT):
                    tile = tile_of(s, t)
                    ps, b = filled(act, tile), BANK[tile][0]
                    if a in ("va", "vb"):
                        act.copy(v_sb[:, t, :], ps[:]).then_inc(bank_drained[b], 1)
                    else:
                        act.copy(stage_z[:, STAGE[a], t, :], ps[:]).then_inc(bank_drained[b], 1)
            elif kind == "ix_back":
                v = filled(act, s)[:, 0:NT * (HD + NH)].rearrange("p (t k) -> p t k", t=NT)
                act.copy(stage_z[:, 1, :, 0:HD], v[:, :, 0:HD])
                act.copy(stage_z[:, 1, :, HD:2 * HD], v[:, :, 0:HD])
                act.activation(iws[:], v[:, :, HD:HD + NH], ACT.Copy, scale=float(np.float32(NH ** -0.5))
                               ).then_inc(bank_drained[BANK[s][0]], 1)
            elif kind == "router":
                act.wait_ge(logits_t, 1)
                act.copy(small[0:NG + NE, 5, :], bank[1][0:NG + NE, :]).then_inc(logits_t, 1)
            elif kind in ("gate_a", "gate_b", "ple_gate"):
                if not last_half(s):
                    return
                for t in range(NT):
                    ps, b = filled(act, tile_of(s, t)), BANK[tile_of(s, t)][0]
                    if (kind, a) == ("ple_gate", 1):
                        act.wait_ge(ple_added, t + 1)
                    elif GATES.index((kind, a, t)) >= NT:
                        kk, aa, tt = BRANCHES[GATES.index((kind, a, t)) - NT]
                        drained(act, (kk, aa, "tile", tt))
                    act.activation(small[:, t, :], ps[:], ACT.Sigmoid).then_inc(bank_drained[b], 1)
                    if (kind, a) == ("ple_gate", 1) and t:
                        square(3, t - 1, stage_tok)
            elif kind == "rel":
                n = (a - 1) * NH + i
                ps = filled(act, s)
                b = BANK[s][0]
                if n >= 2:
                    act.wait_ge(acc_done, n - 1)
                act.activation(small[:, n % 2, 0:(a + 1) * P], ps[:, 0:(a + 1) * P], ACT.Relu, scale=HD ** -0.5
                               ).then_inc(bank_drained[b], 1)
            elif kind == "scores":
                h, t = unit(i)
                n = NU * BR[a] + i
                drained(act, s)
                if i >= 2:
                    filled(act, ("turn_p", a, i - 2))
                act.activation(small[:, 2 + i % 2, 0:(t + 1) * P], small[:, i % 2, 0:(t + 1) * P], ACT.Exp,
                               bias=nm[:, i % 4:i % 4 + 1], scale=-1.0, accum_out=rs[:, i % 4:i % 4 + 1]
                               ).then_inc(exp_done, 1)
            elif kind == "turn_p":
                if i % 2:
                    return
                h, t = unit(i)
                b = BANK[s][0]
                ps = filled(act, s)
                if i >= 2:
                    filled(act, ("pv", a, i - 2))
                act.copy(small[:, 4 + i % 2, 0:(t + 1) * P], ps[:, 0:(t + 1) * P]).then_inc(bank_drained[b], 1)
        act.wait_ge(eps_set, 1)
        for t in range(NT):
            square(0, t, squares)
            square_root(0, t)
        act.dma_start(br[:, 0:NG], b_grp[0:1, :].partition_broadcast(P)).then_inc(small_in, 16)
        act.dma_start(br[:, NG:NG + NE], b_rt[0:1, :].partition_broadcast(P)).then_inc(small_in, 16)
        for s in FRONT:
            if s == ("turn", "oa", 0):
                act.wait_ge(normed, NT)
                act.dma_start(gain[:], g_ffn[0:1, :].partition_broadcast(P)).then_inc(gain_in, 16)
            if s == ("scores", "a", 0):
                filled(act, ("rel", NT - 1, NH - 1))
                act.dma_start(wr[:, :, 0:NG], w_grp[0].rearrange("(k p) n -> p k n", p=P)).then_inc(small_in, 16)
                act.dma_start(wr[:, :, NG:NG + NE], w_rt[0].rearrange("(k p) n -> p k n", p=P)).then_inc(small_in, 16)
            if s == ("turn", "oa", 0):
                act.wait_ge(small_in, 64)
                act.copy(wr_hi[:], wr[:]).then_inc(wr_split, 1)
            if s == ("out", 0, 0):
                for t in range(NT):
                    filled(act, ("branch_b", 1, "tile", t))
                act.dma_start(pin, p[0, 0].rearrange("(t p) d -> p t d", p=P)).then_inc(p_in, 16)
            if s == ("router", 0, 0):
                split_high(act, N_FRONT + 2)
                split_high(act, N_FRONT + 3)
            if s == ("gate_a", 0, 0):
                for x_ in "ab":
                    for cc in range(NT):
                        filled(act, ("turn", "o" + x_, cc))
                act.dma_start(xres, x[0].rearrange("(t p) d -> p t d", p=P)).then_inc(x_back, 16)
            step(s)
            if s in (("turn", "h", 3), ("turn", "h", KD - 1)):
                split_high(act, 0 if s[2] == 3 else 1)
        act.wait_ge(normed, 2 * NT)
        act.dma_start(h2_d.rearrange("(t p) d -> p t d", p=P), stage_tok).then_inc(h2_out, 16)
        act.dma_start(gain[:], g_ple[0:1, :].partition_broadcast(P)).then_inc(gain_in, 16)
        act.wait_ge(fill_ready, 1)
        act.dma_start(table_d.rearrange("(p n) w -> p (n w)", p=P), table[:, 0:NE * CH, :].rearrange("p n w -> p (n w)")
                      ).then_inc(table_filled, 16)
        act.wait_ge(ngmax_done, 1)
        for t in range(NT):
            ins = act.activation(rs_small[:, 4 * NT + NG * t:4 * NT + NG * (t + 1)], logits[:, t, 0:NG], ACT.Exp,
                                 bias=rs_small[:, t:t + 1], accum_out=rs_small[:, NT + t:NT + t + 1])
        ins.then_inc(gexp_done, 1)
        act.wait_ge(e2_done, 1)
        act.activation(rs_small[:, 3 * NT:4 * NT], rs_small[:, 2 * NT:3 * NT], ACT.Exp).then_inc(gexp_done, 1)
        act.wait_ge(table_written, 16 * 2 * NT)
        act.dma_start(table[:, 0:NE * CH, :].rearrange("p n w -> p (n w)"), table_d.rearrange("(p n) w -> p (n w)", p=P)
                      ).then_inc(table_in, 16)

        def rows_high(b, done, n_rows=FIRST):
            act.copy(xt_view(xt_hi, b, n_rows), x_turns(n_rows)).then_inc(done, 1)

        def silu(done, n_rows=FIRST):
            act.activation(small[0:n_rows, 0, :], bank[2][0:n_rows, :], ACT.Silu).then_inc(done, 1)

        def hidden_high(done, n_rows=FIRST):
            act.copy(ht_hi[:, :, 0:n_rows], h_turns(n_rows)).then_inc(done, 1)

        def weigh(b, done, n_rows=FIRST):
            act.activation(y_sb[0:n_rows, b], psum[0:n_rows, 5:7, :].rearrange("p b s -> p (b s)"), ACT.Copy,
                           scale=pair_of[0:n_rows, b, 2:3].bitcast(F32)).then_inc(done, 1)

        act.wait_ge(x_turned, 1)
        rows_high(0, xt_hi_done)
        split_high(act, N_FRONT + 4)
        act.wait_ge(gate_done, 1)
        silu(silu_done)

        def expert(e0, i=0):
            e, b, n = e0 + 2 * i, e0 % 2, BASE_E + 6 * e0
            more = e0 != NE - 1
            split_high(act, n + 3, i)
            if more:
                act.wait_ge(x_turned, e + 2)
                wait_for(act, up_done, e)
                rows_high(1 - b, xt_hi_done)
                split_high(act, n + 4, i)
                split_high(act, n + 5, i)
            act.wait_ge(hid_turned, e + 1)
            wait_for(act, down_done, e)
            hidden_high(ht_hi_done)
            if more:
                split_high(act, n + 6, i)
                split_high(act, n + 7, i)
                act.wait_ge(gate_done, e + 2)
                act.wait_ge(hid_done, e + 1)
                silu(silu_done)
                split_high(act, n + 8, i)
            act.wait_ge(down_done, e + 1)
            wait_for(act, scattered, 16 * e)
            act.wait_ge(pairs_set, e + 1)
            weigh(b, y_done)

        expert(0)
        with act.Fori(0, NE // 2 - 1) as i:
            expert(1, i)
            expert(2, i)
        expert(NE - 1)
        act.wait_ge(over_list, 1)
        n_over = act.value_load(over[0:1, 16:17], min_val=0, max_val=NOVER)
        with act.If(n_over > 0):
            with act.Fori(0, NOVER) as i:
                with act.If(i < n_over):
                    act.wait_ge(ov["turned"], i + 1)
                    rows_high(0, ov["xt_hi"], P)
                    for r, name in enumerate(OVER_HALVES):
                        if name == "down0":
                            act.wait_ge(ov["gate"], i + 1)
                            silu(ov["silu"], P)
                        act.wait_ge(ov["loaded"], 96 * i + 16 * r + 16)
                        if r >= SPLIT:
                            act.wait_ge(ov["started"], 6 * i + r - 1)
                        else:
                            act.wait_ge(half_started, N_FRONT + N_EXP)
                            act.wait_ge(down_done, NE)
                        act.copy(w_hi[:, r % SPLIT, :], raw[:, r % RAW, :]).then_inc(ov["hi"], 1)
                    act.wait_ge(ov["hid_turned"], i + 1)
                    hidden_high(ov["ht_hi"], P)
                    act.wait_ge(ov["down"], i + 1)
                    act.wait_ge(ov["pairs"], i + 1)
                    weigh(0, ov["y"], P)
                    act.wait_ge(ov["scattered"], 16 * i + 16)
                    act.sem_inc(ov["act_end"], 1)
        for n in range(AHEAD):
            split_high(act, N_FRONT + N_EXP + n)
        for s in BACK:
            if s == ("turn", "h3", 0):
                act.wait_ge(normed, 3 * NT)
                act.dma_start(gain[:], g_final.rearrange("(a d) -> a d", a=1).partition_broadcast(P)).then_inc(gain_in, 16)
            step(s)

    @block.vector
    def _(dve):
        chain = [0]

        def link(ins):
            chain[0] += 1
            ins.then_inc(dve_chain, 1)
            dve.wait_ge(dve_chain, chain[0])

        def norm(n, src, t):
            dve.wait_ge(root, NT * n + t + 1)
            ms, sq, v, y, a, inv = (stat[:, 4 * k + t:4 * k + t + 1] for k in range(6))
            dve.tensor_scalar(v, ms, 1.0 / D, EPS, ALU.mult, ALU.add)
            link(dve.reciprocal(y, sq))
            link(dve.tensor_tensor(a, y, y, ALU.mult))
            link(dve.tensor_tensor(a, a, v, ALU.mult))
            link(dve.tensor_scalar(a, a, -0.5, 1.5, ALU.mult, ALU.add))
            link(dve.tensor_tensor(inv, a, y, ALU.mult))
            if t == 0:
                dve.wait_ge(gain_in, 16 * (n + 1))
            dve.scalar_tensor_tensor(out=stage_tok[:, t], in0=src[:, t], scalar=inv, in1=gain[:],
                                     op0=ALU.mult, op1=ALU.mult).then_inc(normed, 1)

        def step(s):
            kind, a, i = s
            if kind in WEIGHTS and HALF_OF[s] + AHEAD < N_ALL and s != ("ple_proj", 1, 0):
                split_low(dve, HALF_OF[s] + AHEAD)
            if kind == "norm":
                if a == "ple":
                    for t in range(NT):
                        dve.wait_ge(pairs_in[t % 2], 16 * (t // 2 + 1))
                        link(dve.tensor_tensor(y_in[:, t % 2, 0:D], y_in[:, t % 2, 0:D], y_in[:, t % 2, D:2 * D], ALU.add))
                        dve.tensor_tensor(xres[:, t], xres[:, t], y_in[:, t % 2, 0:D], ALU.add).then_inc(pairs_added, 1)
                        if t == 1:
                            split_low(dve, HALF_OF[("ple_proj", 1, 0)] + AHEAD)
                        if t:
                            norm(2, xres, t - 1)
                for t in range(NT) if a == "final" else [NT - 1]:
                    norm({"ffn": 1, "ple": 2, "final": 3}[a], xres, t)
                return
            if kind == "topk":
                topk_round(a)
                return
            if kind == "select":
                select()
                return
            b = BANK[s][0] if s in BANK else None
            if kind == "turn":
                if a not in SPLIT_TURNS:
                    return
                if a == "h" and i % 2 == 0 and i // 2 + 1 < NT:
                    norm(0, stage_tok, i // 2 + 1)
                n_turned[0] += 1
                dve.wait_ge(turn_hi, n_turned[0])
                hi, lo = turn_dst(s)
                ps = bank[b].rearrange("p (k s) -> p k s", k=4) if a in ROW_TURNS else bank[b]
                dve.tensor_tensor(lo, ps, hi.bitcast(F32), ALU.subtract).then_inc(bank_drained[b], 1)
            elif kind == "rel":
                t, h = a, i
                n = (t - 1) * NH + h
                w = (t + 1) * P
                drained(dve, s)
                if n == 0:
                    dve.wait_ge(const_in, 16)
                if h == 0:
                    base = c("causal")[:, (NT - t) * P:(NT + 1) * P]
                else:
                    base = score(t)
                    dve.wait_ge(acc_done, n)
                dve.scalar_tensor_tensor(out=score(t), in0=small[:, n % 2, 0:w], scalar=iws[:, t, h:h + 1],
                                         in1=base, op0=ALU.mult, op1=ALU.add).then_inc(acc_done, 1)
            elif kind == "scores":
                h, t = unit(i)
                w = (t + 1) * P
                n = NU * BR[a] + i
                ps = filled(dve, s)
                if i >= 2:
                    dve.wait_ge(exp_done, n - 1)
                bias = score(t) if a == "b" and t else c("causal")[:, (NT - t) * P:(NT + 1) * P]
                dve.tensor_tensor_reduce(out=small[:, i % 2, 0:w], in0=ps[:, 0:w], in1=bias, scale=-HD ** -0.5,
                                         scalar=3.0e38, op0=ALU.add, op1=ALU.min, accum_out=nm[:, i % 4:i % 4 + 1]
                                         ).then_inc(bank_drained[b], 1)
            elif kind == "turn_p":
                if not i % 2:
                    return
                h, t = unit(i)
                ps = filled(dve, s)
                if i >= 2:
                    filled(dve, ("pv", a, i - 2))
                dve.tensor_copy(small[:, 4 + i % 2, 0:(t + 1) * P], ps[:, 0:(t + 1) * P]).then_inc(bank_drained[b], 1)
            elif kind == "pv":
                h, t = unit(i)
                link(dve.reciprocal(ri[:, i % 4:i % 4 + 1], rs[:, i % 4:i % 4 + 1]))
                ps = filled(dve, s)
                dve.tensor_scalar(o_sb[a][:, t, h * HD:(h + 1) * HD], ps[:, 0:HD], ri[:, i % 4:i % 4 + 1], None, ALU.mult
                                  ).then_inc(bank_drained[b], 1)
            elif kind in ("branch_a", "branch_b"):
                gate = "gate_" + kind[-1]
                for t in range(NT):
                    tile = tile_of(s, t)
                    drained(dve, (gate, a, "tile", t))
                    ps, b = filled(dve, tile), BANK[tile][0]
                    dst = stage_tok[:, t, a * 512:(a + 1) * 512]
                    if kind == "branch_a":
                        dve.tensor_tensor(dst, small[:, t, :], ps[:], ALU.mult).then_inc(bank_drained[b], 1)
                    else:
                        tmp = small[:, 4 + t % 2, :]
                        dve.tensor_tensor(tmp, small[:, t, :], ps[:], ALU.mult).then_inc(bank_drained[b], 1)
                        drained(dve, tile)
                        drained(dve, ("branch_a", a, "tile", t))
                        dve.tensor_tensor(dst, dst, tmp, ALU.add).then_inc(merged_done, 1)
            elif kind == "out":
                if not last_half(s):
                    return
                for t in range(NT):
                    tile = tile_of(s, t)
                    ps, b = filled(dve, tile), BANK[tile][0]
                    dve.wait_ge(x_back, 16)
                    dst = xres[:, t, a * 512:(a + 1) * 512]
                    dve.tensor_tensor(dst, dst, ps[:], ALU.add).then_inc(bank_drained[b], 1)
                    if a and t:
                        norm(1, xres, t - 1)
            elif kind == "ple_gate":
                if not last_half(s):
                    return
                for t in range(NT):
                    drained(dve, ("ple_proj", a, "tile", t))
                    drained(dve, ("ple_gate", a, "tile", t))
                    link(dve.tensor_tensor(small[:, t, :], small[:, t, :], proj_sb[:, a, t, :], ALU.mult))
                    dst = xres[:, t, a * 512:(a + 1) * 512]
                    dve.tensor_tensor(dst, dst, small[:, t, :], ALU.add).then_inc(ple_added, 1)

        n_turned = [0]

        def topk_round(r):
            if r == 0:
                dve.wait_ge(acc_done, (NT - 1) * NH)
            for t in range(1, NT):
                if r:
                    dve.wait_ge(mark_done, (NT - 1) * (r - 1) + t)
                dve.max(m8[:, t, :], score(t)).then_inc(max_done, 1)
            for t in range(1, NT):
                dve.wait_ge(max_done, (NT - 1) * r + t)
                dve.match_replace(score(t), m8[:, t, :], score(t), MARK).then_inc(mark_done, 1)

        def select():
            for t in range(1, NT):
                dve.wait_ge(mark_done, (NT - 1) * (DSA_TOPK // 8 - 1) + t)
                dve.tensor_scalar(score(t), score(t), 0.9 * MARK, NEG, ALU.is_gt, ALU.mult).then_inc(selected, 1)
            dve.wait_ge(selected, NT - 1)

        def route():
            def small_col(n):
                return rs_small[:, n * NT:(n + 1) * NT]

            def spread(v, k):
                return v.unsqueeze(2).to_broadcast([P, NT, k])

            def first_largest(dst, src, top, desc, k, tmp):
                link(dve.tensor_reduce(top, src, AX.X, ALU.max))
                link(dve.tensor_tensor(tmp, src, spread(top, k), ALU.is_equal))
                link(dve.tensor_tensor(tmp, tmp, desc, ALU.mult))
                link(dve.tensor_reduce(small_col(9), tmp, AX.X, ALU.max))
                link(dve.tensor_tensor(dst, tmp, spread(small_col(9), k), ALU.is_equal))

            def block_(n, k=NE):
                return rt[:, n * NT * NE:n * NT * NE + NT * k].rearrange("p (t k) -> p t k", t=NT)

            masked, m1, m2, tmp, group, pen = block_(0), block_(1), block_(2), block_(3), block_(5, NG), block_(6, NG)
            gmax, v1, v2 = small_col(8), small_col(10), small_col(11)
            r_ = BANK[("router", 0, 0)][0]
            ps = filled(dve, ("router", 0, 0))
            dve.wait_ge(small_in, 64)
            dve.tensor_tensor(logits, ps[:, 0:NT * (NG + NE)].rearrange("p (t k) -> p t k", t=NT),
                              br[:].unsqueeze(1).to_broadcast([P, NT, NG + NE]), ALU.add).then_inc(bank_drained[r_], 1)
            drained(dve, ("router", 0, 0))
            first_largest(group, logits[:, :, 0:NG], gmax, c4("desc_group", NG), NG, block_(7, NG))
            dve.tensor_scalar(small_col(0), gmax, -1.0, None, ALU.mult).then_inc(ngmax_done, 1)
            link(dve.tensor_scalar(pen, group, -1.0, -NEG, ALU.add, ALU.mult))
            for g in range(NG):
                ins = dve.tensor_tensor(masked[:, :, g * EPG:(g + 1) * EPG],
                                        logits[:, :, NG + g * EPG:NG + (g + 1) * EPG],
                                        pen[:, :, g:g + 1].to_broadcast([P, NT, EPG]), ALU.add)
            link(ins)
            first_largest(m1, masked, v1, c4("desc_expert", NE), NE, tmp)
            link(dve.scalar_tensor_tensor(out=masked, in0=m1, scalar=NEG, in1=masked, op0=ALU.mult, op1=ALU.add))
            first_largest(m2, masked, v2, c4("desc_expert", NE), NE, tmp)
            dve.tensor_tensor(small_col(2), v2, v1, ALU.subtract).then_inc(e2_done, 1)
            dve.tensor_tensor(member, m1, m2, ALU.add).then_inc(top_done, 1)
            dve.wait_ge(top_done, 1)
            dve.tensor_copy(member_wide.rearrange("p t (e c) -> p (t e) c", c=CH),
                            member.rearrange("p t e -> p (t e)").unsqueeze(2).to_broadcast([P, NT * NE, CH])
                            ).then_inc(top_done, 1)
            dve.wait_ge(fill_ready, 2)
            dve.wait_ge(gexp_done, 2)
            link(dve.tensor_scalar(small_col(12), small_col(3), 1.0, None, ALU.add))
            link(dve.reciprocal(small_col(13), small_col(12)))
            link(dve.reciprocal(small_col(14), small_col(1)))
            wv = [rows[:, k * NT:(k + 1) * NT, 2].bitcast(F32) for k in range(2)]
            link(dve.tensor_tensor(wv[0], small_col(13), small_col(14), ALU.mult))
            link(dve.tensor_tensor(wv[1], wv[0], small_col(3), ALU.mult))
            for k in range(2):
                dve.tensor_copy(rows[:, k * NT:(k + 1) * NT, 0], c("token"))
                link(dve.tensor_scalar(rows[:, k * NT:(k + 1) * NT, 1], c("token"), 2.0, float(k), ALU.mult, ALU.add))
            dve.wait_ge(rank_done, 1)
            nec = NE * CH
            both = lambda v: v.unsqueeze(1).to_broadcast([P, 2] + list(v.shape[1:]))
            chosen = rt[:, NT * NE:3 * NT * NE].rearrange("p (k t e) -> p k t e", k=2, t=NT)
            tmp2 = rt[:, 5 * NT * NE:7 * NT * NE].rearrange("p (k t e) -> p k t e", k=2, t=NT)
            rank, chunk, at = (rs_small[:, n * NT:(n + 2) * NT] for n in (16, 18, 20))
            link(dve.tensor_tensor(tmp2, chosen, both(bank[1][:, 0:NT * NE].rearrange("p (t e) -> p t e", t=NT)), ALU.mult))
            link(dve.tensor_reduce(rank.rearrange("p (k t) -> p k t", k=2), tmp2, AX.X, ALU.add))
            link(dve.tensor_tensor(tmp2, chosen, both(c4("four_e", NE)), ALU.mult))
            link(dve.tensor_reduce(at.rearrange("p (k t) -> p k t", k=2), tmp2, AX.X, ALU.add))
            link(dve.tensor_scalar(chunk, rank, float(P), None, ALU.is_ge))
            for cc in range(2, CH):
                link(dve.scalar_tensor_tensor(out=chunk, in0=rank, scalar=float(cc * P), in1=chunk,
                                              op0=ALU.is_ge, op1=ALU.add))
            link(dve.scalar_tensor_tensor(out=at, in0=rank, scalar=float(nec), in1=at, op0=ALU.mult, op1=ALU.add))
            link(dve.scalar_tensor_tensor(out=at, in0=chunk, scalar=float(1 - P * nec), in1=at, op0=ALU.mult, op1=ALU.add))
            link(dve.tensor_copy(dest[:], at))
            dve.sem_inc(rows_ready, 1)
            dve.wait_ge(count_done, 1)
            dve.tensor_tensor(over_f[:, 0:1], bank[2][:, 0:1], c("limit"), ALU.is_gt).then_inc(member_f, 1)
            dve.wait_ge(list_done, 1)
            link(dve.tensor_copy(over_f[:, 1:2], bank[3][:, 0:1]))
            dve.tensor_scalar(over_f[:, 8:24], c("places"), over_f[:, 1:2], over_f[:, 0:1], ALU.is_equal, ALU.mult
                              ).then_inc(member_f, 1)
            dve.wait_ge(list_done, 2)
            link(dve.tensor_copy(over[0:1, 0:16], bank[4][0:1, 0:16]))
            dve.tensor_copy(over[0:1, 16:17], bank[5][0:1, 0:1]).then_inc(over_list, 1)

        dve.memset(eps[:], EPS).then_inc(eps_set, 1)
        dve.memset(table[:], OOB).then_inc(fill_ready, 1)
        dve.memset(rows[:], 0).then_inc(fill_ready, 1)
        norm(0, stage_tok, 0)
        for s in FRONT:
            if s == ("turn", "oa", 0):
                dve.wait_ge(wr_split, 1)
                dve.tensor_tensor(wr_lo[:], wr[:], wr_hi[:].bitcast(F32), ALU.subtract).then_inc(wr_split, 1)
            if s == ("router", 0, 0):
                split_low(dve, N_FRONT + 2)
                split_low(dve, N_FRONT + 3)
            step(s)
            if s in (("turn", "h", 3), ("turn", "h", KD - 1)):
                split_low(dve, 0 if s[2] == 3 else 1)
        route()
        def rows_low(b, done, n_rows=FIRST):
            dve.tensor_tensor(xt_view(xt_lo, b, n_rows), x_turns(n_rows), xt_view(xt_hi, b, n_rows).bitcast(F32),
                              ALU.subtract).then_inc(done, 1)

        def hidden(done, n_rows=FIRST):
            dve.tensor_tensor(small[0:n_rows, 1, :], small[0:n_rows, 0, :], bank[3][0:n_rows, :], ALU.mult
                              ).then_inc(done, 1)

        def hidden_low(done, n_rows=FIRST):
            dve.tensor_tensor(ht_lo[:, :, 0:n_rows], h_turns(n_rows), ht_hi[:, :, 0:n_rows].bitcast(F32), ALU.subtract
                              ).then_inc(done, 1)

        dve.wait_ge(xt_hi_done, 1)
        rows_low(0, xt_done)
        split_low(dve, N_FRONT + 4)

        def expert(e0, i=0):
            e, b, n = e0 + 2 * i, e0 % 2, BASE_E + 6 * e0
            more = e0 != NE - 1
            if more:
                split_low(dve, n + 3, i)
                dve.wait_ge(xt_hi_done, e + 2)
                rows_low(1 - b, xt_done)
                split_low(dve, n + 4, i)
            dve.wait_ge(silu_done, e + 1)
            dve.wait_ge(up_done, e + 1)
            wait_for(dve, hid_turned, e)
            hidden(hid_done)
            if more:
                split_low(dve, n + 5, i)
            else:
                split_low(dve, n + 3, i)
            dve.wait_ge(ht_hi_done, e + 1)
            hidden_low(ht_done)
            if more:
                split_low(dve, n + 6, i)
                split_low(dve, n + 7, i)
                split_low(dve, n + 8, i)

        expert(0)
        with dve.Fori(0, NE // 2 - 1) as i:
            expert(1, i)
            expert(2, i)
        expert(NE - 1)
        dve.wait_ge(over_list, 1)
        n_over = dve.value_load(over[0:1, 16:17], min_val=0, max_val=NOVER)
        with dve.If(n_over > 0):
            with dve.Fori(0, NOVER) as i:
                with dve.If(i < n_over):
                    dve.wait_ge(ov["xt_hi"], i + 1)
                    rows_low(0, ov["xt"], P)
                    for r, name in enumerate(OVER_HALVES):
                        dve.wait_ge(ov["hi"], 6 * i + r + 1)
                        dve.tensor_tensor(w_lo[:, r % SPLIT, :], raw[:, r % RAW, :], w_hi[:, r % SPLIT, :].bitcast(F32),
                                          ALU.subtract).then_inc(ov["lo"], 1)
                    dve.wait_ge(ov["silu"], i + 1)
                    dve.wait_ge(ov["up"], i + 1)
                    hidden(ov["hid"], P)
                    dve.wait_ge(ov["ht_hi"], i + 1)
                    hidden_low(ov["ht"], P)
        for n in range(AHEAD):
            split_low(dve, N_FRONT + N_EXP + n)
        for s in BACK:
            step(s)

    @block.gpsimd
    def _(pool):
        chain = [0]

        def link(ins):
            chain[0] += 1
            ins.then_inc(pool_chain, 1)
            pool.wait_ge(pool_chain, chain[0])

        def rope(name):
            heads = 2 if name == "ix" else NH
            z = stage_z[:, STAGE[name]].rearrange("p t (h d) -> p t h d", d=HD)[:, :, 0:heads]
            x1, x2 = z[:, :, :, 0:HALF], z[:, :, :, HALF:ROT]
            cos, sin = (c(n).rearrange("p (t h d) -> p t h d", t=NT, h=NH)[:, :, 0:heads] for n in ("cos", "sin"))
            part = [rope_t[:, :, 0:heads, k * HALF:(k + 1) * HALF] for k in range(4)]
            for step in [("ix_back", 0, 0)] if name == "ix" else [("z", name, "tile", t) for t in range(NT)]:
                drained(pool, step)
            for k, (xx, f) in enumerate(((x1, cos), (x2, sin), (x2, cos), (x1, sin))):
                link(pool.tensor_tensor(part[k], xx, f, ALU.mult))
            link(pool.tensor_tensor(x1, part[0], part[1], ALU.subtract))
            link(pool.tensor_tensor(x2, part[2], part[3], ALU.add))
            pool.sem_inc(roped, 1)

        pool.wait_ge(const_in, 16)
        for s in FRONT:
            if s[0] == "rope":
                rope(s[1])
        pool.wait_ge(h2_out, 16)
        for k in range(KD):
            filled(pool, ("turn", "h2", k))
        link(pool.memset(xg, 0.0))
        pool.wait_ge(rows_ready, 1)
        pool.wait_ge(table_filled, 16)
        for n in range(2 * NT):
            pool.indirect_dma_start(out=table_d, out_offset=bass.IndirectOffsetOnAxis(ap=dest[:, n:n + 1], axis=0),
                                    in_=rows[:, n, :], in_offset=None, bounds_check=P * NE * CH - 1,
                                    oob_is_err=False).then_inc(table_written, 16)

        def gather(b, done, n_rows=FIRST):
            pool.sem_inc(pool_steps, 1)
            pool.indirect_dma_start(out=xg[0:n_rows, b], out_offset=None, in_=h2_d,
                                    in_offset=bass.IndirectOffsetOnAxis(ap=row_of[0:n_rows, b, 0:1], axis=0),
                                    bounds_check=S - 1, oob_is_err=False).then_inc(done, 16)

        def scatter(b, done, n_rows=FIRST):
            pool.sem_inc(pool_steps, 1)
            pool.indirect_dma_start(out=pairs_d,
                                    out_offset=bass.IndirectOffsetOnAxis(ap=pair_of[0:n_rows, b, 1:2], axis=0),
                                    in_=y_sb[0:n_rows, b], in_offset=None,
                                    bounds_check=2 * S - 1, oob_is_err=False).then_inc(done, 16)

        pool.wait_ge(table_in, 16)
        for e in range(2):
            pool.tensor_copy(row_of[:, e, :], table[:, CH * e, :]).then_inc(rows_set, 1)
        for e in range(2):
            pool.wait_ge(rows_set, e + 1)
            if e:
                pool.wait_ge(gathered, 16)
            gather(e, gathered)

        def expert(e0, i=0):
            e, b = e0 + 2 * i, e0 % 2
            if e0 != NE - 1:
                pool.wait_ge(gathered, 16 * e + 32)
                pool.tensor_copy(row_of[:, b, :].unsqueeze(1), table[:, bass.ds(CH * (e + 2), 1), :]
                                 ).then_inc(rows_set, 1)
                pool.wait_ge(rows_set, e + 3)
                pool.wait_ge(x_turned, e + 1)
                gather(b, gathered)
            wait_for(pool, scattered, 16 * e)
            pool.tensor_copy(pair_of[:, b, :].unsqueeze(1), table[:, bass.ds(CH * e, 1), :]).then_inc(pairs_set, 1)
            pool.wait_ge(pairs_set, e + 1)
            pool.wait_ge(y_done, e + 1)
            scatter(b, scattered)

        expert(0)
        with pool.Fori(0, NE // 2 - 1) as i:
            expert(1, i)
            expert(2, i)
        expert(NE - 1)
        pool.wait_ge(over_list, 1)
        n_over = pool.value_load(over[0:1, 16:17], min_val=0, max_val=NOVER)
        with pool.If(n_over > 0):
            with pool.Fori(0, NOVER) as i:
                with pool.If(i < n_over):
                    pool.wait_ge(scattered, 16 * NE)
                    pool.wait_ge(gathered, 16 * NE + 16)
                    code = pool.value_load(over[0:1, bass.ds(i, 1)], min_val=0, max_val=NE * CH - 1)
                    pool.tensor_copy(row_of[:, 0, :].unsqueeze(1), table[:, bass.ds(code, 1), :]).then_inc(ov["rows"], 1)
                    pool.tensor_copy(pair_of[:, 0, :].unsqueeze(1), table[:, bass.ds(code, 1), :]).then_inc(ov["pairs"], 1)
                    pool.wait_ge(ov["rows"], i + 1)
                    pool.wait_ge(ov["pairs"], i + 1)
                    gather(0, ov["gathered"], P)
                    pool.wait_ge(ov["y"], i + 1)
                    scatter(0, ov["scattered"], P)
                    pool.wait_ge(ov["scattered"], 16 * i + 16)
                    pool.sem_inc(ov["pool_end"], 1)

    block.__exit__(None, None, None)


_INS = ["x", "p", "g_attn", "w_in", "w_br_a", "w_br_b", "w_out", "g_ffn", "w_grp", "b_grp", "w_rt", "b_rt",
        "w_gate", "w_up", "w_down", "g_ple", "w_ple_gate", "w_ple_proj", "g_final"]


def kernel(**inputs):
    import concourse.bacc as bacc
    from concourse.bass_utils import run_bass_kernel_spmd

    nc = bacc.Bacc("TRN2", target_bir_lowering=False, num_devices=1)
    arrays, args = {}, []
    for name in _INS:
        a = np.ascontiguousarray(inputs[name])
        arrays[f"in_{name}"] = a
        args.append(nc.dram_tensor(f"in_{name}", a.shape, mybir.dt.from_np(a.dtype), kind="ExternalInput").ap())
    arrays["constants"] = constants()
    args.append(nc.dram_tensor("constants", (P, NCONST), F32, kind="ExternalInput").ap())
    out = nc.dram_tensor("out", (1, S, D), F32, kind="ExternalOutput").ap()
    layer_kernel(nc, *args, out)
    r = run_bass_kernel_spmd(nc, [arrays], core_ids=[0])
    return r.results[0]["out"]
```
